# Optimizing a Trainium2 kernel written in Bass

```python
import math
import jax, jax.numpy as jnp
from jax import lax
import numpy as np

D_MODEL = 1024
BATCH = 1
SEQ = 1024
DEPTH = 1
DEC_BATCH = 1
DEC_SEQ = 1024
PAST_LEN = 128

N_RET_HEADS = 8
RET_QK_DIM = D_MODEL // 16
RET_V_DIM = D_MODEL // N_RET_HEADS
RET_QK = N_RET_HEADS * RET_QK_DIM
RET_V = N_RET_HEADS * RET_V_DIM
CHUNK = 128
ROPE_BASE = 10000.0
POOL_WINDOWS = (2, 4, 8, 16)
N_POOL_GROUPS = 4
POOL_WIDTH = D_MODEL // 2
POOL_GROUP_IN = POOL_WIDTH // N_POOL_GROUPS
POOL_GROUP_OUT = D_MODEL // N_POOL_GROUPS
D_FF = 128 * ((8 * D_MODEL // 3 + 127) // 128)
CONV_WIDTH = 3
N_MOD = 6
EPS = 1e-6
IN_WIDTH = 2 * RET_QK + 2 * RET_V + POOL_WIDTH + 2 * D_MODEL
IN_SPLITS = (RET_QK, 2 * RET_QK, 2 * RET_QK + RET_V, 2 * RET_QK + 2 * RET_V,
             2 * RET_QK + 2 * RET_V + POOL_WIDTH, 2 * RET_QK + 2 * RET_V + POOL_WIDTH + D_MODEL)

kernel_name = "gated_retention_pool_encoder"

def _rmsnorm(x, g):
    xf = x.astype(jnp.float32)
    return xf * lax.rsqrt(jnp.mean(xf * xf, axis=-1, keepdims=True) + EPS) * g.astype(jnp.float32)

def _rope_tables(s):
    half = RET_QK_DIM // 2
    inv_freq = ROPE_BASE ** (-jnp.arange(half, dtype=jnp.float32) / half)
    ang = jnp.arange(s, dtype=jnp.float32)[:, None] * inv_freq[None, :]
    return jnp.cos(ang)[None, :, None, :], jnp.sin(ang)[None, :, None, :]

def _rotary(t, cos, sin):
    t1, t2 = jnp.split(t, 2, axis=-1)
    return jnp.concatenate([t1 * cos - t2 * sin, t1 * sin + t2 * cos], axis=-1)

def _retention_one_direction(q, k, v, log_g, strict):
    b, s, h, dk = q.shape
    dv = v.shape[-1]
    n = s // CHUNK

    def chunks(t):
        return t.reshape(b, n, CHUNK, h, t.shape[-1]).transpose(1, 0, 3, 2, 4)

    idx = jnp.arange(CHUNK, dtype=jnp.float32)
    diff = idx[:, None] - idx[None, :]
    allowed = diff >= (1.0 if strict else 0.0)
    decay_in = jnp.where(allowed[None], jnp.exp(jnp.where(allowed, diff, 0.0)[None] * log_g[:, None, None]), 0.0)
    decay_q = jnp.exp((idx + 1.0)[None, :] * log_g[:, None])[None, :, :, None]
    decay_k = jnp.exp((CHUNK - 1.0 - idx)[None, :] * log_g[:, None])[None, :, :, None]
    decay_chunk = jnp.exp(CHUNK * log_g)[None, :, None, None]

    def step(state, qkv):
        qc, kc, vc = qkv
        scores = jnp.einsum('bhqd,bhkd->bhqk', qc, kc) * decay_in
        inner = jnp.einsum('bhqk,bhke->bhqe', scores, vc)
        cross = jnp.einsum('bhqd,bhde->bhqe', qc * decay_q, state)
        new_state = decay_chunk * state + jnp.einsum('bhkd,bhke->bhde', kc * decay_k, vc)
        return new_state, inner + cross

    state0 = jnp.zeros((b, h, dk, dv), jnp.float32)
    _, out = lax.scan(step, state0, (chunks(q), chunks(k), chunks(v)))
    return out.transpose(1, 0, 3, 2, 4).reshape(b, s, h, dv)

def _multiscale_pool(p):
    s = p.shape[1]
    pos = jnp.arange(s)
    outs = []
    for gi, w in enumerate(POOL_WINDOWS):
        pg = p[..., gi * POOL_GROUP_IN:(gi + 1) * POOL_GROUP_IN]
        cs = jnp.pad(jnp.cumsum(pg, axis=1), ((0, 0), (1, 0), (0, 0)))
        lo = jnp.clip(pos - w // 2, 0, s)
        hi = jnp.clip(pos + w // 2, 0, s)
        cnt = (hi - lo).astype(jnp.float32)
        mean = (jnp.take(cs, hi, axis=1) - jnp.take(cs, lo, axis=1)) / cnt[None, :, None]
        outs.append(mean - pg)
    return jnp.stack(outs, axis=2)

def _dwconv_centred(u, w, bias):
    up = jnp.pad(u, ((0, 0), (1, 1), (0, 0)))
    return up[:, :-2] * w[0] + up[:, 1:-1] * w[1] + up[:, 2:] * w[2] + bias

def _layer(x, c, w_ada, b_ada, g_mix, w_in, ret_decay_f, ret_decay_b, ret_gn_gain,
           w_pool_grp, pool_scale, w_out, g_ffn, w_up, conv_w, conv_b, w_down):
    dt = x.dtype
    b, s, _ = x.shape
    mod = jnp.dot(jax.nn.silu(c), w_ada) + b_ada
    shift1, scale1, gate1, shift2, scale2, gate2 = [m[:, None, :] for m in jnp.split(mod, N_MOD, axis=-1)]

    h = (_rmsnorm(x, g_mix) * (1.0 + scale1) + shift1).astype(dt)
    proj = jnp.einsum('bsd,de->bse', h, w_in)
    q, k, v, g_sw, p, gate_a, gate_b = jnp.split(proj, IN_SPLITS, axis=-1)

    cos, sin = _rope_tables(s)
    qh = _rotary(q.astype(jnp.float32).reshape(b, s, N_RET_HEADS, RET_QK_DIM), cos, sin)
    kh = _rotary(k.astype(jnp.float32).reshape(b, s, N_RET_HEADS, RET_QK_DIM), cos, sin) * (RET_QK_DIM ** -0.5)
    vh = v.astype(jnp.float32).reshape(b, s, N_RET_HEADS, RET_V_DIM)
    log_g_f = jax.nn.log_sigmoid(ret_decay_f.astype(jnp.float32))
    log_g_b = jax.nn.log_sigmoid(ret_decay_b.astype(jnp.float32))
    ret_f = _retention_one_direction(qh, kh, vh, log_g_f, strict=False)
    ret_b = _retention_one_direction(qh[:, ::-1], kh[:, ::-1], vh[:, ::-1], log_g_b, strict=True)[:, ::-1]
    ret = ret_f + ret_b
    mu = jnp.mean(ret, axis=-1, keepdims=True)
    var = jnp.mean(jnp.square(ret - mu), axis=-1, keepdims=True)
    ret = ((ret - mu) * lax.rsqrt(var + EPS)).reshape(b, s, RET_V) * ret_gn_gain.astype(jnp.float32)
    branch_a = jax.nn.silu(g_sw.astype(jnp.float32)) * ret

    pooled = _multiscale_pool(p.astype(jnp.float32))
    branch_b = jnp.einsum('bsgi,gio->bsgo', pooled, w_pool_grp.astype(jnp.float32)).reshape(b, s, D_MODEL)
    branch_b = branch_b * pool_scale.astype(jnp.float32)

    merged = jax.nn.sigmoid(gate_a.astype(jnp.float32)) * branch_a + jax.nn.sigmoid(gate_b.astype(jnp.float32)) * branch_b
    mix_out = jnp.einsum('bsd,de->bse', merged.astype(dt), w_out)
    x = x + gate1 * mix_out

    h2 = (_rmsnorm(x, g_ffn) * (1.0 + scale2) + shift2).astype(dt)
    up = jnp.einsum('bsd,df->bsf', h2, w_up)
    up = _dwconv_centred(up, conv_w, conv_b)
    act, lin = jnp.split(up, 2, axis=-1)
    ffn = jnp.einsum('bsf,fd->bsd', jax.nn.gelu(act) * lin, w_down)
    return x + gate2 * ffn

def _encoder(x, c, w_ada, b_ada, g_mix, w_in, ret_decay_f, ret_decay_b, ret_gn_gain,
             w_pool_grp, pool_scale, w_out, g_ffn, w_up, conv_w, conv_b, w_down, g_final):
    for l in range(DEPTH):
        x = _layer(x, c, w_ada[l], b_ada[l], g_mix[l], w_in[l], ret_decay_f[l], ret_decay_b[l],
                   ret_gn_gain[l], w_pool_grp[l], pool_scale[l], w_out[l], g_ffn[l], w_up[l],
                   conv_w[l], conv_b[l], w_down[l])
    return _rmsnorm(x, g_final).astype(x.dtype)

def setup_inputs(seed: int = 0) -> dict:
    key = jax.random.key(seed)
    ks = jax.random.split(key, 24)
    f32 = jnp.float32
    nrm = lambda k, shape, scale: jax.random.normal(k, shape, f32) * scale
    base_logit = jnp.log(2.0 ** (5.0 + jnp.arange(N_RET_HEADS, dtype=f32)) - 1.0)
    return {
        "x_prompt": nrm(ks[0], (BATCH, SEQ, D_MODEL), 1.0),
        "x_sample": nrm(ks[1], (DEC_BATCH, DEC_SEQ, D_MODEL), 1.0),
        "c_prompt": nrm(ks[2], (BATCH, D_MODEL), 1.0),
        "c_sample": nrm(ks[3], (DEC_BATCH, D_MODEL), 1.0),
        "w_ada": nrm(ks[4], (DEPTH, D_MODEL, N_MOD * D_MODEL), D_MODEL ** -0.5),
        "b_ada": nrm(ks[5], (DEPTH, N_MOD * D_MODEL), 0.02),
        "g_mix": 1.0 + nrm(ks[6], (DEPTH, D_MODEL), 0.05),
        "w_in": nrm(ks[7], (DEPTH, D_MODEL, IN_WIDTH), D_MODEL ** -0.5),
        "ret_decay_f": base_logit[None, :] + nrm(ks[8], (DEPTH, N_RET_HEADS), 0.1),
        "ret_decay_b": base_logit[None, :] + nrm(ks[9], (DEPTH, N_RET_HEADS), 0.1),
        "ret_gn_gain": 1.0 + nrm(ks[10], (DEPTH, RET_V), 0.05),
        "w_pool_grp": nrm(ks[11], (DEPTH, N_POOL_GROUPS, POOL_GROUP_IN, POOL_GROUP_OUT), POOL_GROUP_IN ** -0.5),
        "pool_scale": 1.0 + nrm(ks[12], (DEPTH, D_MODEL), 0.1),
        "w_out": nrm(ks[13], (DEPTH, D_MODEL, D_MODEL), D_MODEL ** -0.5),
        "g_ffn": 1.0 + nrm(ks[14], (DEPTH, D_MODEL), 0.05),
        "w_up": nrm(ks[15], (DEPTH, D_MODEL, 2 * D_FF), D_MODEL ** -0.5),
        "conv_w": nrm(ks[16], (DEPTH, CONV_WIDTH, 2 * D_FF), CONV_WIDTH ** -0.5),
        "conv_b": nrm(ks[17], (DEPTH, 2 * D_FF), 0.02),
        "w_down": nrm(ks[18], (DEPTH, D_FF, D_MODEL), D_FF ** -0.5),
        "g_final": 1.0 + nrm(ks[19], (D_MODEL,), 0.05),
    }

def reference(x_prompt, x_sample, c_prompt, c_sample, w_ada, b_ada, g_mix, w_in, ret_decay_f,
              ret_decay_b, ret_gn_gain, w_pool_grp, pool_scale, w_out, g_ffn, w_up, conv_w, conv_b,
              w_down, g_final):
    y_prompt = _encoder(x_prompt, c_prompt, w_ada, b_ada, g_mix, w_in, ret_decay_f, ret_decay_b,
                        ret_gn_gain, w_pool_grp, pool_scale, w_out, g_ffn, w_up, conv_w, conv_b,
                        w_down, g_final)
    y_sample = _encoder(x_sample, c_sample, w_ada, b_ada, g_mix, w_in, ret_decay_f, ret_decay_b,
                        ret_gn_gain, w_pool_grp, pool_scale, w_out, g_ffn, w_up, conv_w, conv_b,
                        w_down, g_final)
    return (y_prompt, y_sample)


_drawn_inputs = setup_inputs


def setup_inputs(seed=0):
    import zlib

    import numpy as np

    out = dict(_drawn_inputs(seed))
    spreads = {}
    factors = {'ret_gn_gain': 4.165, 'conv_b': 4.596}
    for name, (base, spread) in spreads.items():
        noise = np.random.default_rng([zlib.crc32(name.encode()), seed]).standard_normal(out[name].shape)
        drawn = base * np.exp(spread * noise) if base else spread * noise
        out[name] = __import__('jax').numpy.asarray(drawn.astype(out[name].dtype))
    for name, factor in factors.items():
        out[name] = (out[name] * factor).astype(out[name].dtype)
    return out
```

```python
from contextlib import ExitStack

import numpy as np

import concourse.bass as bass
import concourse.mybir as mybir

F32 = mybir.dt.float32
F32R = mybir.dt.float32r
ACT = mybir.ActivationFunctionType
ALU = mybir.AluOpType

P = 128
D = 1024
S = 1024
KC = D // P
TT = S // P
HALF = 512
N_SEQ = 2
HEADS = 8
DK = 64
PAIRS = HEADS // 2
D_FF = 2816
FC = D_FF // P
GROUPS = FC // 2
POOL_W = 512
EPS = 1e-6
K_SCALE = DK ** -0.5
PAD = 8
Q0, K0, V0, GS0, P0 = 0, 512, 1024, 2048, 3072
GA0 = P0 + POOL_W
GB0 = GA0 + D

C_COS = 0
C_SIN = C_COS + TT * 32
C_DIFP = C_SIN + TT * 32
C_DIFN = C_DIFP + P
C_ID = C_DIFN + P
C_POS = C_ID + P
POOL_COLS = 21
C_POOL = C_POS + 4
C_ALL = C_POOL + PAIRS * POOL_COLS

T_DQ, T_DK, T_DC, T_GAIN, T_PS, T_LGF, T_LGB, T_POOL = 0, 4, 8, 10, 12, 14, 16, 18
T_BUILT = 18
T_ALL = T_BUILT + POOL_COLS

R_BADA, R_GMIX, R_GAIN, R_PS, R_GFFN, R_GFIN, R_C, R_ALL = 0, 48, 56, 64, 72, 80, 88, 104


class Tally:

    ORDER = ("pre", "mix", "mid", "ffn", "post")
    TIMES = {"pre": 1, "mix": PAIRS, "mid": 1, "ffn": GROUPS, "post": 1}

    def __init__(self, sem, setup=0, **per):
        self.sem, self.setup, self.per = sem, setup, per
        self.seq = sum(self.TIMES[r] * per.get(r, 0) for r in self.ORDER)

    def at(self, where, n):
        region, seq, it = where
        base = self.setup + n
        for r in self.ORDER[:self.ORDER.index(region)]:
            base += self.TIMES[r] * self.per.get(r, 0)
        if self.seq:
            base = seq * self.seq + base
        if self.per.get(region, 0) and self.TIMES[region] > 1:
            base = it * self.per[region] + base
        return self.sem, base


STEPS = {
    "pre": [(f"X{t}", t % 4) for t in range(TT)] + [("ST", 0), ("R", 1)],
    "mix": [("Q0", 1), ("Q1", 2), ("Q2", 3), ("Q3", 0), ("P", 1), ("GS0", 2), ("TQ", 3), ("TK", 0), ("TD0", 1),
            ("KV0", 3), ("SC0", 0), ("GA0", 2), ("O0", 1), ("TD1", 3), ("KV1", 0), ("SC1", 2), ("GB0", 3),
            ("O1", 1), ("BB0", 0), ("TR0", 2), ("GS1", 3), ("GA1", 1), ("TR1", 0), ("GB1", 2), ("BB1", 3),
            ("W0", 1), ("W1", 2), ("W2", 3), ("W3", 0), ("W4", 1), ("W5", 2), ("W6", 3), ("W7", 0)],
    "mid": [("ST", 1), ("R", 2)],
    "ffn": [("U0", 0), ("U1", 1), ("U2", 2), ("U3", 3)] + [(f"W{d}", d % 4) for d in range(KC)],
    "post": [("ST", 0), ("R", 1)] + [(f"Y{t}", (t + 2) % 4) for t in range(TT)],
}
BLOCKS = {
    "mix": [(3, 0), (3, 1), (3, 2), (3, 0), (1, 1), (1, 2), (1, 0), (1, 1), (1, 2), (1, 0), (1, 1), (1, 2), (1, 1)],
    "ffn": [(3, 0), (3, 1), (1, 2), (1, 0), (1, 1), (1, 2)],
}
N_MIX, N_FFN = len(BLOCKS["mix"]), len(BLOCKS["ffn"])


def constants():
    c = np.zeros((P, C_ALL), np.float32)
    half = DK // 2
    inv = np.float32(10000.0) ** (-np.arange(half, dtype=np.float32) / np.float32(half))
    ang = np.arange(S, dtype=np.float32)[:, None] * inv[None, :].astype(np.float32)
    for col, f in ((C_COS, np.cos), (C_SIN, np.sin)):
        t = f(ang).astype(np.float32).reshape(TT, P, half).transpose(1, 0, 2)
        c[:, col:col + TT * half] = t.reshape(P, TT * half)
    p = np.arange(P)
    dif = p[None, :] - p[:, None]
    c[:, C_DIFP:C_DIFP + P] = np.maximum(dif, 0)
    c[:, C_DIFN:C_DIFN + P] = np.maximum(-dif, 0)
    c[:, C_ID:C_ID + P] = np.eye(P)
    c[:, C_POS:C_POS + 4] = np.stack([p + 1, P - p, P - 1 - p, p], 1)
    for g in range(PAIRS):
        w = 2 ** (g + 1)
        o = C_POOL + g * POOL_COLS
        c[:, o:o + 4] = [1.0 if level <= g else 0.0 for level in range(4)]
        c[:, o + 4] = 1.0 / w
        t = np.concatenate([np.arange(PAD), np.arange(S - PAD, S)])
        cnt = np.minimum(t + w // 2, S) - np.maximum(t - w // 2, 0)
        c[:, o + 5:o + 21] = np.float32(w) / cnt.astype(np.float32)
    return c


def encoder_program(nc, x, c, w_ada, b_ada, g_mix, w_in, decay_f, decay_b, gn_gain, w_pool, pool_scale,
                    w_out, g_ffn, w_up, conv_w, conv_b, w_down, g_final, consts, y):
    ctx = ExitStack()
    with ctx:
        def sb(name, shape, dt=F32, stack=ctx):
            return stack.enter_context(nc.sbuf_tensor(name, shape, dt))

        def sem(name):
            return ctx.enter_context(nc.semaphore(name))

        ps = ctx.enter_context(nc.psum_tensor("ps", [P, 4, 2 * HALF], F32))

        xT = sb("xT", [P, KC, S])
        h_hi = sb("h_hi", [P, KC, S], F32R)
        h_lo = sb("h_lo", [P, KC, S], F32R)
        w_raw = sb("w_raw", [P, 2, 1024])
        w_hi = sb("w_hi", [P, 3, 1024], F32R)
        w_lo = sb("w_lo", [P, 3, 1024], F32R)
        cst = sb("cst", [P, C_ALL])
        ones = sb("ones", [P, P])
        vecT = sb("vecT", [P, R_ALL])
        convT = sb("convT", [P, 2 * FC, 4])
        modT = sb("modT", [P, N_SEQ, 48])
        modS = sb("modS", [P, 48])
        pairT = sb("pairT", [P, PAIRS, T_BUILT])
        pairS = sb("pairS", [P, T_ALL])
        convS = sb("convS", [P, 2, 2, 4])
        lg = sb("lg", [P, 2, PAIRS, 2])
        small = sb("small", [P, 8, 16])
        msq = sb("msq", [P, TT])
        rstd = sb("rstd", [P, TT])
        mhalf = sb("mhalf", [P, TT])
        bst = sb("bst", [P, TT, 6])
        mv = sb("mv", [P, TT, 2])
        veps = sb("veps", [P, TT])
        grs = sb("grs", [P, TT])

        ident = cst[:, C_ID:C_ID + P]

        mix = ExitStack()
        m_hi = sb("m_hi", [P, 2, S], F32R, mix)
        m_lo = sb("m_lo", [P, 2, S], F32R, mix)
        rot = sb("rot", [P, TT, 256], F32, mix)
        v_sb = sb("v_sb", [P, TT, 256], F32, mix)
        tokb = sb("tokb", [P, TT, P], F32, mix)
        kdp = sb("kdp", [P, TT, P], F32, mix)
        qdT = sb("qdT", [P, S], F32, mix)
        qT = sb("qT", [P, S], F32, mix)
        kT = sb("kT", [P, S], F32, mix)
        state = sb("state", [P, S + 2 * PAD], F32, mix)
        bufA = sb("bufA", [P, S], F32, mix)
        bufB = sb("bufB", [P, S], F32, mix)
        poolU = sb("poolU", [P, S + 2 * PAD], F32, mix)
        dec = sb("dec", [P, 2, P], F32, mix)
        wpool = sb("wpool", [P, 256], F32, mix)
        mix.close()

        ffn = ExitStack()
        f_pad = sb("f_pad", [P, 4 * S], F32, ffn)
        acc = sb("acc", [P, S], F32, ffn)
        sq = sb("sq", [P, 2, S], F32, ffn)
        rrow = sb("rrow", [P, S], F32, ffn)
        diag = sb("diag", [P, S], F32, ffn)
        tn = sb("tn", [P, 2, S], F32, ffn)
        hf = sb("hf", [P, 2, S], F32, ffn)
        xin = sb("xin", [P, 4, S], F32, ffn)
        ffn.close()
        ffn2 = ExitStack()
        a_hi = sb("a_hi", [P, 2, S], F32R, ffn2)
        a_lo = sb("a_lo", [P, 2, S], F32R, ffn2)
        f_pad2 = sb("f_pad2", [P, 9 * S], F32, ffn2)
        ca = sb("ca", [P, S], F32, ffn2)
        cl = sb("cl", [P, S], F32, ffn2)
        ffn2.close()
        start = ExitStack()
        ada = sb("ada", [P, 8, KC, 256], F32, start)
        rows = sb("rows", [P, 3, P], F32, start)
        start.close()

        def tally(name, setup=0, **per):
            return Tally(sem(name), setup, **per)

        full = [tally(f"psum_full{n}", 0, **{r: sum(slot == n for _, slot in STEPS[r]) for r in STEPS})
                for n in range(4)]

        def place(region, step):
            slot = dict(STEPS[region])[step]
            turns = [name for name, other in STEPS[region] if other == slot]
            return slot, turns.index(step) + 1

        def brought(region, i):
            return 16 * sum(n for j, (n, _) in enumerate(BLOCKS[region]) if j % 2 == i % 2 and j <= i)

        raw_in = [tally(f"raw_in{r}", 0, mix=brought("mix", N_MIX - 1 - (N_MIX - 1 - r) % 2),
                        ffn=brought("ffn", N_FFN - 2 + r)) for r in range(2)]
        hi_done = tally("w_hi_done", 0, mix=N_MIX, ffn=N_FFN)
        lo_done = tally("w_lo_done", 1, mix=N_MIX, ffn=N_FFN)
        q_block = tally("q_block_used", 0, mix=3)

        const_in = sem("const_in")
        rows_in = sem("rows_in")
        decay_in = sem("decay_in")
        ones_set = sem("ones_set")
        ada_in = [sem(f"ada_in{i}") for i in range(8)]
        ada_used = sem("ada_used")
        vec_done = sem("vec_done")
        table_step = sem("table_step")
        table_act = sem("table_act")
        table_args = sem("table_args")
        sil_tanh = sem("sil_tanh")
        sil_done = sem("sil_done")
        setup_done = sem("setup_done")

        x_in = [tally(f"x_in{i}", 0, pre=32) for i in range(4)]
        vec_turned = sem("vec_turned")
        xT_set = [tally("xT_set_dve", 0, pre=TT // 2), tally("xT_set_act", 0, pre=TT // 2)]
        mod_set = tally("mod_set", 0, pre=1)
        sq_done = tally("sq_done", 0, pre=KC, mid=KC, post=KC)
        acc_done = tally("acc_done", 0, pre=KC - 1, mid=KC - 1, post=KC - 1)
        msq_done = tally("msq_done", 0, pre=1, mid=1, post=1)
        rstd_done = tally("rstd_done", 0, pre=1, mid=1, post=1)
        diag_done = tally("diag_done", 0, pre=1, mid=1, post=1)
        rrow_done = tally("rrow_done", 0, pre=1, mid=1, post=1)
        tn_done = tally("tn_done", 0, pre=KC, mid=KC)
        hhi_done = tally("h_hi_done", 0, pre=KC, mid=KC)
        hlo_done = tally("h_lo_done", 0, pre=KC, mid=KC)
        res_done = tally("residual_done", 1, mix=KC, ffn=KC)
        y_scaled = tally("y_scaled", 0, post=KC)
        y_copied = [tally("y_copied_dve", 1, post=TT // 2), tally("y_copied_act", 1, post=TT // 2)]
        y_out = [tally(f"y_out{i}", 1, post=32) for i in range(4)]

        pair_set = tally("pair_set", 0, mix=1)
        dec_arg = tally("dec_arg", 0, mix=4)
        dec_done = tally("dec_done", 0, mix=1)
        wpool_in = tally("wpool_in", 0, mix=16)
        v_done = tally("v_done", 0, mix=4)
        rope_mul = tally("rope_mul", 0, mix=4)
        rope_done = tally("rope_done", 0, mix=4)
        qT_done = tally("qT_done", 0, mix=1)
        kT_done = tally("kT_done", 0, mix=1)
        qd_done = tally("qd_done", 0, mix=2)
        kd_done = tally("kd_done", 0, mix=2)
        qdT_done = tally("qdT_done", 0, mix=2)
        state_step = tally("state_step", 0, mix=2 * (2 + 14))
        pt_done = tally("scores_done", 0, mix=2)
        p_copied = tally("p_copied", 0, mix=1)
        pool_step = tally("pool_step", 0, mix=8)
        stat_done = tally("gn_stats", 0, mix=2)
        mv_done = tally("gn_moments", 0, mix=2)
        veps_done = tally("gn_veps", 0, mix=2)
        grs_done = tally("gn_rstd", 0, mix=2)
        cent_done = tally("gn_centred", 0, mix=2)
        retn_done = tally("gn_done", 0, mix=2)
        th_done = tally("tanh_swish", 0, mix=2)
        sw_done = tally("swish_done", 0, mix=2)
        ta_done = tally("tanh_a", 0, mix=2)
        ga_done = tally("gate_a_done", 0, mix=2)
        tb_done = tally("tanh_b", 0, mix=2)
        ma_done = tally("branch_a_done", 0, mix=2)
        mb_done = tally("branch_b_done", 1, mix=2)
        mg_done = tally("merged", 0, mix=2)
        mhi_done = tally("merged_hi", 0, mix=2)
        mlo_done = tally("merged_lo", 0, mix=2)

        conv_set = tally("conv_set", 0, ffn=1)
        mid_tap = tally("middle_tap", 0, ffn=4)
        side_tap = tally("side_taps", 0, ffn=8)
        gelu_done = tally("gelu_done", 0, ffn=2)
        prod_done = tally("prod_done", 0, ffn=2)
        ahi_done = tally("a_hi_done", 0, ffn=2)
        alo_done = tally("a_lo_done", 0, ffn=2)

        def slot_of(where, step):
            return place(where[0], step)[0]

        def filled(where, step):
            slot, turn = place(where[0], step)
            return full[slot].at(where, turn)

        def sq_view(ap, n):
            return ap.rearrange("p (a b) -> p a b", a=n)

        w_in_v = w_in.rearrange("(k p) n -> p k n", p=P)
        w_out_v = w_out.rearrange("(k p) n -> p k n", p=P)
        w_pool_v = w_pool.rearrange("g p n -> p g n")
        w_up_v = w_up.rearrange("(k p) n -> p k n", p=P)
        w_down_v = w_down.rearrange("(k p) n -> p k n", p=P)
        w_ada_v = w_ada.rearrange("(k p) n -> p k n", p=P)

        block = ctx.enter_context(nc.Block())

        @block.sync
        def _(sp):
            sp.dma_start(cst[:, :], consts).then_inc(const_in, 16)
            chunked = "(c p) -> c p"
            parts = [(0, R_BADA, b_ada.rearrange(chunked, p=P)), (0, R_GMIX, g_mix.rearrange(chunked, p=P)),
                     (0, R_GAIN, gn_gain.rearrange(chunked, p=P)), (0, R_PS, pool_scale.rearrange(chunked, p=P)),
                     (0, R_GFFN, g_ffn.rearrange(chunked, p=P)), (0, R_GFIN, g_final.rearrange(chunked, p=P)),
                     (0, R_C, c.rearrange("s (c p) -> (s c) p", p=P)),
                     (1, 0, conv_w[0:2, :].rearrange("t (c p) -> (t c) p", p=P)),
                     (2, 0, conv_w[2:3, :].rearrange("t (c p) -> (t c) p", p=P)),
                     (2, 2 * FC, conv_b.rearrange(chunked, p=P))]
            for i, r, src in parts:
                sp.dma_start(rows[r:r + src.shape[0], i, :], src).then_inc(rows_in, 16)
            for i, src in enumerate((decay_f, decay_b)):
                sp.dma_start(lg[:, i, :, :].rearrange("p a b -> p (a b)"), src.partition_broadcast(P)).then_inc(decay_in, 16)
            with sp.Fori(0, 3) as it:
                for s in range(8):
                    sp.wait_ge(ada_used, it * 8 + (s + 1))
                    sp.dma_start(ada[:, s, :, :], w_ada_v[:, :, bass.ds(it * 2048 + s * 256, 256)]).then_inc(ada_in[s], 16)

            def load(where, i, parts):
                sp.wait_ge(*lo_done.at(where, max(i - 1, 0)))
                for dst, src in parts:
                    sp.dma_start(dst, src).then_inc(raw_in[i % 2].sem, 16)

            def mix_block(where, i):
                pr = where[2]
                if i < 4:
                    dst = sq_view(w_raw[:, i % 2, :], 2)
                    load(where, i, [(dst[:, :, a:a + n], w_in_v[:, 2 * i:2 * i + 2, bass.ds(col, n)])
                                    for a, n, col in ((0, P, pr * P + Q0), (P, P, pr * P + K0),
                                                      (2 * P, 2 * P, pr * 2 * P + V0))])
                elif i < 11:
                    col = {4: pr * P + P0, 5: pr * 2 * P + GS0, 6: pr * 2 * P + GA0, 7: pr * 2 * P + GB0,
                           8: pr * 2 * P + (GS0 + P), 9: pr * 2 * P + (GA0 + P), 10: pr * 2 * P + (GB0 + P)}[i]
                    load(where, i, [(sq_view(w_raw[:, i % 2, :], KC), w_in_v[:, :, bass.ds(col, P)])])
                else:
                    src = w_out_v[:, bass.ds(pr * 2, 2), (i - 11) * HALF:(i - 10) * HALF]
                    load(where, i, [(sq_view(w_raw[:, i % 2, :], 2), src)])

            def ffn_block(where, i):
                g = where[2]
                if i < 4:
                    dst = sq_view(w_raw[:, i % 2, :], KC)
                    src = w_up_v[:, :, bass.ds(g * 2 * P + ((i // 2) * P + (i % 2) * D_FF), P)]
                    cuts = (0, 3, 6, KC) if i < 2 else (0, KC)
                    load(where, i, [(dst[:, a:b, :], src[:, a:b, :]) for a, b in zip(cuts, cuts[1:])])
                else:
                    src = w_down_v[:, bass.ds(g * 2, 2), (i - 4) * HALF:(i - 3) * HALF]
                    load(where, i, [(sq_view(w_raw[:, i % 2, :], 2), src)])

            with sp.Fori(0, N_SEQ) as seq:
                with sp.Fori(0, PAIRS) as pr:
                    where = ("mix", seq, pr)
                    for i in range(N_MIX):
                        mix_block(where, i)
                        if i == 6:
                            sp.wait_ge(*mb_done.at(where, 0))
                            sp.dma_start(wpool[:, :].unsqueeze(1), w_pool_v[:, bass.ds(pr, 1), :]).then_inc(wpool_in.sem, 16)
                with sp.Fori(0, GROUPS) as g:
                    for i in range(N_FFN):
                        ffn_block(("ffn", seq, g), i)
            for i in range(2):
                mix_block(("mix", N_SEQ, 0), i)

        @block.tensor
        def _(pe):
            def weights(where, i):
                pe.wait_ge(*hi_done.at(where, i + 1))
                pe.wait_ge(*lo_done.at(where, i + 1))
                return BLOCKS[where[0]][i][1]

            def three_passes(slot, w_slot, col, act_hi, act_lo, k, first, last):
                for n, (w, a) in enumerate(((w_hi, act_hi), (w_hi, act_lo), (w_lo, act_hi))):
                    for b in range(2):
                        ins = pe.matmul(ps[:, slot, b * HALF:(b + 1) * HALF], w[:, w_slot, col:col + P],
                                        a[:, k, b * HALF:(b + 1) * HALF],
                                        start=first and n == 0, stop=last and n == 2)
                return ins

            def unit(where, i, step, norm=None):
                ws = weights(where, i)
                slot = slot_of(where, step)
                for k in range(KC):
                    if norm is not None:
                        pe.wait_ge(*hhi_done.at(norm, k + 1))
                        pe.wait_ge(*hlo_done.at(norm, k + 1))
                    ins = three_passes(slot, ws, k * P, h_hi, h_lo, k, k == 0, k == KC - 1)
                ins.then_inc(full[slot].sem, 1)

            def turn(where, step, source):
                slot = slot_of(where, step)
                for t in range(TT):
                    ins = pe.transpose(ps[:, slot, t * P:(t + 1) * P], source(t), ident)
                ins.then_inc(full[slot].sem, 1)

            def partial(where, block0, act_hi, act_lo, hi_t, lo_t, slot_read):
                for half in range(2):
                    ws = weights(where, block0 + half)
                    for k in range(2):
                        if half == 0:
                            pe.wait_ge(*hi_t.at(where, k + 1))
                            pe.wait_ge(*lo_t.at(where, k + 1))
                        for j in range(4):
                            slot = slot_of(where, f"W{4 * half + j}")
                            if k == 0 and half == 0:
                                pe.wait_ge(*slot_read[j])
                            elif k == 0:
                                pe.wait_ge(*res_done.at(where, j + 1))
                            ins = three_passes(slot, ws, k * HALF + j * P, act_hi, act_lo, k, k == 0, k == 1)
                            if k == 1:
                                ins.then_inc(full[slot].sem, 1)

            def norm_stats(where):
                pe.wait_ge(*acc_done.at(where, KC - 1))
                slot = slot_of(where, "ST")
                for t in range(TT):
                    ins = pe.matmul(ps[:, slot, t:t + 1], acc[:, t * P:(t + 1) * P], ones[:, 0:1], start=True, stop=True)
                ins.then_inc(full[slot].sem, 1)
                slot = slot_of(where, "R")
                pe.wait_ge(*diag_done.at(where, 1))
                for b in range(2):
                    ins = pe.matmul(ps[:, slot, b * HALF:(b + 1) * HALF], ones[:, :], diag[:, b * HALF:(b + 1) * HALF],
                                    start=True, stop=True)
                ins.then_inc(full[slot].sem, 1)

            pe.sem_inc(ada_used, 8)
            pe.wait_ge(const_in, 16)
            pe.wait_ge(rows_in, 16 * 10)
            pe.wait_ge(ones_set, 2)
            for i, n in enumerate((R_ALL, 4 * FC, 4 * FC)):
                n = min(n, R_ALL if i == 0 else 2 * 2 * FC)
                ins = pe.transpose(ps[:, 0, i * P:i * P + n], rows[0:n, i, :], cst[0:n, C_ID:C_ID + n])
            ins.then_inc(vec_turned, 1)
            pe.wait_ge(sil_done, 1)
            with pe.Fori(0, 3) as it:
                for s in range(8):
                    pe.wait_ge(ada_in[s], it * 16 + 16)
                    for j in range(2):
                        for k in range(KC):
                            ins = pe.matmul(ps[:, 1, bass.ds(it * 32 + (4 * s + 2 * j), 2)], ada[:, s, k, j * P:(j + 1) * P],
                                            small[:, 7, k:2 * KC:KC], start=k == 0, stop=k == KC - 1)
                    ins.then_inc(ada_used, 1)
            pe.wait_ge(setup_done, 1)

            with pe.Fori(0, N_SEQ) as seq:
                pre = ("pre", seq, 0)
                for t in range(TT):
                    pe.wait_ge(*x_in[t % 4].at(pre, 16 * (t // 4 + 1)))
                    if t < 4:
                        for i in range(2):
                            pe.wait_ge(*y_copied[i].at(pre, 0))
                    else:
                        pe.wait_ge(*xT_set[t % 2].at(pre, (t - 4) // 2 + 1))
                    turn(pre, f"X{t}", lambda k: xin[:, t % 4, k * P:(k + 1) * P])
                norm_stats(pre)
                with pe.Fori(0, PAIRS) as pr:
                    where = ("mix", seq, pr)
                    pe.wait_ge(*res_done.at(where, 0))
                    for i in range(4):
                        ws = weights(where, i)
                        for k in (2 * i, 2 * i + 1):
                            pe.wait_ge(*hhi_done.at(pre, k + 1))
                            pe.wait_ge(*hlo_done.at(pre, k + 1))
                        for t in range(TT):
                            slot = slot_of(where, f"Q{t // 2}")
                            for k in (2 * i, 2 * i + 1):
                                col = (k % 2) * HALF
                                for n, (a, w) in enumerate(((h_hi, w_hi), (h_hi, w_lo), (h_lo, w_hi))):
                                    ins = pe.matmul(ps[:, slot, (t % 2) * HALF:(t % 2 + 1) * HALF],
                                                    a[:, k, t * P:(t + 1) * P], w[:, ws, col:col + HALF],
                                                    start=k == 0 and n == 0, stop=k == KC - 1 and n == 2)
                            if i == 3 and t % 2:
                                ins.then_inc(full[slot].sem, 1)
                        if i < 3:
                            ins.then_inc(q_block.sem, 1)

                    def decayed(h):
                        pe.wait_ge(*qd_done.at(where, h + 1))
                        if h == 0:
                            pe.wait_ge(*p_copied.at(where, 1))
                        else:
                            pe.wait_ge(*state_step.at(where, 16))
                        turn(where, f"TD{h}", lambda t: tokb[:, t, :])
                        slot = slot_of(where, f"KV{h}")
                        if h == 0:
                            pe.wait_ge(*qT_done.at(where, 1))
                        else:
                            pe.wait_ge(*pt_done.at(where, 1))
                        pe.wait_ge(*kd_done.at(where, h + 1))
                        pe.wait_ge(*v_done.at(where, 4))
                        for t in range(TT):
                            ins = pe.matmul(ps[:, slot, t * P:(t + 1) * P], kdp[:, t, :], v_sb[:, t, h * P:(h + 1) * P],
                                            start=True, stop=True)
                        ins.then_inc(full[slot].sem, 1)
                        slot = slot_of(where, f"SC{h}")
                        if h:
                            pe.wait_ge(*ta_done.at(where, 1))
                        pe.wait_ge(*qT_done.at(where, 1))
                        pe.wait_ge(*kT_done.at(where, 1))
                        rows_h = slice(h * DK, (h + 1) * DK)
                        for t in range(TT):
                            ins = pe.matmul(ps[:, slot, t * P:(t + 1) * P], kT[rows_h, t * P:(t + 1) * P],
                                            qT[rows_h, t * P:(t + 1) * P], start=True, stop=True)
                        ins.then_inc(full[slot].sem, 1)

                    def outputs(h):
                        slot = slot_of(where, f"O{h}")
                        if h:
                            pe.wait_ge(*cent_done.at(where, 1))
                        pe.wait_ge(*pt_done.at(where, h + 1))
                        pe.wait_ge(*state_step.at(where, 16 * (h + 1)))
                        pe.wait_ge(*qdT_done.at(where, h + 1))
                        for t in range(TT):
                            o = ps[:, slot, t * P:(t + 1) * P]
                            pe.matmul(o, kdp[:, t, :], v_sb[:, t, h * P:(h + 1) * P], start=True, stop=False)
                            ins = pe.matmul(o, qdT[:, t * P:(t + 1) * P], state[:, t * P:(t + 1) * P], start=False, stop=True)
                        ins.then_inc(full[slot].sem, 1)

                    def branch_b(h):
                        slot = slot_of(where, f"BB{h}")
                        if h == 0:
                            pe.wait_ge(*state_step.at(where, 32))
                        else:
                            pe.wait_ge(*sw_done.at(where, 2))
                        pe.wait_ge(*pool_step.at(where, 8))
                        pe.wait_ge(*wpool_in.at(where, 16))
                        for b in range(2):
                            ins = pe.matmul(ps[:, slot, b * HALF:(b + 1) * HALF], wpool[:, h * P:(h + 1) * P],
                                            poolU[:, b * HALF:(b + 1) * HALF], start=True, stop=True)
                        ins.then_inc(full[slot].sem, 1)

                    def turn_ret(h):
                        pe.wait_ge(*retn_done.at(where, h + 1))
                        if h == 0:
                            pe.wait_ge(*pt_done.at(where, 2))
                        else:
                            pe.wait_ge(*mb_done.at(where, 1))
                        turn(where, f"TR{h}", lambda t: tokb[:, t, :])

                    pe.wait_ge(*v_done.at(where, 1))
                    unit(where, 4, "P")
                    pe.wait_ge(*v_done.at(where, 2))
                    unit(where, 5, "GS0")
                    pe.wait_ge(*rope_done.at(where, 4))
                    pe.wait_ge(*v_done.at(where, 4))
                    for i, step in enumerate(("TQ", "TK")):
                        turn(where, step, lambda t: rot[:, t, i * P:(i + 1) * P])
                    decayed(0)
                    pe.wait_ge(*sw_done.at(where, 1))
                    unit(where, 6, "GA0")
                    outputs(0)
                    decayed(1)
                    pe.wait_ge(*qdT_done.at(where, 2))
                    unit(where, 7, "GB0")
                    outputs(1)
                    branch_b(0)
                    turn_ret(0)
                    pe.wait_ge(*tb_done.at(where, 1))
                    unit(where, 8, "GS1")
                    pe.wait_ge(*cent_done.at(where, 2))
                    unit(where, 9, "GA1")
                    turn_ret(1)
                    pe.wait_ge(*ma_done.at(where, 1))
                    unit(where, 10, "GB1")
                    branch_b(1)
                    partial(where, 11, m_hi, m_lo, mhi_done, mlo_done,
                            [ta_done.at(where, 2), tb_done.at(where, 2), mb_done.at(where, 2), ma_done.at(where, 2)])
                mid = ("mid", seq, 0)
                norm_stats(mid)
                with pe.Fori(0, GROUPS) as g:
                    where = ("ffn", seq, g)
                    pe.wait_ge(*res_done.at(where, 0))
                    for i in range(4):
                        unit(where, i, f"U{i}", mid if i == 0 else None)
                    partial(where, 4, a_hi, a_lo, ahi_done, alo_done,
                            [side_tap.at(where, 2 * i + 2) for i in range(4)])
                post = ("post", seq, 0)
                norm_stats(post)
                pe.wait_ge(*y_scaled.at(post, KC))
                for t in range(TT):
                    if t >= 4:
                        pe.wait_ge(*y_copied[t % 2].at(post, (t - 4) // 2 + 1))
                    turn(post, f"Y{t}", lambda k: xT[:, k, t * P:(t + 1) * P])

        @block.scalar
        def _(act):
            def split(where, i):
                act.wait_ge(*raw_in[i % 2].at(where, brought(where[0], i)))
                act.activation(w_hi[:, BLOCKS[where[0]][i][1], :], w_raw[:, i % 2, :], ACT.Copy).then_inc(hi_done.sem, 1)

            def evac(where, step, dst, t):
                slot = slot_of(where, step)
                act.wait_ge(*filled(where, step))
                act.activation(dst, ps[:, slot, :], ACT.Copy).then_inc(t.sem, 1)

            def tanh_half(where, step, dst, t):
                slot = slot_of(where, step)
                act.wait_ge(*filled(where, step))
                act.activation(dst[:, :], ps[:, slot, :], ACT.Tanh, scale=0.5).then_inc(t.sem, 1)

            def squares(where, ready):
                for k in range(KC):
                    ready(k)
                    if k >= 3:
                        act.wait_ge(*acc_done.at(where, k - 2))
                    dst = acc[:, :] if k == 0 else sq[:, k % 2, :]
                    act.activation(dst, xT[:, k, :], ACT.Square).then_inc(sq_done.sem, 1)

            def modulate(where, shift, scale):
                for k in range(KC):
                    act.wait_ge(*tn_done.at(where, k + 1))
                    if k >= 2:
                        act.wait_ge(*hlo_done.at(where, k - 1))
                    a, b = modS[:, scale + k:scale + k + 1], modS[:, shift + k:shift + k + 1]
                    act.activation(hf[:, k % 2, :], tn[:, k % 2, :], ACT.Identity, bias=b, scale=a)
                    act.activation(h_hi[:, k, :], tn[:, k % 2, :], ACT.Identity, bias=b, scale=a).then_inc(hhi_done.sem, 1)

            for t in [y_copied[1]] + y_out:
                act.sem_inc(t.sem, 1)
            act.wait_ge(table_step, 1)
            act.activation(small[:, 1, :], small[:, 0, :], ACT.Exp, scale=-1.0).then_inc(table_act, 1)
            act.wait_ge(vec_done, 1)
            act.activation(small[:, 6, :], vecT[:, R_C:R_C + 2 * KC], ACT.Tanh, scale=0.5).then_inc(sil_tanh, 1)
            act.wait_ge(table_args, 1)
            act.activation(pairT[:, :, 0:T_GAIN], pairT[:, :, 0:T_GAIN], ACT.Exp).then_inc(table_act, 1)
            first = ("mix", 0, 0)
            split(first, 0)
            split(first, 1)
            act.wait_ge(setup_done, 1)

            with act.Fori(0, N_SEQ) as seq:
                pre = ("pre", seq, 0)

                def load_x(t):
                    act.wait_ge(*y_out[t % 4].at(pre, 0))
                    act.dma_start(xin[:, t % 4, :], x[bass.ds(seq * S + t * P, P), :]).then_inc(x_in[t % 4].sem, 16)

                for t in range(4):
                    load_x(t)
                for t in range(TT):
                    slot = slot_of(pre, f"X{t}")
                    act.wait_ge(*filled(pre, f"X{t}"))
                    if t + 4 < TT:
                        load_x(t + 4)
                    if t % 2:
                        act.activation(xT[:, :, t * P:(t + 1) * P], sq_view(ps[:, slot, :], KC),
                                       ACT.Copy).then_inc(xT_set[1].sem, 1)

                def x_ready(k):
                    if k == 0:
                        act.wait_ge(*xT_set[0].at(pre, TT // 2))
                        act.wait_ge(*xT_set[1].at(pre, TT // 2))
                        act.wait_ge(*mod_set.at(pre, 1))
                squares(pre, x_ready)
                evac(pre, "R", rrow[:, :], rrow_done)
                modulate(pre, 0, 8)
                with act.Fori(0, PAIRS) as pr:
                    where = ("mix", seq, pr)
                    split(where, 2)
                    act.wait_ge(*q_block.at(where, 1))
                    split(where, 3)
                    act.wait_ge(*q_block.at(where, 2))
                    split(where, 4)
                    act.wait_ge(*dec_arg.at(where, 4))
                    act.activation(dec[:, :, :], dec[:, :, :], ACT.Exp).then_inc(dec_done.sem, 1)
                    act.wait_ge(*q_block.at(where, 3))
                    split(where, 5)
                    for i in range(4):
                        slot = slot_of(where, f"Q{i}")
                        act.wait_ge(*filled(where, f"Q{i}"))
                        act.wait_ge(*rope_mul.at(where, i + 1))
                        act.activation(v_sb[:, 2 * i:2 * i + 2, :], sq_view(ps[:, slot, :], 2)[:, :, 2 * P:4 * P],
                                       ACT.Copy).then_inc(v_done.sem, 1)
                    evac(where, "P", state[:, PAD:PAD + S], p_copied)
                    act.wait_ge(*filled(where, "Q3"))
                    split(where, 6)
                    act.wait_ge(*rope_done.at(where, 4))
                    tanh_half(where, "GS0", bufA, th_done)
                    act.wait_ge(*filled(where, "P"))
                    split(where, 7)
                    evac(where, "TQ", qT[:, :], qT_done)
                    evac(where, "TK", kT[:, :], kT_done)
                    evac(where, "TD0", qdT[:, :], qdT_done)
                    act.wait_ge(*filled(where, "GS0"))
                    split(where, 8)
                    tanh_half(where, "GA0", bufB, ta_done)
                    evac(where, "TD1", qdT[:, :], qdT_done)
                    act.wait_ge(*filled(where, "GA0"))
                    split(where, 9)
                    act.wait_ge(*ga_done.at(where, 1))
                    tanh_half(where, "GB0", bufB, tb_done)
                    act.wait_ge(*filled(where, "GB0"))
                    split(where, 10)
                    act.wait_ge(*mg_done.at(where, 1))
                    act.activation(m_hi[:, 0, :], bufA[:, :], ACT.Copy).then_inc(mhi_done.sem, 1)
                    act.wait_ge(*mlo_done.at(where, 1))
                    tanh_half(where, "GS1", bufA, th_done)
                    act.wait_ge(*filled(where, "GS1"))
                    split(where, 11)
                    tanh_half(where, "GA1", bufB, ta_done)
                    act.wait_ge(*ga_done.at(where, 2))
                    tanh_half(where, "GB1", bufB, tb_done)
                    act.wait_ge(*filled(where, "GB1"))
                    split(where, 12)
                    act.wait_ge(*mg_done.at(where, 2))
                    act.activation(m_hi[:, 1, :], bufA[:, :], ACT.Copy).then_inc(mhi_done.sem, 1)
                    act.wait_ge(*filled(where, "GA1"))
                    split(("mix", seq, pr + 1), 0)
                    act.wait_ge(*filled(where, "W7"))
                    split(("mix", seq, pr + 1), 1)
                mid = ("mid", seq, 0)
                squares(mid, lambda k: act.wait_ge(*res_done.at(("mix", seq, PAIRS - 1), k + 1)))
                evac(mid, "R", rrow[:, :], rrow_done)
                modulate(mid, 24, 32)
                with act.Fori(0, GROUPS) as g:
                    where = ("ffn", seq, g)

                    def middle_tap(i, dst):
                        slot = slot_of(where, f"U{i}")
                        act.wait_ge(*filled(where, f"U{i}"))
                        col = convS[:, i % 2, i // 2, :]
                        act.activation(dst[:, :], ps[:, slot, :], ACT.Identity, bias=col[:, 3:4],
                                       scale=col[:, 1:2]).then_inc(mid_tap.sem, 1)

                    def gelu(j):
                        act.wait_ge(*side_tap.at(where, 4 * j + 2))
                        act.activation(ca[:, :], ca[:, :], ACT.Gelu_apprx_tanh).then_inc(gelu_done.sem, 1)

                    def high(j):
                        act.wait_ge(*prod_done.at(where, j + 1))
                        act.activation(a_hi[:, j, :], cl[:, :], ACT.Copy).then_inc(ahi_done.sem, 1)

                    act.wait_ge(*conv_set.at(where, 1))
                    middle_tap(0, ca)
                    split(where, 2)
                    gelu(0)
                    middle_tap(1, cl)
                    act.wait_ge(*filled(where, "U0"))
                    split(where, 3)
                    high(0)
                    middle_tap(2, ca)
                    act.wait_ge(*filled(where, "U1"))
                    split(where, 4)
                    gelu(1)
                    act.wait_ge(*alo_done.at(where, 1))
                    middle_tap(3, cl)
                    act.wait_ge(*filled(where, "U2"))
                    split(where, 5)
                    high(1)
                    act.wait_ge(*filled(where, "U3"))
                    split(("ffn", seq, g + 1), 0)
                    act.wait_ge(*filled(where, "W3"))
                    split(("ffn", seq, g + 1), 1)
                post = ("post", seq, 0)
                squares(post, lambda k: act.wait_ge(*res_done.at(("ffn", seq, GROUPS - 1), k + 1)))
                evac(post, "R", rrow[:, :], rrow_done)
                for t in range(TT):
                    if t % 2:
                        if t >= 4:
                            act.wait_ge(*y_out[t % 4].at(post, 16))
                        evac(post, f"Y{t}", xin[:, t % 4, :], y_copied[1])
                    act.wait_ge(*y_copied[t % 2].at(post, t // 2 + 1))
                    act.dma_start(y[bass.ds(seq * S + t * P, P), :], xin[:, t % 4, :]).then_inc(y_out[t % 4].sem, 16)
            for i in range(4):
                act.wait_ge(*y_out[i].at(("post", N_SEQ - 1, 0), 32))

        @block.gpsimd
        def _(pool):
            def remainder(where, i):
                ws = BLOCKS[where[0]][i][1]
                pool.wait_ge(*hi_done.at(where, i + 1))
                pool.tensor_tensor(w_lo[:, ws, :], w_raw[:, i % 2, :], w_hi[:, ws, :].bitcast(F32),
                                   ALU.subtract).then_inc(lo_done.sem, 1)

            def inverse_root(dst, src):
                return pool.tensor_tensor(dst, src, mhalf[:, :], ALU.pow)

            def norm_rstd(where):
                pool.wait_ge(*msq_done.at(where, 1))
                inverse_root(rstd[:, :], msq[:, :]).then_inc(rstd_done.sem, 1)

            pool.sem_inc(lo_done.sem, 1)
            pool.wait_ge(ones_set, 2)
            first = ("mix", 0, 0)
            remainder(first, 0)
            remainder(first, 1)
            with pool.Fori(0, N_SEQ) as seq:
                norm_rstd(("pre", seq, 0))
                with pool.Fori(0, PAIRS) as pr:
                    where = ("mix", seq, pr)
                    for i in range(2, N_MIX):
                        remainder(where, i)
                        if i in (9, 10):
                            h = i - 9
                            pool.wait_ge(*veps_done.at(where, h + 1))
                            inverse_root(grs[:, :], veps[:, :]).then_inc(grs_done.sem, 1)
                    remainder(("mix", seq, pr + 1), 0)
                    remainder(("mix", seq, pr + 1), 1)
                norm_rstd(("mid", seq, 0))
                with pool.Fori(0, GROUPS) as g:
                    for i in range(2, N_FFN):
                        remainder(("ffn", seq, g), i)
                    remainder(("ffn", seq, g + 1), 0)
                    remainder(("ffn", seq, g + 1), 1)
                norm_rstd(("post", seq, 0))

        @block.vector
        def _(dve):
            steps = [0]

            def step(ins):
                ins.then_inc(table_step, 1)
                steps[0] += 1
                dve.wait_ge(table_step, steps[0])

            def norm_scale(where):
                for k in range(1, KC):
                    dve.wait_ge(*sq_done.at(where, k + 1))
                    if k > 1:
                        dve.wait_ge(*acc_done.at(where, k - 1))
                    dve.tensor_tensor(acc[:, :], acc[:, :], sq[:, k % 2, :], ALU.add).then_inc(acc_done.sem, 1)
                slot = slot_of(where, "ST")
                dve.wait_ge(*filled(where, "ST"))
                dve.tensor_scalar(msq[:, :], ps[:, slot, 0:TT], 1.0 / D, EPS, ALU.mult, ALU.add).then_inc(msq_done.sem, 1)
                dve.wait_ge(*rstd_done.at(where, 1))
                for t in range(TT):
                    ins = dve.tensor_scalar(diag[:, t * P:(t + 1) * P], ident, rstd[:, t:t + 1], None, ALU.mult)
                ins.then_inc(diag_done.sem, 1)
                dve.wait_ge(*rrow_done.at(where, 1))

            def norm_apply(where):
                for k in range(KC + 1):
                    if k < KC:
                        if k >= 2:
                            dve.wait_ge(*hhi_done.at(where, k - 1))
                        dve.tensor_tensor(tn[:, k % 2, :], xT[:, k, :], rrow[:, :], ALU.mult).then_inc(tn_done.sem, 1)
                    if k:
                        dve.wait_ge(*hhi_done.at(where, k))
                        dve.tensor_tensor(h_lo[:, k - 1, :], hf[:, (k - 1) % 2, :], h_hi[:, k - 1, :].bitcast(F32),
                                          ALU.subtract).then_inc(hlo_done.sem, 1)

            def update_residual(where, gate):
                for d in range(KC):
                    slot = slot_of(where, f"W{d}")
                    dve.wait_ge(*filled(where, f"W{d}"))
                    dve.scalar_tensor_tensor(xT[:, d, :], ps[:, slot, :], modS[:, gate + d:gate + d + 1], xT[:, d, :],
                                             ALU.mult, ALU.add).then_inc(res_done.sem, 1)

            dve.sem_inc(res_done.sem, 1)
            dve.sem_inc(y_copied[0].sem, 1)
            dve.sem_inc(mb_done.sem, 1)
            dve.memset(ones[:, :], 1.0).then_inc(ones_set, 1)
            dve.memset(mhalf[:, :], -0.5).then_inc(ones_set, 1)
            dve.wait_ge(decay_in, 32)
            logit = lg[:, :, :, :].rearrange("p a b c -> p (a b c)")
            step(dve.scalar_tensor_tensor(small[:, 0, :], logit, -1.0, logit, ALU.mult, ALU.max))
            dve.wait_ge(table_act, 1)
            step(dve.tensor_scalar(small[:, 2, :], small[:, 1, :], 2.0, None, ALU.add))
            step(dve.reciprocal(small[:, 2, :], small[:, 2, :]))
            step(dve.tensor_tensor(small[:, 3, :], small[:, 1, :], small[:, 2, :], ALU.mult))
            step(dve.tensor_tensor(small[:, 4, :], small[:, 3, :], small[:, 3, :], ALU.mult))
            step(dve.tensor_scalar(small[:, 5, :], small[:, 4, :], 1.0 / 17, None, ALU.mult))
            for k in range(7, 0, -1):
                step(dve.scalar_tensor_tensor(small[:, 5, :], small[:, 5, :], 1.0 / (2 * k + 1), small[:, 4, :],
                                              ALU.add, ALU.mult))
            step(dve.scalar_tensor_tensor(small[:, 5, :], small[:, 5, :], 1.0, small[:, 3, :], ALU.add, ALU.mult))
            step(dve.tensor_scalar(small[:, 0, :], logit, 0.0, None, ALU.min))
            step(dve.scalar_tensor_tensor(logit, small[:, 5, :], -2.0, small[:, 0, :], ALU.mult, ALU.add))
            dve.wait_ge(const_in, 16)
            for i, col in enumerate((T_DQ, T_DK)):
                for d in range(2):
                    pos = cst[:, C_POS + 2 * i + d:C_POS + 2 * i + d + 1]
                    dve.tensor_scalar(pairT[:, :, col + d:col + 4:2], lg[:, d, :, :], pos, None, ALU.mult)
            for d in range(2):
                half = slice(d * DK, (d + 1) * DK)
                dve.tensor_scalar(pairT[half, :, T_DC:T_DC + 2], lg[half, d, :, :], float(P), None, ALU.mult)
            for d, col in enumerate((T_LGF, T_LGB)):
                ins = dve.tensor_copy(pairT[:, :, col:col + 2], lg[:, d, :, :])
            ins.then_inc(table_args, 1)
            dve.wait_ge(vec_turned, 1)
            dve.tensor_copy(vecT[:, :], ps[:, 0, 0:R_ALL]).then_inc(vec_done, 1)
            for i in range(2):
                ins = dve.tensor_copy(convT[:, :, 2 * i:2 * i + 2],
                                      ps[:, 0, (i + 1) * P:(i + 1) * P + 4 * FC].rearrange("p (t j) -> p j t", t=2))
            dve.wait_ge(sil_tanh, 1)
            step(dve.scalar_tensor_tensor(small[:, 6, :], small[:, 6, :], 1.0, vecT[:, R_C:R_C + 2 * KC], ALU.add, ALU.mult))
            dve.tensor_scalar(small[:, 7, :], small[:, 6, :], 0.5, None, ALU.mult).then_inc(sil_done, 1)
            dve.wait_ge(table_act, 2)
            dve.tensor_scalar(pairT[:, :, T_DK:T_DK + 4], pairT[:, :, T_DK:T_DK + 4], K_SCALE, None, ALU.mult)
            for col, row, factor in ((T_GAIN, R_GAIN, 0.25), (T_PS, R_PS, 0.5)):
                step(dve.tensor_scalar(pairT[:, :, col:col + 2], vecT[:, row:row + 8].rearrange("p (a b) -> p a b", b=2),
                                       factor, None, ALU.mult))
            dve.wait_ge(ada_used, 24 + 8)
            step(dve.tensor_tensor(modT[:, :, :], ps[:, 1, 0:96].rearrange("p (a s) -> p s a", s=2),
                                   vecT[:, R_BADA:R_BADA + 48].unsqueeze(1).to_broadcast([P, 2, 48]), ALU.add))
            for col, row in ((8, R_GMIX), (32, R_GFFN)):
                step(dve.scalar_tensor_tensor(modT[:, :, col:col + 8], modT[:, :, col:col + 8], 1.0,
                                              vecT[:, row:row + 8].unsqueeze(1).to_broadcast([P, 2, 8]), ALU.add, ALU.mult))
            dve.sem_inc(setup_done, 1)

            with dve.Fori(0, N_SEQ) as seq:
                pre = ("pre", seq, 0)
                dve.tensor_copy(modS[:, :], modT[:, bass.ds(seq, 1), :].rearrange("p a b -> p (a b)")).then_inc(mod_set.sem, 1)
                for t in range(0, TT, 2):
                    slot = slot_of(pre, f"X{t}")
                    dve.wait_ge(*filled(pre, f"X{t}"))
                    dve.tensor_copy(xT[:, :, t * P:(t + 1) * P], sq_view(ps[:, slot, :], KC)).then_inc(xT_set[0].sem, 1)
                norm_scale(pre)
                norm_apply(pre)
                with dve.Fori(0, PAIRS) as pr:
                    where = ("mix", seq, pr)

                    def scal(col):
                        return pairS[:, col:col + 1]

                    start_at = dve.snap(PAD - (pr * pr * pr + 5 * pr + 6) // 6)

                    dve.tensor_copy(pairS[:, 0:T_BUILT], pairT[:, bass.ds(pr, 1), :].rearrange("p a b -> p (a b)"))
                    dve.tensor_copy(pairS[:, T_BUILT:T_ALL],
                                    cst[:, bass.ds(pr * POOL_COLS + C_POOL, POOL_COLS)]).then_inc(pair_set.sem, 1)
                    dve.wait_ge(*pair_set.at(where, 1))
                    for h in range(2):
                        dve.tensor_scalar(dec[:, h, :], cst[:, C_DIFP:C_DIFP + P], scal(T_LGF + h), None,
                                          ALU.mult).then_inc(dec_arg.sem, 1)
                    for h in range(2):
                        dve.wait_ge(*dec_arg.at(where, h + 1))
                        dve.scalar_tensor_tensor(dec[:, h, :], cst[:, C_DIFN:C_DIFN + P], scal(T_LGB + h), dec[:, h, :],
                                                 ALU.mult, ALU.add).then_inc(dec_arg.sem, 1)

                    def rope_products(i):
                        slot = slot_of(where, f"Q{i}")
                        dve.wait_ge(*filled(where, f"Q{i}"))
                        qk = sq_view(ps[:, slot, :], 2)[:, :, 0:2 * P].rearrange("p t (v e) -> p t v e", e=32)
                        if i >= 2:
                            dve.wait_ge(*rope_done.at(where, i - 1))
                        for buf, col in ((bufA, C_COS), (bufB, C_SIN)):
                            table = cst[:, col + 64 * i:col + 64 * i + 64].rearrange("p (t e) -> p t e", t=2)
                            ins = dve.tensor_tensor(
                                buf[:, (i % 2) * HALF:(i % 2 + 1) * HALF].rearrange("p (t v e) -> p t v e", t=2, e=32),
                                qk, table.unsqueeze(2).to_broadcast([P, 2, 8, 32]), ALU.mult)
                        ins.then_inc(rope_mul.sem, 1)

                    def rope_sums(i):
                        dve.wait_ge(*rope_mul.at(where, i + 1))
                        a, b = (buf[:, (i % 2) * HALF:(i % 2 + 1) * HALF].rearrange("p (v s e) -> p v s e", s=2, e=32)
                                for buf in (bufA, bufB))
                        out = rot[:, 2 * i:2 * i + 2, :].rearrange("p t (v s e) -> p (t v) s e", s=2, e=32)
                        dve.tensor_tensor(out[:, :, 0, :], a[:, :, 0, :], b[:, :, 1, :], ALU.subtract)
                        dve.tensor_tensor(out[:, :, 1, :], a[:, :, 1, :], b[:, :, 0, :], ALU.add).then_inc(rope_done.sem, 1)

                    for i in range(5):
                        if i < 4:
                            rope_products(i)
                        if i:
                            rope_sums(i - 1)

                    def decayed(h, first_col, src, dst, t):
                        for d in range(2):
                            ins = dve.tensor_scalar(dst[:, :, d * DK:(d + 1) * DK], rot[:, :, src + h * DK:src + (h + 1) * DK],
                                                    scal(first_col + 2 * h + d), None, ALU.mult)
                        ins.then_inc(t.sem, 1)

                    f, b = slice(0, DK), slice(DK, P)

                    def first_states(h):
                        dve.memset(state[f, 0:P], 0.0).then_inc(state_step.sem, 1)
                        dve.memset(state[b, (TT - 1) * P:TT * P], 0.0).then_inc(state_step.sem, 1)

                    def states(h):
                        dc = T_DC + h
                        slot = slot_of(where, f"KV{h}")
                        dve.wait_ge(*filled(where, f"KV{h}"))
                        for n in range(1, TT):
                            for rows_d, last, new, back in ((f, n - 1, n, 2), (b, TT - n, TT - 1 - n, 2)):
                                at = 16 * h + 2 * n + (1 if rows_d is b else 0)
                                dve.wait_ge(*state_step.at(where, at + 1 - back))
                                dve.scalar_tensor_tensor(
                                    state[rows_d, new * P:(new + 1) * P], state[rows_d, last * P:(last + 1) * P],
                                    pairS[rows_d, dc:dc + 1], ps[rows_d, slot, last * P:(last + 1) * P],
                                    ALU.mult, ALU.add).then_inc(state_step.sem, 1)

                    def scores(h):
                        slot = slot_of(where, f"SC{h}")
                        dve.wait_ge(*filled(where, f"SC{h}"))
                        if h == 0:
                            dve.wait_ge(*dec_done.at(where, 1))
                        dve.scalar_tensor_tensor(kdp[:, :, :], sq_view(ps[:, slot, :], TT), K_SCALE,
                                                 dec[:, h, :].unsqueeze(1).to_broadcast([P, TT, P]),
                                                 ALU.mult, ALU.mult).then_inc(pt_done.sem, 1)

                    def statistics(h):
                        slot = slot_of(where, f"O{h}")
                        dve.wait_ge(*filled(where, f"O{h}"))
                        for t in range(TT):
                            ins = dve.bn_stats(bst[:, t, :], ps[:, slot, t * P:(t + 1) * P])
                        ins.then_inc(stat_done.sem, 1)

                    def aggregate(h):
                        for t in range(TT):
                            ins = dve.bn_aggr(mv[:, t, :], bst[:, t, :])
                        ins.then_inc(mv_done.sem, 1)
                        dve.wait_ge(*mv_done.at(where, h + 1))
                        dve.tensor_scalar(veps[:, :], mv[:, :, 1], EPS, None, ALU.add).then_inc(veps_done.sem, 1)

                    def centred(h, turned):
                        dve.wait_ge(*filled(where, turned))
                        slot = place("mix", f"O{h}")[0]
                        dve.tensor_tensor(tokb[:, :, :], sq_view(ps[:, slot, :], TT),
                                          mv[:, :, 0:1].to_broadcast([P, TT, P]), ALU.subtract).then_inc(cent_done.sem, 1)

                    def normed(h):
                        dve.wait_ge(*grs_done.at(where, h + 1))
                        dve.wait_ge(*cent_done.at(where, h + 1))
                        dve.tensor_tensor(tokb[:, :, :], tokb[:, :, :], grs[:, :].unsqueeze(2).to_broadcast([P, TT, P]),
                                          ALU.mult).then_inc(retn_done.sem, 1)

                    def swish(h):
                        slot = slot_of(where, f"GS{h}")
                        dve.wait_ge(*filled(where, f"GS{h}"))
                        dve.wait_ge(*th_done.at(where, h + 1))
                        dve.scalar_tensor_tensor(bufA[:, :], bufA[:, :], 1.0, ps[:, slot, :], ALU.add,
                                                 ALU.mult).then_inc(sw_done.sem, 1)

                    def gate_a(h):
                        dve.wait_ge(*ta_done.at(where, h + 1))
                        dve.wait_ge(*sw_done.at(where, h + 1))
                        dve.scalar_tensor_tensor(bufA[:, :], bufB[:, :], 1.0, bufA[:, :], ALU.add,
                                                 ALU.mult).then_inc(ga_done.sem, 1)

                    def branch_a(h):
                        slot = slot_of(where, f"TR{h}")
                        dve.wait_ge(*filled(where, f"TR{h}"))
                        dve.wait_ge(*ga_done.at(where, h + 1))
                        dve.scalar_tensor_tensor(bufA[:, :], ps[:, slot, :], scal(T_GAIN + h), bufA[:, :], ALU.mult,
                                                 ALU.mult).then_inc(ma_done.sem, 1)

                    def branch_b(h):
                        slot = slot_of(where, f"BB{h}")
                        dve.wait_ge(*filled(where, f"BB{h}"))
                        dve.wait_ge(*tb_done.at(where, h + 1))
                        dve.scalar_tensor_tensor(bufB[:, :], bufB[:, :], 1.0, ps[:, slot, :], ALU.add,
                                                 ALU.mult).then_inc(mb_done.sem, 1)

                    def merge(h):
                        dve.wait_ge(*ma_done.at(where, h + 1))
                        dve.wait_ge(*mb_done.at(where, h + 1))
                        dve.scalar_tensor_tensor(bufA[:, :], bufB[:, :], scal(T_PS + h), bufA[:, :], ALU.mult,
                                                 ALU.add).then_inc(mg_done.sem, 1)

                    def merge_low(h):
                        dve.wait_ge(*mhi_done.at(where, h + 1))
                        dve.tensor_tensor(m_lo[:, h, :], bufA[:, :], m_hi[:, h, :].bitcast(F32),
                                          ALU.subtract).then_inc(mlo_done.sem, 1)

                    dve.wait_ge(*rope_done.at(where, 4))
                    decayed(0, T_DQ, 0, tokb, qd_done)
                    decayed(0, T_DK, P, kdp, kd_done)

                    for at in (0, PAD + S):
                        dve.memset(state[:, at:at + PAD], 0.0).then_inc(pool_step.sem, 1)
                    dve.wait_ge(*p_copied.at(where, 1))
                    src, length = state, S + 2 * PAD
                    for level in range(4):
                        dve.wait_ge(*pool_step.at(where, 2 + level))
                        length -= 1 << level
                        dve.scalar_tensor_tensor(poolU[:, 0:length], src[:, 1 << level:(1 << level) + length],
                                                 scal(T_POOL + level), src[:, 0:length], ALU.mult,
                                                 ALU.add).then_inc(pool_step.sem, 1)
                        src = poolU
                    dve.wait_ge(*pool_step.at(where, 6))
                    for n, at in ((0, 0), (1, S - PAD)):
                        edge = poolU[:, bass.ds(start_at + at, PAD)]
                        ins = dve.tensor_tensor(edge, edge, pairS[:, T_POOL + 5 + 8 * n:T_POOL + 13 + 8 * n], ALU.mult)
                    ins.then_inc(pool_step.sem, 1)
                    dve.wait_ge(*pool_step.at(where, 7))
                    dve.scalar_tensor_tensor(poolU[:, 0:S], poolU[:, bass.ds(start_at, S)], scal(T_POOL + 4),
                                             state[:, PAD:PAD + S], ALU.mult, ALU.subtract).then_inc(pool_step.sem, 1)
                    swish(0)
                    dve.wait_ge(*pool_step.at(where, 8))
                    first_states(0)
                    states(0)
                    dve.wait_ge(*filled(where, "TD0"))
                    decayed(1, T_DQ, 0, tokb, qd_done)
                    scores(0)
                    gate_a(0)
                    dve.wait_ge(*filled(where, "O0"))
                    decayed(1, T_DK, P, kdp, kd_done)
                    statistics(0)
                    dve.wait_ge(*stat_done.at(where, 1))
                    first_states(1)
                    aggregate(0)
                    centred(0, "TD1")
                    states(1)
                    scores(1)
                    normed(0)
                    statistics(1)
                    dve.wait_ge(*stat_done.at(where, 2))
                    branch_b(0)
                    aggregate(1)
                    branch_a(0)
                    merge(0)
                    merge_low(0)
                    centred(1, "TR0")
                    normed(1)
                    swish(1)
                    gate_a(1)
                    branch_a(1)
                    branch_b(1)
                    merge(1)
                    merge_low(1)
                    update_residual(where, 16)
                norm_scale(("mid", seq, 0))
                norm_apply(("mid", seq, 0))
                with dve.Fori(0, GROUPS) as g:
                    where = ("ffn", seq, g)
                    dve.tensor_copy(convS[:, :, :, :], convT[:, :, :].rearrange("p (l c) t -> p l c t", l=2)[:, :, bass.ds(g * 2, 2), :]).then_inc(conv_set.sem, 1)

                    def side_taps(i, dst):
                        slot = place("ffn", f"U{i}")[0]
                        dve.wait_ge(*mid_tap.at(where, i + 1))
                        col = convS[:, i % 2, i // 2, :]
                        dve.scalar_tensor_tensor(dst[:, 1:S], ps[:, slot, 0:S - 1], col[:, 0:1], dst[:, 1:S],
                                                 ALU.mult, ALU.add).then_inc(side_tap.sem, 1)
                        dve.wait_ge(*side_tap.at(where, 2 * i + 1))
                        dve.scalar_tensor_tensor(dst[:, 0:S - 1], ps[:, slot, 1:S], col[:, 2:3], dst[:, 0:S - 1],
                                                 ALU.mult, ALU.add).then_inc(side_tap.sem, 1)

                    dve.wait_ge(*conv_set.at(where, 1))
                    for j in range(2):
                        side_taps(2 * j, ca)
                        side_taps(2 * j + 1, cl)
                        dve.wait_ge(*gelu_done.at(where, j + 1))
                        dve.wait_ge(*side_tap.at(where, 4 * j + 4))
                        dve.tensor_tensor(cl[:, :], cl[:, :], ca[:, :], ALU.mult).then_inc(prod_done.sem, 1)
                        dve.wait_ge(*ahi_done.at(where, j + 1))
                        dve.tensor_tensor(a_lo[:, j, :], cl[:, :], a_hi[:, j, :].bitcast(F32),
                                          ALU.subtract).then_inc(alo_done.sem, 1)
                    update_residual(where, 40)
                post = ("post", seq, 0)
                norm_scale(post)
                for k in range(KC):
                    dve.scalar_tensor_tensor(xT[:, k, :], xT[:, k, :], vecT[:, R_GFIN + k:R_GFIN + k + 1], rrow[:, :],
                                             ALU.mult, ALU.mult).then_inc(y_scaled.sem, 1)
                for t in range(0, TT, 2):
                    slot = slot_of(post, f"Y{t}")
                    dve.wait_ge(*filled(post, f"Y{t}"))
                    if t >= 4:
                        dve.wait_ge(*y_out[t % 4].at(post, 16))
                    dve.tensor_copy(xin[:, t % 4, :], ps[:, slot, :]).then_inc(y_copied[0].sem, 1)


def kernel(x_prompt, x_sample, c_prompt, c_sample, w_ada, b_ada, g_mix, w_in, ret_decay_f, ret_decay_b,
           ret_gn_gain, w_pool_grp, pool_scale, w_out, g_ffn, w_up, conv_w, conv_b, w_down, g_final):
    import concourse.bacc as bacc
    from concourse.bass_utils import run_bass_kernel_spmd

    arrays = {
        "x": np.concatenate([np.asarray(x_prompt), np.asarray(x_sample)], 0).reshape(N_SEQ * S, D),
        "c": np.concatenate([np.asarray(c_prompt), np.asarray(c_sample)], 0),
        "w_ada": np.asarray(w_ada)[0], "b_ada": np.asarray(b_ada)[0], "g_mix": np.asarray(g_mix)[0],
        "w_in": np.asarray(w_in)[0], "decay_f": np.asarray(ret_decay_f)[0], "decay_b": np.asarray(ret_decay_b)[0],
        "gn_gain": np.asarray(ret_gn_gain)[0], "w_pool": np.asarray(w_pool_grp)[0],
        "pool_scale": np.asarray(pool_scale)[0], "w_out": np.asarray(w_out)[0], "g_ffn": np.asarray(g_ffn)[0],
        "w_up": np.asarray(w_up)[0], "conv_w": np.asarray(conv_w)[0], "conv_b": np.asarray(conv_b)[0],
        "w_down": np.asarray(w_down)[0], "g_final": np.asarray(g_final), "consts": constants(),
    }
    arrays = {n: np.ascontiguousarray(a) for n, a in arrays.items()}
    nc = bacc.Bacc("TRN2", target_bir_lowering=False, num_devices=1)
    args = [nc.dram_tensor(f"in_{n}", a.shape, F32, kind="ExternalInput").ap() for n, a in arrays.items()]
    args.append(nc.dram_tensor("out_y", (N_SEQ * S, D), F32, kind="ExternalOutput").ap())
    encoder_program(nc, *args)
    r = run_bass_kernel_spmd(nc, [{f"in_{n}": a for n, a in arrays.items()}], core_ids=[0])
    y = r.results[0]["out_y"].reshape(N_SEQ, 1, S, D)
    return y[0], y[1]
```

```python
from contextlib import ExitStack

import numpy as np

import concourse.bass as bass
import concourse.mybir as mybir

F32 = mybir.dt.float32
F32R = mybir.dt.float32r
ACT = mybir.ActivationFunctionType
ALU = mybir.AluOpType

P = 128
D = 1024
S = 1024
KC = D // P
TT = S // P
HALF = 512
N_SEQ = 2
HEADS = 8
DK = 64
PAIRS = HEADS // 2
D_FF = 2816
FC = D_FF // P
GROUPS = FC // 2
POOL_W = 512
EPS = 1e-6
K_SCALE = DK ** -0.5
PAD = 8
Q0, K0, V0, GS0, P0 = 0, 512, 1024, 2048, 3072
GA0 = P0 + POOL_W
GB0 = GA0 + D

C_COS = 0
C_SIN = C_COS + TT * 32
C_DIFP = C_SIN + TT * 32
C_DIFN = C_DIFP + P
C_ID = C_DIFN + P
C_POS = C_ID + P
POOL_COLS = 21
C_POOL = C_POS + 4
C_ALL = C_POOL + PAIRS * POOL_COLS

T_DQ, T_DK, T_DC, T_GAIN, T_PS, T_LGF, T_LGB, T_POOL = 0, 4, 8, 10, 12, 14, 16, 18
T_BUILT = 18
T_ALL = T_BUILT + POOL_COLS

R_BADA, R_GMIX, R_GAIN, R_PS, R_GFFN, R_C, R_ALL = 0, 48, 56, 64, 72, 80, 96

ADA_RING = 8
ADA_GROUPS = 2 * D // HALF
ADA_PARTS = 3
ADA_ROWS = ADA_GROUPS * 2
Y_RING = 6


class Tally:

    ORDER = (("first", 0), ("mix", 0), ("mid", 0), ("ffn", 0), ("swap", 0), ("mix", 1), ("mid", 1), ("ffn", 1),
             ("last", 1))
    TIMES = {"first": 1, "mix": PAIRS, "mid": 1, "ffn": GROUPS, "swap": 1, "last": 1}

    def __init__(self, sem, setup=0, **per):
        self.sem, self.setup, self.per = sem, setup, per

    def at(self, where, n):
        region, seq, it = where
        base = self.setup + n
        for r, _ in self.ORDER[:self.ORDER.index((region, seq))]:
            base += self.TIMES[r] * self.per.get(r, 0)
        if self.per.get(region, 0) and self.TIMES[region] > 1:
            base = it * self.per[region] + base
        return self.sem, base


STEPS = {
    "first": [(f"X{t}", t % 4) for t in range(TT)] + [("R", 1)],
    "mix": [("Q0", 1), ("Q1", 2), ("Q2", 3), ("Q3", 0), ("P", 1), ("GS0", 2), ("TQ", 3), ("TK", 0), ("TD0", 1),
            ("KV0", 3), ("SC0", 0), ("GA0", 2), ("O0", 1), ("TD1", 3), ("KV1", 0), ("SC1", 2), ("GB0", 3),
            ("O1", 1), ("BB0", 0), ("TR0", 2), ("GS1", 3), ("GA1", 1), ("TR1", 0), ("GB1", 2), ("BB1", 3),
            ("W0", 1), ("W1", 2), ("W2", 3), ("W3", 0), ("W4", 1), ("W5", 2), ("W6", 3), ("W7", 0)],
    "mid": [("ST", 1), ("R", 0)],
    "ffn": [(f"U{i}", (i + 1) % 4) for i in range(4)] + [(f"W{d}", (d + 1) % 4) for d in range(KC)],
    "swap": [("X0", 1), ("X1", 2), ("X2", 3), ("X3", 0), ("Y0", 1), ("Y1", 2), ("X4", 3), ("X5", 0), ("Y2", 1), ("Y3", 2),
             ("X6", 3), ("X7", 0), ("Y4", 1), ("Y5", 2), ("R", 3), ("Y6", 0), ("Y7", 3)],
    "last": [(f"Y{t}", (t + 1) % 4) for t in range(TT)],
}
BLOCKS = {
    "mix": [(3, 0), (3, 1), (3, 2), (3, 0), (1, 1), (1, 0), (1, 2), (1, 1), (1, 0), (1, 2), (1, 1), (1, 0), (1, 2)],
    "ffn": [(3, 0), (3, 1), (1, 2), (1, 0), (1, 1), (1, 2)],
}
N_MIX, N_FFN = len(BLOCKS["mix"]), len(BLOCKS["ffn"])


def constants():
    c = np.zeros((P, C_ALL), np.float32)
    half = DK // 2
    inv = np.float32(10000.0) ** (-np.arange(half, dtype=np.float32) / np.float32(half))
    ang = np.arange(S, dtype=np.float32)[:, None] * inv[None, :].astype(np.float32)
    for col, f in ((C_COS, np.cos), (C_SIN, np.sin)):
        t = f(ang).astype(np.float32).reshape(TT, P, half).transpose(1, 0, 2)
        c[:, col:col + TT * half] = t.reshape(P, TT * half)
    p = np.arange(P)
    dif = p[None, :] - p[:, None]
    c[:, C_DIFP:C_DIFP + P] = np.maximum(dif, 0)
    c[:, C_DIFN:C_DIFN + P] = np.maximum(-dif, 0)
    c[:, C_ID:C_ID + P] = np.eye(P)
    c[:, C_POS:C_POS + 4] = np.stack([p + 1, P - p, P - 1 - p, p], 1)
    for g in range(PAIRS):
        w = 2 ** (g + 1)
        o = C_POOL + g * POOL_COLS
        c[:, o:o + 4] = [1.0 if level <= g else 0.0 for level in range(4)]
        c[:, o + 4] = 1.0 / w
        t = np.concatenate([np.arange(PAD), np.arange(S - PAD, S)])
        cnt = np.minimum(t + w // 2, S) - np.maximum(t - w // 2, 0)
        c[:, o + 5:o + 21] = np.float32(w) / cnt.astype(np.float32)
    return c


def encoder_program(nc, x, c, w_ada, b_ada, g_mix, w_in, decay_f, decay_b, gn_gain, w_pool, pool_scale,
                    w_out, g_ffn, w_up, conv_w, conv_b, w_down, g_final, consts, y):
    ctx = ExitStack()
    with ctx:
        def sb(name, shape, dt=F32, stack=ctx):
            return stack.enter_context(nc.sbuf_tensor(name, shape, dt))

        def sem(name):
            return ctx.enter_context(nc.semaphore(name))

        ps = ctx.enter_context(nc.psum_tensor("ps", [P, 4, 2 * HALF], F32))

        roles = ExitStack()
        xT = [sb("xT0", [P, KC, S], F32, roles)]
        h_hi = [sb("h_hi0", [P, KC, S], F32R, roles)]
        h_lo = [sb("h_lo0", [P, KC, S], F32R, roles)]
        roles.close()
        h_lo.append(sb("h_lo1", [P, KC, S], F32R))
        xT.append(sb("xT1", [P, KC, S]))
        h_hi.append(sb("h_hi1", [P, KC, S], F32R))
        w_raw = sb("w_raw", [P, 2, 1024])
        w_hi = sb("w_hi", [P, 3, 1024], F32R)
        w_lo = sb("w_lo", [P, 3, 1024], F32R)
        cst = sb("cst", [P, C_ALL])
        ones = sb("ones", [P, P])
        vecT = sb("vecT", [P, R_ALL])
        convT = sb("convT", [P, 2 * FC, 4])
        modT = sb("modT", [P, N_SEQ, 48])
        silT = sb("silT", [P, KC, 2 * ADA_ROWS - N_SEQ])
        pairT = sb("pairT", [P, PAIRS, T_BUILT])
        pairS = sb("pairS", [P, T_ALL])
        convS = sb("convS", [P, 2, 2, 4])
        lg = sb("lg", [P, 2, PAIRS, 2])
        small = sb("small", [P, 8, 16])
        msq = sb("msq", [P, TT])
        x_ms = sb("x_ms", [P, TT])
        y_ms = sb("y_ms", [P, TT])
        y_rstd = sb("y_rstd", [P, TT])
        rstd = sb("rstd", [P, TT])
        zeros = sb("zeros", [P, TT])
        mhalf = sb("mhalf", [P, TT])
        bst = sb("bst", [P, TT, 6])
        mv = sb("mv", [P, TT, 2])
        veps = sb("veps", [P, TT])
        grs = sb("grs", [P, TT])

        ident = cst[:, C_ID:C_ID + P]

        mix = ExitStack()
        m_hi = sb("m_hi", [P, 2, S], F32R, mix)
        m_lo = sb("m_lo", [P, 2, S], F32R, mix)
        rot = sb("rot", [P, TT, 256], F32, mix)
        v_sb = sb("v_sb", [P, TT, 256], F32, mix)
        tokb = sb("tokb", [P, TT, P], F32, mix)
        kdp = sb("kdp", [P, TT, P], F32, mix)
        qdT = sb("qdT", [P, S], F32, mix)
        qT = sb("qT", [P, S], F32, mix)
        kT = sb("kT", [P, S], F32, mix)
        state = sb("state", [P, S + 2 * PAD], F32, mix)
        bufA = sb("bufA", [P, S], F32, mix)
        bufB = sb("bufB", [P, S], F32, mix)
        poolU = sb("poolU", [P, S + 2 * PAD], F32, mix)
        dec = sb("dec", [P, 2, P], F32, mix)
        wpool = sb("wpool", [P, 256], F32, mix)
        mix.close()

        other = ExitStack()
        a_hi = sb("a_hi", [P, 2, S], F32R, other)
        a_lo = sb("a_lo", [P, 2, S], F32R, other)
        ca = sb("ca", [P, S], F32, other)
        cl = sb("cl", [P, S], F32, other)
        g_row = sb("g_row", [P, S], F32, other)
        spare = sb("spare", [P, S], F32, other)
        tn = sb("tn", [P, 2, S], F32, other)
        hf = sb("hf", [P, 2, S], F32, other)
        diag = sb("diag", [P, S], F32, other)
        xin = sb("xin", [P, 4, S], F32, other)
        rrow = sb("rrow", [P, S], F32, other)
        other.close()
        out = ExitStack()
        y_sb = sb("y_sb", [P, Y_RING, S], F32, out)
        out.close()
        start = ExitStack()
        ada = sb("ada", [P, ADA_RING, 2, HALF], F32, start)
        over_tn = sb("over_tn", [P, 2, S], F32, start)
        rows = sb("rows", [P, 3, P], F32, start)
        hf_rest = sb("hf_rest", [P, 2 * S - 3 * P], F32, start)
        diag_over = sb("diag_over", [P, S], F32, start)
        ada_rows = sb("ada_rows", [ADA_ROWS, 2, HALF], F32, start)
        start.close()
        sq = xin

        def tally(name, setup=0, **per):
            return Tally(sem(name), setup, **per)

        full = [tally(f"psum_full{n}", 0, **{r: sum(slot == n for _, slot in STEPS[r]) for r in STEPS})
                for n in range(4)]

        def place(region, step):
            slot = dict(STEPS[region])[step]
            turns = [name for name, other in STEPS[region] if other == slot]
            return slot, turns.index(step) + 1

        def brought(region, i):
            return 16 * sum(n for j, (n, _) in enumerate(BLOCKS[region]) if j % 2 == i % 2 and j <= i)

        raw_in = [tally(f"raw_in{r}", 0, mix=brought("mix", N_MIX - 1 - (N_MIX - 1 - r) % 2),
                        ffn=brought("ffn", N_FFN - 2 + r)) for r in range(2)]
        hi_done = tally("w_hi_done", 0, mix=N_MIX, ffn=N_FFN)
        lo_done = tally("w_lo_done", 1, mix=N_MIX, ffn=N_FFN)
        q_block = tally("q_block_used", 0, mix=3)

        const_in = sem("const_in")
        rows_in = sem("rows_in")
        decay_in = sem("decay_in")
        ones_set = sem("ones_set")
        ada_in = [sem(f"ada_in{i}") for i in range(ADA_RING)]
        ada_used = sem("ada_used")
        ada_rows_set = sem("ada_rows_set")
        ada_turned = sem("ada_turned")
        mod_based = sem("mod_based")
        mod_ready = sem("mod_ready")
        vec_done = sem("vec_done")
        table_step = sem("table_step")
        sil_step = sem("sil_step")
        table_act = sem("table_act")
        table_args = sem("table_args")
        sil_tanh = sem("sil_tanh")
        sil_done = sem("sil_done")

        vec_turned = sem("vec_turned")
        x_in = [tally(f"x_in{i}", 0, first=32, swap=32) for i in range(4)]
        x_squared = tally("x_squared", 0, first=TT, swap=TT)
        xT_set = [tally(f"xT_set_{e}", 0, first=TT // 2, swap=TT // 2) for e in ("dve", "act")]
        sq_done = tally("sq_done", 0, mid=KC)
        sq_used = tally("sq_used", 0, mid=KC)
        msq_done = tally("msq_done", 0, mid=1)
        rstd_done = tally("rstd_done", 0, first=1, mid=1, swap=1)
        diag_done = tally("diag_done", 0, first=2, mid=2, swap=2)
        rrow_done = tally("rrow_done", 0, first=1, swap=1)
        tn_done = tally("tn_done", 0, first=KC, mid=KC, swap=KC)
        hhi_done = tally("h_hi_done", 0, first=KC, mid=KC, swap=KC)
        hlo_done = tally("h_lo_done", 0, first=KC, mid=KC, swap=KC)
        res_done = tally("residual_done", 4, mix=KC, ffn=KC)
        g_row_in = tally("g_row_in", 0, mid=16)
        y_squared = tally("y_squared", 0, swap=TT, last=TT)
        x_eps = tally("x_plus_eps", 0, first=1, swap=1)
        y_eps = tally("y_plus_eps", 0, swap=TT // 2, last=TT // 2)
        y_rstd_done = tally("y_rstd_done", 0, swap=TT // 2, last=TT // 2)
        y_scaled = tally("y_scaled", 0, swap=TT, last=TT)
        y_out = [tally(f"y_out{i}", 0, swap=16 * len(range(i, TT, Y_RING)), last=16 * len(range(i, TT, Y_RING)))
                 for i in range(Y_RING)]

        pair_set = tally("pair_set", 0, mix=1)
        dec_arg = tally("dec_arg", 0, mix=4)
        dec_done = tally("dec_done", 0, mix=1)
        wpool_in = tally("wpool_in", 0, mix=16)
        v_done = tally("v_done", 0, mix=4)
        rope_mul = tally("rope_mul", 0, mix=4)
        rope_done = tally("rope_done", 0, mix=4)
        qT_done = tally("qT_done", 0, mix=1)
        kT_done = tally("kT_done", 0, mix=1)
        qd_done = tally("qd_done", 0, mix=2)
        kd_done = tally("kd_done", 0, mix=2)
        qdT_done = tally("qdT_done", 0, mix=2)
        state_step = tally("state_step", 0, mix=2 * (2 + 14))
        pt_done = tally("scores_done", 0, mix=2)
        p_copied = tally("p_copied", 0, mix=1)
        pool_step = tally("pool_step", 0, mix=8)
        stat_done = tally("gn_stats", 0, mix=2)
        mv_done = tally("gn_moments", 0, mix=2)
        veps_done = tally("gn_veps", 0, mix=2)
        grs_done = tally("gn_rstd", 0, mix=2)
        cent_done = tally("gn_centred", 0, mix=2)
        retn_done = tally("gn_done", 0, mix=2)
        th_done = tally("tanh_swish", 0, mix=2)
        sw_done = tally("swish_done", 0, mix=2)
        ta_done = tally("tanh_a", 0, mix=2)
        ga_done = tally("gate_a_done", 0, mix=2)
        tb_done = tally("tanh_b", 0, mix=2)
        ma_done = tally("branch_a_done", 0, mix=2)
        mb_done = tally("branch_b_done", 1, mix=2)
        mg_done = tally("merged", 0, mix=2)
        mhi_done = tally("merged_hi", 0, mix=2)
        mlo_done = tally("merged_lo", 0, mix=2)

        conv_set = tally("conv_set", 0, ffn=1)
        mid_tap = tally("middle_tap", 0, ffn=4)
        side_tap = tally("side_taps", 0, ffn=8)
        gelu_done = tally("gelu_done", 0, ffn=2)
        prod_done = tally("prod_done", 0, ffn=2)
        ahi_done = tally("a_hi_done", 0, ffn=2)
        alo_done = tally("a_lo_done", 0, ffn=2)

        def slot_of(where, step):
            return place(where[0], step)[0]

        def filled(where, step):
            slot, turn = place(where[0], step)
            return full[slot].at(where, turn)

        def sq_view(ap, n):
            return ap.rearrange("p (a b) -> p a b", a=n)

        w_in_v = w_in.rearrange("(k p) n -> p k n", p=P)
        w_out_v = w_out.rearrange("(k p) n -> p k n", p=P)
        w_pool_v = w_pool.rearrange("g p n -> p g n")
        w_up_v = w_up.rearrange("(k p) n -> p k n", p=P)
        w_down_v = w_down.rearrange("(k p) n -> p k n", p=P)
        w_ada_v = w_ada.rearrange("(k p) n -> p k n", p=P)

        block = ctx.enter_context(nc.Block())

        @block.sync
        def _(sp):
            sp.dma_start(cst[:, :], consts).then_inc(const_in, 16)
            chunked = "(c p) -> c p"
            parts = [(0, R_BADA, b_ada.rearrange(chunked, p=P)), (0, R_GMIX, g_mix.rearrange(chunked, p=P)),
                     (0, R_GAIN, gn_gain.rearrange(chunked, p=P)), (0, R_PS, pool_scale.rearrange(chunked, p=P)),
                     (0, R_GFFN, g_ffn.rearrange(chunked, p=P)),
                     (0, R_C, c.rearrange("s (c p) -> (s c) p", p=P)),
                     (1, 0, conv_w[0:2, :].rearrange("t (c p) -> (t c) p", p=P)),
                     (2, 0, conv_w[2:3, :].rearrange("t (c p) -> (t c) p", p=P)),
                     (2, 2 * FC, conv_b.rearrange(chunked, p=P))]
            for i, r, src in parts:
                sp.dma_start(rows[r:r + src.shape[0], i, :], src).then_inc(rows_in, 16)
            for i, src in enumerate((decay_f, decay_b)):
                sp.dma_start(lg[:, i, :, :].rearrange("p a b -> p (a b)"), src.partition_broadcast(P)).then_inc(decay_in, 16)
            with sp.Fori(0, ADA_PARTS * ADA_GROUPS // 2) as it:
                for s in range(ADA_RING):
                    sp.wait_ge(ada_used, it * ADA_RING + (s + 1))
                    k = 2 * (s % 4)
                    src = w_ada_v[:, k:k + 2, bass.ds((it * 2 + s // 4) * HALF, HALF)]
                    sp.dma_start(ada[:, s, :, :], src).then_inc(ada_in[s], 16)

            def load(where, i, parts):
                sp.wait_ge(*lo_done.at(where, max(i - 1, 0)))
                for dst, src in parts:
                    sp.dma_start(dst, src).then_inc(raw_in[i % 2].sem, 16)

            def mix_block(where, i):
                region, _, pr = where
                if i < 4:
                    dst = sq_view(w_raw[:, i % 2, :], 2)
                    load(where, i, [(dst[:, :, a:a + n], w_in_v[:, 2 * i:2 * i + 2, bass.ds(col, n)])
                                    for a, n, col in ((0, P, pr * P + Q0), (P, P, pr * P + K0),
                                                      (2 * P, 2 * P, pr * 2 * P + V0))])
                elif i < 11:
                    col = {4: pr * P + P0, 5: pr * 2 * P + GS0, 6: pr * 2 * P + GA0, 7: pr * 2 * P + GB0,
                           8: pr * 2 * P + (GS0 + P), 9: pr * 2 * P + (GA0 + P), 10: pr * 2 * P + (GB0 + P)}[i]
                    load(where, i, [(sq_view(w_raw[:, i % 2, :], KC), w_in_v[:, :, bass.ds(col, P)])])
                else:
                    src = w_out_v[:, bass.ds(pr * 2, 2), (i - 11) * HALF:(i - 10) * HALF]
                    load(where, i, [(sq_view(w_raw[:, i % 2, :], 2), src)])

            def ffn_block(where, i):
                g = where[2]
                if i < 4:
                    dst = sq_view(w_raw[:, i % 2, :], KC)
                    src = w_up_v[:, :, bass.ds(g * 2 * P + ((i // 2) * P + (i % 2) * D_FF), P)]
                    cuts = (0, 3, 6, KC) if i < 2 else (0, KC)
                    load(where, i, [(dst[:, a:b, :], src[:, a:b, :]) for a, b in zip(cuts, cuts[1:])])
                else:
                    src = w_down_v[:, bass.ds(g * 2, 2), (i - 4) * HALF:(i - 3) * HALF]
                    load(where, i, [(sq_view(w_raw[:, i % 2, :], 2), src)])

            for seq in range(N_SEQ):
                with sp.Fori(0, PAIRS) as pr:
                    where = ("mix", seq, pr)
                    for i in range(N_MIX):
                        mix_block(where, i)
                        if i == 6:
                            sp.wait_ge(*mb_done.at(where, 0))
                            sp.dma_start(wpool[:, :].unsqueeze(1), w_pool_v[:, bass.ds(pr, 1), :]).then_inc(wpool_in.sem, 16)
                with sp.Fori(0, GROUPS) as g:
                    for i in range(N_FFN):
                        ffn_block(("ffn", seq, g), i)
            for i in range(2):
                mix_block(("last", 1, 0), i)

        @block.tensor
        def _(pe):
            def weights(where, i):
                pe.wait_ge(*hi_done.at(where, i + 1))
                pe.wait_ge(*lo_done.at(where, i + 1))
                return BLOCKS[where[0]][i][1]

            def three_passes(slot, w_slot, col, act_hi, act_lo, k, first, last):
                for n, (w, a) in enumerate(((w_hi, act_hi), (w_hi, act_lo), (w_lo, act_hi))):
                    for b in range(2):
                        ins = pe.matmul(ps[:, slot, b * HALF:(b + 1) * HALF], w[:, w_slot, col:col + P],
                                        a[:, k, b * HALF:(b + 1) * HALF],
                                        start=first and n == 0, stop=last and n == 2)
                return ins

            def one_pass(slot, w, act, k, last):
                for b in range(2):
                    ins = pe.matmul(ps[:, slot, b * HALF:(b + 1) * HALF], w, act[:, k, b * HALF:(b + 1) * HALF],
                                    start=False, stop=last)
                return ins

            def unit(where, i, step, norm=None):
                ws = weights(where, i)
                slot = slot_of(where, step)
                for k in range(KC):
                    if norm is not None:
                        pe.wait_ge(*hhi_done.at(norm, k + 1))
                        pe.wait_ge(*hlo_done.at(norm, k + 1))
                    ins = three_passes(slot, ws, k * P, h_hi[where[1]], h_lo[where[1]], k, k == 0, k == KC - 1)
                ins.then_inc(full[slot].sem, 1)

            def turn(where, step, source):
                slot = slot_of(where, step)
                for t in range(TT):
                    ins = pe.transpose(ps[:, slot, t * P:(t + 1) * P], source(t), ident)
                ins.then_inc(full[slot].sem, 1)

            def partial(where, block0, act_hi, act_lo, hi_t, lo_t, slot_read):
                for half in range(2):
                    ws = weights(where, block0 + half)
                    steps = [slot_of(where, f"W{4 * half + j}") for j in range(4)]
                    if half == 0:
                        pe.wait_ge(*hi_t.at(where, 1))
                        pe.wait_ge(*lo_t.at(where, 1))
                    for j, slot in enumerate(steps):
                        if half == 0:
                            pe.wait_ge(*slot_read[j])
                        else:
                            pe.wait_ge(*res_done.at(where, j + 1))
                        three_passes(slot, ws, j * P, act_hi, act_lo, 0, True, False)
                    if half == 0:
                        pe.wait_ge(*hi_t.at(where, 2))
                        for j, slot in enumerate(steps):
                            col = slice(HALF + j * P, HALF + (j + 1) * P)
                            one_pass(slot, w_hi[:, ws, col], act_hi, 1, False)
                            one_pass(slot, w_lo[:, ws, col], act_hi, 1, False)
                        pe.wait_ge(*lo_t.at(where, 2))
                        for j, slot in enumerate(steps):
                            col = slice(HALF + j * P, HALF + (j + 1) * P)
                            one_pass(slot, w_hi[:, ws, col], act_lo, 1, True).then_inc(full[slot].sem, 1)
                    else:
                        for j, slot in enumerate(steps):
                            three_passes(slot, ws, HALF + j * P, act_hi, act_lo, 1, False,
                                         True).then_inc(full[slot].sem, 1)

            def spread_rstd(where):
                slot = slot_of(where, "R")
                for b in range(2):
                    pe.wait_ge(*diag_done.at(where, b + 1))
                    ins = pe.matmul(ps[:, slot, b * HALF:(b + 1) * HALF], ones[:, :], diag[:, b * HALF:(b + 1) * HALF],
                                    start=True, stop=True)
                ins.then_inc(full[slot].sem, 1)

            def turn_x(where, t):
                pe.wait_ge(*x_in[t % 4].at(where, 16 * (t // 4 + 1)))
                turn(where, f"X{t}", lambda k: xin[:, t % 4, k * P:(k + 1) * P])

            def turn_y(where, t):
                turn(where, f"Y{t}", lambda k: xT[where[1]][:, k, t * P:(t + 1) * P])

            pe.sem_inc(ada_used, ADA_RING)
            pe.wait_ge(const_in, 16)
            pe.wait_ge(rows_in, 16 * 9)
            pe.wait_ge(ones_set, 3)
            for i, n in enumerate((R_ALL, 4 * FC, 4 * FC)):
                ins = pe.transpose(ps[:, 3, i * P:i * P + n], rows[0:n, i, :], cst[0:n, C_ID:C_ID + n])
            ins.then_inc(vec_turned, 1)
            first = ("first", 0, 0)
            for t in range(TT):
                if t == 3:
                    pe.wait_ge(vec_done, 2)
                if t >= 4:
                    pe.wait_ge(*xT_set[t % 2].at(first, (t - 4) // 2 + 1))
                turn_x(first, t)
            for e in range(2):
                pe.wait_ge(*xT_set[e].at(first, TT // 2))
            spread_rstd(first)

            ada_slot = (2, 3, 0)

            def ada_turn(part):
                pe.wait_ge(ada_rows_set, part + 1)
                for j in range(4):
                    ins = pe.transpose(ps[:, ada_slot[part], HALF + j * ADA_ROWS:HALF + (j + 1) * ADA_ROWS],
                                       ada_rows[:, part % 2, j * P:(j + 1) * P], cst[0:ADA_ROWS, C_ID:C_ID + ADA_ROWS])
                ins.then_inc(ada_turned, 1)

            pe.wait_ge(sil_done, 1)
            for part in range(ADA_PARTS):
                for g in range(ADA_GROUPS):
                    window = N_SEQ * (ADA_GROUPS - 1 - g)
                    for k in range(KC):
                        turn_no, s = divmod((part * ADA_GROUPS + g) * 4 + k // 2, ADA_RING)
                        if k % 2 == 0:
                            pe.wait_ge(ada_in[s], 16 * (turn_no + 1))
                        ins = pe.matmul(ps[0:ADA_ROWS, ada_slot[part], 0:HALF], silT[:, k, window:window + ADA_ROWS],
                                        ada[:, s, k % 2, :], start=g == 0 and k == 0,
                                        stop=g == ADA_GROUPS - 1 and k == KC - 1)
                        if k % 2:
                            ins.then_inc(ada_used, 1)
                        if part and g == 0 and k == 3:
                            ada_turn(part - 1)
            ada_turn(ADA_PARTS - 1)
            pe.wait_ge(mod_based, ADA_PARTS)

            for seq in range(N_SEQ):
                pre = ("swap", 0, 0) if seq else first
                if seq:
                    for step, ready in (("X0", res_done.at(pre, -3)), ("X1", res_done.at(pre, -2)),
                                        ("X2", res_done.at(pre, -1)), ("X3", res_done.at(pre, 0)),
                                        ("Y0", xT_set[0].at(pre, 1)), ("Y1", xT_set[1].at(pre, 1)),
                                        ("X4", xT_set[0].at(pre, 2)), ("X5", xT_set[1].at(pre, 2)),
                                        ("Y2", y_scaled.at(pre, 1)), ("Y3", y_scaled.at(pre, 2)),
                                        ("X6", xT_set[0].at(pre, 3)), ("X7", xT_set[1].at(pre, 3)),
                                        ("Y4", y_scaled.at(pre, 3)), ("Y5", y_scaled.at(pre, 4)),
                                        ("R", xT_set[0].at(pre, 4)), ("Y6", xT_set[1].at(pre, 4)),
                                        ("Y7", rrow_done.at(pre, 1))):
                        pe.wait_ge(*ready)
                        if step == "R":
                            spread_rstd(pre)
                        elif step[0] == "X":
                            turn_x(pre, int(step[1]))
                        else:
                            turn_y(pre, int(step[1]))
                    pe.wait_ge(*y_scaled.at(pre, TT))
                with pe.Fori(0, PAIRS) as pr:
                    where = ("mix", seq, pr)
                    for i in range(4):
                        ws = weights(where, i)
                        for k in (2 * i, 2 * i + 1):
                            pe.wait_ge(*hhi_done.at(pre, k + 1))
                            pe.wait_ge(*hlo_done.at(pre, k + 1))
                        for t in range(TT):
                            slot = slot_of(where, f"Q{t // 2}")
                            if i == 0 and t % 2 == 0:
                                pe.wait_ge(*res_done.at(where, t // 2 - 3))
                            for k in (2 * i, 2 * i + 1):
                                col = (k % 2) * HALF
                                for n, (a, w) in enumerate(((h_hi[seq], w_hi), (h_hi[seq], w_lo),
                                                         (h_lo[seq], w_hi))):
                                    ins = pe.matmul(ps[:, slot, (t % 2) * HALF:(t % 2 + 1) * HALF],
                                                    a[:, k, t * P:(t + 1) * P], w[:, ws, col:col + HALF],
                                                    start=k == 0 and n == 0, stop=k == KC - 1 and n == 2)
                            if i == 3 and t % 2:
                                ins.then_inc(full[slot].sem, 1)
                        if i < 3:
                            ins.then_inc(q_block.sem, 1)

                    def decayed(h):
                        pe.wait_ge(*qd_done.at(where, h + 1))
                        if h == 0:
                            pe.wait_ge(*p_copied.at(where, 1))
                        else:
                            pe.wait_ge(*state_step.at(where, 16))
                        turn(where, f"TD{h}", lambda t: tokb[:, t, :])
                        slot = slot_of(where, f"KV{h}")
                        if h == 0:
                            pe.wait_ge(*qT_done.at(where, 1))
                        else:
                            pe.wait_ge(*pt_done.at(where, 1))
                        pe.wait_ge(*kd_done.at(where, h + 1))
                        pe.wait_ge(*v_done.at(where, 4))
                        for t in range(TT):
                            ins = pe.matmul(ps[:, slot, t * P:(t + 1) * P], kdp[:, t, :], v_sb[:, t, h * P:(h + 1) * P],
                                            start=True, stop=True)
                        ins.then_inc(full[slot].sem, 1)
                        slot = slot_of(where, f"SC{h}")
                        if h:
                            pe.wait_ge(*ta_done.at(where, 1))
                        pe.wait_ge(*qT_done.at(where, 1))
                        pe.wait_ge(*kT_done.at(where, 1))
                        rows_h = slice(h * DK, (h + 1) * DK)
                        for t in range(TT):
                            ins = pe.matmul(ps[:, slot, t * P:(t + 1) * P], kT[rows_h, t * P:(t + 1) * P],
                                            qT[rows_h, t * P:(t + 1) * P], start=True, stop=True)
                        ins.then_inc(full[slot].sem, 1)

                    def outputs(h):
                        slot = slot_of(where, f"O{h}")
                        if h:
                            pe.wait_ge(*cent_done.at(where, 1))
                        pe.wait_ge(*pt_done.at(where, h + 1))
                        pe.wait_ge(*state_step.at(where, 16 * (h + 1)))
                        pe.wait_ge(*qdT_done.at(where, h + 1))
                        for t in range(TT):
                            o = ps[:, slot, t * P:(t + 1) * P]
                            pe.matmul(o, kdp[:, t, :], v_sb[:, t, h * P:(h + 1) * P], start=True, stop=False)
                            ins = pe.matmul(o, qdT[:, t * P:(t + 1) * P], state[:, t * P:(t + 1) * P], start=False, stop=True)
                        ins.then_inc(full[slot].sem, 1)

                    def branch_b(h):
                        slot = slot_of(where, f"BB{h}")
                        if h == 0:
                            pe.wait_ge(*state_step.at(where, 32))
                        else:
                            pe.wait_ge(*sw_done.at(where, 2))
                        pe.wait_ge(*pool_step.at(where, 8))
                        pe.wait_ge(*wpool_in.at(where, 16))
                        for b in range(2):
                            ins = pe.matmul(ps[:, slot, b * HALF:(b + 1) * HALF], wpool[:, h * P:(h + 1) * P],
                                            poolU[:, b * HALF:(b + 1) * HALF], start=True, stop=True)
                        ins.then_inc(full[slot].sem, 1)

                    def turn_ret(h):
                        pe.wait_ge(*retn_done.at(where, h + 1))
                        if h == 0:
                            pe.wait_ge(*pt_done.at(where, 2))
                        else:
                            pe.wait_ge(*mb_done.at(where, 1))
                        turn(where, f"TR{h}", lambda t: tokb[:, t, :])

                    pe.wait_ge(*v_done.at(where, 1))
                    unit(where, 4, "P")
                    pe.wait_ge(*v_done.at(where, 2))
                    unit(where, 5, "GS0")
                    pe.wait_ge(*rope_done.at(where, 4))
                    pe.wait_ge(*v_done.at(where, 4))
                    for i, step in enumerate(("TQ", "TK")):
                        turn(where, step, lambda t: rot[:, t, i * P:(i + 1) * P])
                    decayed(0)
                    pe.wait_ge(*sw_done.at(where, 1))
                    unit(where, 6, "GA0")
                    outputs(0)
                    decayed(1)
                    pe.wait_ge(*qdT_done.at(where, 2))
                    unit(where, 7, "GB0")
                    outputs(1)
                    branch_b(0)
                    turn_ret(0)
                    pe.wait_ge(*tb_done.at(where, 1))
                    unit(where, 8, "GS1")
                    pe.wait_ge(*cent_done.at(where, 2))
                    unit(where, 9, "GA1")
                    turn_ret(1)
                    pe.wait_ge(*ma_done.at(where, 1))
                    unit(where, 10, "GB1")
                    branch_b(1)
                    partial(where, 11, m_hi, m_lo, mhi_done, mlo_done,
                            [ta_done.at(where, 2), tb_done.at(where, 2), mb_done.at(where, 2), ma_done.at(where, 2)])
                mid = ("mid", seq, 0)
                slot = slot_of(mid, "ST")
                pe.wait_ge(*res_done.at(mid, -3))
                pe.matmul(ps[:, slot, 0:TT], ident, zeros[:, :], start=True, stop=False)
                for k in range(KC):
                    pe.wait_ge(*sq_done.at(mid, k + 1))
                    for t in range(TT):
                        ins = pe.matmul(ps[:, slot, t:t + 1], sq[:, k % 4, t * P:(t + 1) * P], ones[:, 0:1],
                                        start=False, stop=(k, t) == (KC - 1, TT - 1))
                    if k < KC - 1:
                        ins.then_inc(sq_used.sem, 1)
                ins.then_inc(full[slot].sem, 1)
                spread_rstd(mid)
                with pe.Fori(0, GROUPS) as g:
                    where = ("ffn", seq, g)
                    for i in range(4):
                        pe.wait_ge(*res_done.at(where, i - 3))
                        unit(where, i, f"U{i}", mid if i == 0 else None)
                    partial(where, 4, a_hi, a_lo, ahi_done, alo_done,
                            [side_tap.at(where, 2 * i + 2) for i in range(4)])
            last = ("last", 1, 0)
            pe.wait_ge(*res_done.at(last, 0))
            for t in range(TT):
                if t >= 4:
                    pe.wait_ge(*y_scaled.at(last, t - 3))
                turn_y(last, t)

        @block.scalar
        def _(act):
            def split(where, i):
                act.wait_ge(*raw_in[i % 2].at(where, brought(where[0], i)))
                act.activation(w_hi[:, BLOCKS[where[0]][i][1], :], w_raw[:, i % 2, :], ACT.Copy).then_inc(hi_done.sem, 1)

            def evac(where, step, dst, t):
                slot = slot_of(where, step)
                act.wait_ge(*filled(where, step))
                act.activation(dst, ps[:, slot, :], ACT.Copy).then_inc(t.sem, 1)

            def tanh_half(where, step, dst, t):
                slot = slot_of(where, step)
                act.wait_ge(*filled(where, step))
                act.activation(dst[:, :], ps[:, slot, :], ACT.Tanh, scale=0.5).then_inc(t.sem, 1)

            def square_x(where, t):
                act.wait_ge(*x_in[t % 4].at(where, 16 * (t // 4 + 1)))
                if t >= 2:
                    act.wait_ge(*x_squared.at(where, t - 1))
                act.activation(tn[:, t % 2, :], xin[:, t % 4, :], ACT.Square, scale=D ** -0.5,
                               accum_out=x_ms[:, t:t + 1]).then_inc(x_squared.sem, 1)

            def load_x(seq, t):
                act.dma_start(xin[:, t % 4, :], x[seq * S + t * P:seq * S + (t + 1) * P, :]).then_inc(x_in[t % 4].sem, 16)

            def reload_x(where, seq, t):
                act.wait_ge(*filled(where, f"X{t}"))
                act.wait_ge(*x_squared.at(where, t + 1))
                load_x(seq, t + 4)

            def copy_x(where, seq, t):
                slot = slot_of(where, f"X{t}")
                act.wait_ge(*filled(where, f"X{t}"))
                act.activation(xT[seq][:, :, t * P:(t + 1) * P], sq_view(ps[:, slot, :], KC),
                               ACT.Copy).then_inc(xT_set[1].sem, 1)

            def square_y(where, t):
                slot = slot_of(where, f"Y{t}")
                act.wait_ge(*filled(where, f"Y{t}"))
                if t >= 2:
                    act.wait_ge(*y_squared.at(where, t - 1))
                act.activation(hf[:, t % 2, :], ps[:, slot, :], ACT.Square, scale=D ** -0.5,
                               accum_out=y_ms[:, t:t + 1]).then_inc(y_squared.sem, 1)

            def store_y(where, t):
                act.wait_ge(*y_scaled.at(where, t + 1))
                act.dma_start(y[where[1] * S + t * P:where[1] * S + (t + 1) * P, :],
                              y_sb[:, t % Y_RING, :]).then_inc(y_out[t % Y_RING].sem, 16)

            def modulate(where, seq, shift, scale):
                for k in range(KC):
                    act.wait_ge(*tn_done.at(where, k + 1))
                    if k >= 2:
                        act.wait_ge(*hlo_done.at(where, k - 1))
                    a, b = modT[:, seq, scale + k:scale + k + 1], modT[:, seq, shift + k:shift + k + 1]
                    act.activation(hf[:, k % 2, :], tn[:, k % 2, :], ACT.Identity, bias=b, scale=a)
                    act.activation(h_hi[seq][:, k, :], tn[:, k % 2, :], ACT.Identity, bias=b, scale=a).then_inc(hhi_done.sem, 1)

            first = ("first", 0, 0)
            for t in range(4):
                load_x(0, t)
            for t in range(4):
                square_x(first, t)
                if t == 1:
                    act.wait_ge(vec_done, 1)
                    act.activation(small[:, 6, :], vecT[:, R_C:R_C + 2 * KC], ACT.Tanh, scale=0.5).then_inc(sil_tanh, 1)
            for t in range(TT):
                if t < 4:
                    reload_x(first, 0, t)
                if t % 2:
                    copy_x(first, 0, t)
                    if t >= 3:
                        for i in ((4, 5), (6,), (7,))[(t - 3) // 2]:
                            square_x(first, i)
            evac(first, "R", rrow[:, :], rrow_done)
            act.wait_ge(mod_ready, 1)
            modulate(first, 0, 0, 8)
            act.wait_ge(table_step, 1)
            act.activation(small[:, 1, :], small[:, 0, :], ACT.Exp, scale=-1.0).then_inc(table_act, 1)
            act.wait_ge(table_args, 1)
            act.activation(pairT[:, :, 0:T_GAIN], pairT[:, :, 0:T_GAIN], ACT.Exp).then_inc(table_act, 1)
            split(("mix", 0, 0), 0)
            split(("mix", 0, 0), 1)

            for seq in range(N_SEQ):
                if seq:
                    swap = ("swap", 0, 0)
                    for t in range(4):
                        square_x(swap, t)
                    reload_x(swap, 1, 0)
                    reload_x(swap, 1, 1)
                    copy_x(swap, 1, 1)
                    reload_x(swap, 1, 2)
                    reload_x(swap, 1, 3)
                    copy_x(swap, 1, 3)
                    square_y(swap, 0)
                    square_y(swap, 1)
                    square_x(swap, 4)
                    square_x(swap, 5)
                    copy_x(swap, 1, 5)
                    square_y(swap, 2)
                    square_y(swap, 3)
                    square_x(swap, 6)
                    square_x(swap, 7)
                    copy_x(swap, 1, 7)
                    store_y(swap, 0)
                    store_y(swap, 1)
                    square_y(swap, 4)
                    square_y(swap, 5)
                    store_y(swap, 2)
                    store_y(swap, 3)
                    evac(swap, "R", rrow[:, :], rrow_done)
                    square_y(swap, 6)
                    square_y(swap, 7)
                    for t in range(4, TT):
                        store_y(swap, t)
                    modulate(swap, 1, 0, 8)
                with act.Fori(0, PAIRS) as pr:
                    where = ("mix", seq, pr)
                    act.wait_ge(*full[0].at(where, 0))
                    split(where, 2)
                    act.wait_ge(*q_block.at(where, 1))
                    split(where, 3)
                    act.wait_ge(*q_block.at(where, 2))
                    split(where, 4)
                    act.wait_ge(*dec_arg.at(where, 4))
                    act.activation(dec[:, :, :], dec[:, :, :], ACT.Exp).then_inc(dec_done.sem, 1)
                    for i in range(4):
                        slot = slot_of(where, f"Q{i}")
                        act.wait_ge(*filled(where, f"Q{i}"))
                        act.wait_ge(*rope_mul.at(where, i + 1))
                        act.activation(v_sb[:, 2 * i:2 * i + 2, :], sq_view(ps[:, slot, :], 2)[:, :, 2 * P:4 * P],
                                       ACT.Copy).then_inc(v_done.sem, 1)
                        if i == 0:
                            act.wait_ge(*filled(where, "Q3"))
                            split(where, 5)
                    split(where, 6)
                    evac(where, "P", state[:, PAD:PAD + S], p_copied)
                    act.wait_ge(*rope_done.at(where, 4))
                    tanh_half(where, "GS0", bufA, th_done)
                    act.wait_ge(*filled(where, "P"))
                    split(where, 7)
                    evac(where, "TQ", qT[:, :], qT_done)
                    evac(where, "TK", kT[:, :], kT_done)
                    evac(where, "TD0", qdT[:, :], qdT_done)
                    act.wait_ge(*filled(where, "GS0"))
                    split(where, 8)
                    tanh_half(where, "GA0", bufB, ta_done)
                    evac(where, "TD1", qdT[:, :], qdT_done)
                    act.wait_ge(*filled(where, "GA0"))
                    split(where, 9)
                    act.wait_ge(*ga_done.at(where, 1))
                    tanh_half(where, "GB0", bufB, tb_done)
                    act.wait_ge(*filled(where, "GB0"))
                    split(where, 10)
                    act.wait_ge(*mg_done.at(where, 1))
                    act.activation(m_hi[:, 0, :], bufA[:, :], ACT.Copy).then_inc(mhi_done.sem, 1)
                    act.wait_ge(*mlo_done.at(where, 1))
                    tanh_half(where, "GS1", bufA, th_done)
                    act.wait_ge(*filled(where, "GS1"))
                    split(where, 11)
                    tanh_half(where, "GA1", bufB, ta_done)
                    act.wait_ge(*ga_done.at(where, 2))
                    tanh_half(where, "GB1", bufB, tb_done)
                    act.wait_ge(*filled(where, "GA1"))
                    split(where, 12)
                    act.wait_ge(*mg_done.at(where, 2))
                    act.activation(m_hi[:, 1, :], bufA[:, :], ACT.Copy).then_inc(mhi_done.sem, 1)
                    act.wait_ge(*filled(where, "GB1"))
                    act.wait_ge(*filled(where, "W3"))
                    split(("mix", seq, pr + 1), 0)
                    split(("mix", seq, pr + 1), 1)
                mid = ("mid", seq, 0)
                for k in range(KC):
                    act.wait_ge(*res_done.at(mid, k - 7))
                    if k >= 4:
                        act.wait_ge(*sq_used.at(mid, k - 3))
                    act.activation(sq[:, k % 4, :], xT[seq][:, k, :], ACT.Square, scale=D ** -0.5).then_inc(sq_done.sem, 1)
                act.dma_start(g_row[:, :], g_final.partition_broadcast(P)).then_inc(g_row_in.sem, 16)
                modulate(mid, seq, 24, 32)
                if seq == 0:
                    for t in range(4):
                        load_x(1, t)
                with act.Fori(0, GROUPS) as g:
                    where = ("ffn", seq, g)

                    def middle_tap(i, dst):
                        slot = slot_of(where, f"U{i}")
                        act.wait_ge(*filled(where, f"U{i}"))
                        col = convS[:, i % 2, i // 2, :]
                        act.activation(dst[:, :], ps[:, slot, :], ACT.Identity, bias=col[:, 3:4],
                                       scale=col[:, 1:2]).then_inc(mid_tap.sem, 1)

                    def gelu(j):
                        act.wait_ge(*side_tap.at(where, 4 * j + 2))
                        act.activation(ca[:, :], ca[:, :], ACT.Gelu_apprx_tanh).then_inc(gelu_done.sem, 1)

                    act.wait_ge(*conv_set.at(where, 1))
                    middle_tap(0, ca)
                    split(where, 2)
                    gelu(0)
                    middle_tap(1, cl)
                    act.wait_ge(*filled(where, "U0"))
                    split(where, 3)
                    act.wait_ge(*prod_done.at(where, 1))
                    middle_tap(2, ca)
                    act.wait_ge(*filled(where, "U1"))
                    split(where, 4)
                    gelu(1)
                    act.wait_ge(*alo_done.at(where, 1))
                    middle_tap(3, cl)
                    act.wait_ge(*filled(where, "U2"))
                    split(where, 5)
                    act.wait_ge(*filled(where, "U3"))
                    split(("ffn", seq, g + 1), 0)
                    act.wait_ge(*filled(where, "W3"))
                    split(("ffn", seq, g + 1), 1)
            last = ("last", 1, 0)
            for t in range(TT):
                square_y(last, t)
                if t >= 3:
                    store_y(last, t - 3)
            for t in range(TT - 3, TT):
                store_y(last, t)
            for t in range(Y_RING):
                act.wait_ge(*y_out[t].at(last, 16 * len(range(t, TT, Y_RING))))

        @block.gpsimd
        def _(pool):
            def remainder(where, i):
                ws = BLOCKS[where[0]][i][1]
                pool.wait_ge(*hi_done.at(where, i + 1))
                pool.tensor_tensor(w_lo[:, ws, :], w_raw[:, i % 2, :], w_hi[:, ws, :].bitcast(F32),
                                   ALU.subtract).then_inc(lo_done.sem, 1)

            def inverse_root(dst, src):
                return pool.tensor_tensor(dst, src, mhalf[:, 0:src.shape[1]], ALU.pow)

            def rstd_of_x(where):
                pool.wait_ge(*x_squared.at(where, TT))
                pool.tensor_scalar(x_ms[:, :], x_ms[:, :], EPS, None, ALU.add).then_inc(x_eps.sem, 1)
                pool.wait_ge(*x_eps.at(where, 1))
                inverse_root(rstd[:, :], x_ms[:, :]).then_inc(rstd_done.sem, 1)

            def rstd_of_y(where, i):
                pool.wait_ge(*y_squared.at(where, 2 * i + 2))
                pair = slice(2 * i, 2 * i + 2)
                pool.tensor_scalar(y_ms[:, pair], y_ms[:, pair], EPS, None, ALU.add).then_inc(y_eps.sem, 1)
                pool.wait_ge(*y_eps.at(where, i + 1))
                inverse_root(y_rstd[:, pair], y_ms[:, pair]).then_inc(y_rstd_done.sem, 1)

            pool.sem_inc(lo_done.sem, 1)
            pool.wait_ge(ones_set, 2)
            rstd_of_x(("first", 0, 0))
            remainder(("mix", 0, 0), 0)
            remainder(("mix", 0, 0), 1)
            for seq in range(N_SEQ):
                if seq:
                    swap = ("swap", 0, 0)
                    rstd_of_y(swap, 0)
                    rstd_of_y(swap, 1)
                    rstd_of_x(swap)
                    rstd_of_y(swap, 2)
                    rstd_of_y(swap, 3)
                with pool.Fori(0, PAIRS) as pr:
                    where = ("mix", seq, pr)
                    for i in range(2, N_MIX):
                        remainder(where, i)
                        if i in (9, 10):
                            h = i - 9
                            pool.wait_ge(*veps_done.at(where, h + 1))
                            inverse_root(grs[:, :], veps[:, :]).then_inc(grs_done.sem, 1)
                    remainder(("mix", seq, pr + 1), 0)
                    remainder(("mix", seq, pr + 1), 1)
                mid = ("mid", seq, 0)
                pool.wait_ge(*msq_done.at(mid, 1))
                inverse_root(rstd[:, :], msq[:, :]).then_inc(rstd_done.sem, 1)
                with pool.Fori(0, GROUPS) as g:
                    for i in range(2, N_FFN):
                        remainder(("ffn", seq, g), i)
                    remainder(("ffn", seq, g + 1), 0)
                    remainder(("ffn", seq, g + 1), 1)
            for i in range(TT // 2):
                rstd_of_y(("last", 1, 0), i)

        @block.vector
        def _(dve):
            steps = [0]

            def step(ins):
                ins.then_inc(table_step, 1)
                steps[0] += 1
                dve.wait_ge(table_step, steps[0])

            def copy_x(where, seq, t):
                slot = slot_of(where, f"X{t}")
                dve.wait_ge(*filled(where, f"X{t}"))
                dve.tensor_copy(xT[seq][:, :, t * P:(t + 1) * P], sq_view(ps[:, slot, :], KC)).then_inc(xT_set[0].sem, 1)

            def scale_y(where, t):
                slot = slot_of(where, f"Y{t}")
                dve.wait_ge(*y_rstd_done.at(where, t // 2 + 1))
                if t >= Y_RING:
                    dve.wait_ge(*y_out[t % Y_RING].at(where, 16))
                dve.scalar_tensor_tensor(y_sb[:, t % Y_RING, :], ps[:, slot, :], y_rstd[:, t:t + 1], g_row[:, :],
                                         ALU.mult, ALU.mult).then_inc(y_scaled.sem, 1)

            def diagonal(where):
                dve.wait_ge(*rstd_done.at(where, 1))
                for b in range(2):
                    dve.tensor_tensor(sq_view(diag[:, b * HALF:(b + 1) * HALF], 4), ident.unsqueeze(1).to_broadcast([P, 4, P]),
                                      rstd[:, 4 * b:4 * b + 4].unsqueeze(2).to_broadcast([P, 4, P]),
                                      ALU.mult).then_inc(diag_done.sem, 1)

            def norm_apply(where, seq, factor):
                for k in range(KC + 1):
                    if k < KC:
                        if k >= 2:
                            dve.wait_ge(*hhi_done.at(where, k - 1))
                        dve.tensor_tensor(tn[:, k % 2, :], xT[seq][:, k, :], factor, ALU.mult).then_inc(tn_done.sem, 1)
                    if k:
                        dve.wait_ge(*hhi_done.at(where, k))
                        dve.tensor_tensor(h_lo[seq][:, k - 1, :], hf[:, (k - 1) % 2, :],
                                          h_hi[seq][:, k - 1, :].bitcast(F32), ALU.subtract).then_inc(hlo_done.sem, 1)

            def update_residual(where, gate):
                seq = where[1]
                for d in range(KC):
                    slot = slot_of(where, f"W{d}")
                    dve.wait_ge(*filled(where, f"W{d}"))
                    dve.scalar_tensor_tensor(xT[seq][:, d, :], ps[:, slot, :], modT[:, seq, gate + d:gate + d + 1],
                                             xT[seq][:, d, :], ALU.mult, ALU.add).then_inc(res_done.sem, 1)

            dve.sem_inc(res_done.sem, 4)
            dve.sem_inc(mb_done.sem, 1)
            dve.memset(silT[:, :, :], 0.0).then_inc(sil_step, 1)
            dve.memset(ones[:, :], 1.0).then_inc(ones_set, 1)
            dve.memset(mhalf[:, :], -0.5).then_inc(ones_set, 1)
            dve.memset(zeros[:, :], 0.0).then_inc(ones_set, 1)
            dve.wait_ge(vec_turned, 1)
            dve.tensor_copy(vecT[:, :], ps[:, 3, 0:R_ALL]).then_inc(vec_done, 1)
            for i in range(2):
                ins = dve.tensor_copy(convT[:, :, 2 * i:2 * i + 2],
                                      ps[:, 3, (i + 1) * P:(i + 1) * P + 4 * FC].rearrange("p (t j) -> p j t", t=2))
            ins.then_inc(vec_done, 1)
            dve.wait_ge(sil_tanh, 1)
            dve.scalar_tensor_tensor(small[:, 6, :], small[:, 6, :], 1.0, vecT[:, R_C:R_C + 2 * KC], ALU.add,
                                     ALU.mult).then_inc(sil_step, 1)
            dve.wait_ge(sil_step, 2)
            mid_col = ADA_ROWS - N_SEQ
            dve.tensor_scalar(silT[:, :, mid_col:mid_col + N_SEQ], small[:, 6, :].rearrange("p (s k) -> p k s", s=N_SEQ),
                              0.5, None, ALU.mult).then_inc(sil_done, 1)
            first = ("first", 0, 0)
            for t in range(0, TT, 2):
                copy_x(first, 0, t)
            diagonal(first)

            def copy_ada(part):
                dve.wait_ge(ada_used, ADA_RING + 4 * ADA_GROUPS * (part + 1))
                if part == 2:
                    dve.wait_ge(ada_turned, 1)
                dve.tensor_copy(ada_rows[:, part % 2, :], ps[0:ADA_ROWS, (2, 3, 0)[part], 0:HALF]).then_inc(ada_rows_set, 1)

            def add_bias(part):
                dve.wait_ge(ada_turned, part + 1)
                a, b = 16 * part, 16 * (part + 1)
                turned = ps[:, (2, 3, 0)[part], HALF:HALF + 4 * ADA_ROWS].rearrange("p (j g s) -> p g j s", g=ADA_GROUPS, s=N_SEQ)
                for s in range(N_SEQ):
                    ins = dve.tensor_tensor(modT[:, s, a:b].rearrange("p (g j) -> p g j", j=4), turned[:, :, :, s],
                                            vecT[:, R_BADA + a:R_BADA + b].rearrange("p (g j) -> p g j", j=4), ALU.add)
                ins.then_inc(mod_based, 1)

            def take_gain(scale, row):
                dve.scalar_tensor_tensor(modT[:, :, scale:scale + 8], modT[:, :, scale:scale + 8], 1.0,
                                         vecT[:, row:row + 8].unsqueeze(1).to_broadcast([P, 2, 8]), ALU.add,
                                         ALU.mult).then_inc(mod_ready, 1)

            copy_ada(0)
            add_bias(0)
            dve.wait_ge(mod_based, 1)
            take_gain(8, R_GMIX)
            dve.wait_ge(*rrow_done.at(first, 1))
            norm_apply(first, 0, rrow[:, :])
            dve.wait_ge(decay_in, 32)
            logit = lg[:, :, :, :].rearrange("p a b c -> p (a b c)")
            step(dve.scalar_tensor_tensor(small[:, 0, :], logit, -1.0, logit, ALU.mult, ALU.max))
            dve.wait_ge(table_act, 1)
            step(dve.tensor_scalar(small[:, 2, :], small[:, 1, :], 2.0, None, ALU.add))
            step(dve.reciprocal(small[:, 2, :], small[:, 2, :]))
            step(dve.tensor_tensor(small[:, 3, :], small[:, 1, :], small[:, 2, :], ALU.mult))
            step(dve.tensor_tensor(small[:, 4, :], small[:, 3, :], small[:, 3, :], ALU.mult))
            step(dve.tensor_scalar(small[:, 5, :], small[:, 4, :], 1.0 / 17, None, ALU.mult))
            for k in range(7, 0, -1):
                step(dve.scalar_tensor_tensor(small[:, 5, :], small[:, 5, :], 1.0 / (2 * k + 1), small[:, 4, :],
                                              ALU.add, ALU.mult))
            step(dve.scalar_tensor_tensor(small[:, 5, :], small[:, 5, :], 1.0, small[:, 3, :], ALU.add, ALU.mult))
            step(dve.tensor_scalar(small[:, 0, :], logit, 0.0, None, ALU.min))
            step(dve.scalar_tensor_tensor(logit, small[:, 5, :], -2.0, small[:, 0, :], ALU.mult, ALU.add))
            dve.wait_ge(const_in, 16)
            for i, col in enumerate((T_DQ, T_DK)):
                for d in range(2):
                    pos = cst[:, C_POS + 2 * i + d:C_POS + 2 * i + d + 1]
                    dve.tensor_scalar(pairT[:, :, col + d:col + 4:2], lg[:, d, :, :], pos, None, ALU.mult)
            for d in range(2):
                half = slice(d * DK, (d + 1) * DK)
                dve.tensor_scalar(pairT[half, :, T_DC:T_DC + 2], lg[half, d, :, :], float(P), None, ALU.mult)
            for d, col in enumerate((T_LGF, T_LGB)):
                ins = dve.tensor_copy(pairT[:, :, col:col + 2], lg[:, d, :, :])
            ins.then_inc(table_args, 1)
            dve.wait_ge(table_act, 2)
            dve.tensor_scalar(pairT[:, :, T_DK:T_DK + 4], pairT[:, :, T_DK:T_DK + 4], K_SCALE, None, ALU.mult)
            for col, row, factor in ((T_GAIN, R_GAIN, 0.25), (T_PS, R_PS, 0.5)):
                step(dve.tensor_scalar(pairT[:, :, col:col + 2], vecT[:, row:row + 8].rearrange("p (a b) -> p a b", b=2),
                                       factor, None, ALU.mult))
            for part in (1, 2):
                copy_ada(part)
                add_bias(part)
            dve.wait_ge(mod_based, 3)
            take_gain(32, R_GFFN)
            dve.wait_ge(mod_ready, 2)

            for seq in range(N_SEQ):
                if seq:
                    swap = ("swap", 0, 0)
                    copy_x(swap, 1, 0)
                    copy_x(swap, 1, 2)
                    dve.wait_ge(*g_row_in.at(swap, 0))
                    scale_y(swap, 0)
                    scale_y(swap, 1)
                    copy_x(swap, 1, 4)
                    scale_y(swap, 2)
                    scale_y(swap, 3)
                    copy_x(swap, 1, 6)
                    diagonal(swap)
                    for t in range(4, TT):
                        scale_y(swap, t)
                    dve.wait_ge(*rrow_done.at(swap, 1))
                    norm_apply(swap, 1, rrow[:, :])
                    for t in range(Y_RING):
                        dve.wait_ge(*y_out[t].at(swap, 16 * len(range(t, TT, Y_RING))))
                with dve.Fori(0, PAIRS) as pr:
                    where = ("mix", seq, pr)

                    def scal(col):
                        return pairS[:, col:col + 1]

                    start_at = dve.snap(PAD - (pr * pr * pr + 5 * pr + 6) // 6)

                    dve.tensor_copy(pairS[:, 0:T_BUILT], pairT[:, bass.ds(pr, 1), :].rearrange("p a b -> p (a b)"))
                    dve.tensor_copy(pairS[:, T_BUILT:T_ALL],
                                    cst[:, bass.ds(pr * POOL_COLS + C_POOL, POOL_COLS)]).then_inc(pair_set.sem, 1)
                    dve.wait_ge(*pair_set.at(where, 1))
                    for h in range(2):
                        dve.tensor_scalar(dec[:, h, :], cst[:, C_DIFP:C_DIFP + P], scal(T_LGF + h), None,
                                          ALU.mult).then_inc(dec_arg.sem, 1)
                    for h in range(2):
                        dve.wait_ge(*dec_arg.at(where, h + 1))
                        dve.scalar_tensor_tensor(dec[:, h, :], cst[:, C_DIFN:C_DIFN + P], scal(T_LGB + h), dec[:, h, :],
                                                 ALU.mult, ALU.add).then_inc(dec_arg.sem, 1)

                    def rope_products(i):
                        slot = slot_of(where, f"Q{i}")
                        dve.wait_ge(*filled(where, f"Q{i}"))
                        qk = sq_view(ps[:, slot, :], 2)[:, :, 0:2 * P].rearrange("p t (v e) -> p t v e", e=32)
                        if i >= 2:
                            dve.wait_ge(*rope_done.at(where, i - 1))
                        for buf, col in ((bufA, C_COS), (bufB, C_SIN)):
                            table = cst[:, col + 64 * i:col + 64 * i + 64].rearrange("p (t e) -> p t e", t=2)
                            ins = dve.tensor_tensor(
                                buf[:, (i % 2) * HALF:(i % 2 + 1) * HALF].rearrange("p (t v e) -> p t v e", t=2, e=32),
                                qk, table.unsqueeze(2).to_broadcast([P, 2, 8, 32]), ALU.mult)
                        ins.then_inc(rope_mul.sem, 1)

                    def rope_sums(i):
                        dve.wait_ge(*rope_mul.at(where, i + 1))
                        a, b = (buf[:, (i % 2) * HALF:(i % 2 + 1) * HALF].rearrange("p (v s e) -> p v s e", s=2, e=32)
                                for buf in (bufA, bufB))
                        out = rot[:, 2 * i:2 * i + 2, :].rearrange("p t (v s e) -> p (t v) s e", s=2, e=32)
                        dve.tensor_tensor(out[:, :, 0, :], a[:, :, 0, :], b[:, :, 1, :], ALU.subtract)
                        dve.tensor_tensor(out[:, :, 1, :], a[:, :, 1, :], b[:, :, 0, :], ALU.add).then_inc(rope_done.sem, 1)

                    for i in range(5):
                        if i < 4:
                            rope_products(i)
                        if i:
                            rope_sums(i - 1)

                    def decayed(h, first_col, src, dst, t):
                        for d in range(2):
                            ins = dve.tensor_scalar(dst[:, :, d * DK:(d + 1) * DK], rot[:, :, src + h * DK:src + (h + 1) * DK],
                                                    scal(first_col + 2 * h + d), None, ALU.mult)
                        ins.then_inc(t.sem, 1)

                    f, b = slice(0, DK), slice(DK, P)

                    def first_states(h):
                        dve.memset(state[f, 0:P], 0.0).then_inc(state_step.sem, 1)
                        dve.memset(state[b, (TT - 1) * P:TT * P], 0.0).then_inc(state_step.sem, 1)

                    def states(h):
                        dc = T_DC + h
                        slot = slot_of(where, f"KV{h}")
                        dve.wait_ge(*filled(where, f"KV{h}"))
                        for n in range(1, TT):
                            for rows_d, last, new, back in ((f, n - 1, n, 2), (b, TT - n, TT - 1 - n, 2)):
                                at = 16 * h + 2 * n + (1 if rows_d is b else 0)
                                dve.wait_ge(*state_step.at(where, at + 1 - back))
                                dve.scalar_tensor_tensor(
                                    state[rows_d, new * P:(new + 1) * P], state[rows_d, last * P:(last + 1) * P],
                                    pairS[rows_d, dc:dc + 1], ps[rows_d, slot, last * P:(last + 1) * P],
                                    ALU.mult, ALU.add).then_inc(state_step.sem, 1)

                    def scores(h):
                        slot = slot_of(where, f"SC{h}")
                        dve.wait_ge(*filled(where, f"SC{h}"))
                        if h == 0:
                            dve.wait_ge(*dec_done.at(where, 1))
                        dve.scalar_tensor_tensor(kdp[:, :, :], sq_view(ps[:, slot, :], TT), K_SCALE,
                                                 dec[:, h, :].unsqueeze(1).to_broadcast([P, TT, P]),
                                                 ALU.mult, ALU.mult).then_inc(pt_done.sem, 1)

                    def statistics(h):
                        slot = slot_of(where, f"O{h}")
                        dve.wait_ge(*filled(where, f"O{h}"))
                        for t in range(TT):
                            ins = dve.bn_stats(bst[:, t, :], ps[:, slot, t * P:(t + 1) * P])
                        ins.then_inc(stat_done.sem, 1)

                    def aggregate(h):
                        for t in range(TT):
                            ins = dve.bn_aggr(mv[:, t, :], bst[:, t, :])
                        ins.then_inc(mv_done.sem, 1)
                        dve.wait_ge(*mv_done.at(where, h + 1))
                        dve.tensor_scalar(veps[:, :], mv[:, :, 1], EPS, None, ALU.add).then_inc(veps_done.sem, 1)

                    def centred(h, turned):
                        dve.wait_ge(*filled(where, turned))
                        slot = place("mix", f"O{h}")[0]
                        dve.tensor_tensor(tokb[:, :, :], sq_view(ps[:, slot, :], TT),
                                          mv[:, :, 0:1].to_broadcast([P, TT, P]), ALU.subtract).then_inc(cent_done.sem, 1)

                    def normed(h):
                        dve.wait_ge(*grs_done.at(where, h + 1))
                        dve.wait_ge(*cent_done.at(where, h + 1))
                        dve.tensor_tensor(tokb[:, :, :], tokb[:, :, :], grs[:, :].unsqueeze(2).to_broadcast([P, TT, P]),
                                          ALU.mult).then_inc(retn_done.sem, 1)

                    def swish(h):
                        slot = slot_of(where, f"GS{h}")
                        dve.wait_ge(*filled(where, f"GS{h}"))
                        dve.wait_ge(*th_done.at(where, h + 1))
                        dve.scalar_tensor_tensor(bufA[:, :], bufA[:, :], 1.0, ps[:, slot, :], ALU.add,
                                                 ALU.mult).then_inc(sw_done.sem, 1)

                    def gate_a(h):
                        dve.wait_ge(*ta_done.at(where, h + 1))
                        dve.wait_ge(*sw_done.at(where, h + 1))
                        dve.scalar_tensor_tensor(bufA[:, :], bufB[:, :], 1.0, bufA[:, :], ALU.add,
                                                 ALU.mult).then_inc(ga_done.sem, 1)

                    def branch_a(h):
                        slot = slot_of(where, f"TR{h}")
                        dve.wait_ge(*filled(where, f"TR{h}"))
                        dve.wait_ge(*ga_done.at(where, h + 1))
                        dve.scalar_tensor_tensor(bufA[:, :], ps[:, slot, :], scal(T_GAIN + h), bufA[:, :], ALU.mult,
                                                 ALU.mult).then_inc(ma_done.sem, 1)

                    def branch_b(h):
                        slot = slot_of(where, f"BB{h}")
                        dve.wait_ge(*filled(where, f"BB{h}"))
                        dve.wait_ge(*tb_done.at(where, h + 1))
                        dve.scalar_tensor_tensor(bufB[:, :], bufB[:, :], 1.0, ps[:, slot, :], ALU.add,
                                                 ALU.mult).then_inc(mb_done.sem, 1)

                    def merge(h):
                        dve.wait_ge(*ma_done.at(where, h + 1))
                        dve.wait_ge(*mb_done.at(where, h + 1))
                        dve.scalar_tensor_tensor(bufA[:, :], bufB[:, :], scal(T_PS + h), bufA[:, :], ALU.mult,
                                                 ALU.add).then_inc(mg_done.sem, 1)

                    def merge_low(h):
                        dve.wait_ge(*mhi_done.at(where, h + 1))
                        dve.tensor_tensor(m_lo[:, h, :], bufA[:, :], m_hi[:, h, :].bitcast(F32),
                                          ALU.subtract).then_inc(mlo_done.sem, 1)

                    dve.wait_ge(*rope_done.at(where, 4))
                    decayed(0, T_DQ, 0, tokb, qd_done)
                    decayed(0, T_DK, P, kdp, kd_done)

                    for at in (0, PAD + S):
                        dve.memset(state[:, at:at + PAD], 0.0).then_inc(pool_step.sem, 1)
                    dve.wait_ge(*p_copied.at(where, 1))
                    src, length = state, S + 2 * PAD
                    for level in range(4):
                        dve.wait_ge(*pool_step.at(where, 2 + level))
                        length -= 1 << level
                        dve.scalar_tensor_tensor(poolU[:, 0:length], src[:, 1 << level:(1 << level) + length],
                                                 scal(T_POOL + level), src[:, 0:length], ALU.mult,
                                                 ALU.add).then_inc(pool_step.sem, 1)
                        src = poolU
                    dve.wait_ge(*pool_step.at(where, 6))
                    for n, at in ((0, 0), (1, S - PAD)):
                        edge = poolU[:, bass.ds(start_at + at, PAD)]
                        ins = dve.tensor_tensor(edge, edge, pairS[:, T_POOL + 5 + 8 * n:T_POOL + 13 + 8 * n], ALU.mult)
                    ins.then_inc(pool_step.sem, 1)
                    dve.wait_ge(*pool_step.at(where, 7))
                    dve.scalar_tensor_tensor(poolU[:, 0:S], poolU[:, bass.ds(start_at, S)], scal(T_POOL + 4),
                                             state[:, PAD:PAD + S], ALU.mult, ALU.subtract).then_inc(pool_step.sem, 1)
                    swish(0)
                    dve.wait_ge(*pool_step.at(where, 8))
                    first_states(0)
                    states(0)
                    dve.wait_ge(*filled(where, "TD0"))
                    decayed(1, T_DQ, 0, tokb, qd_done)
                    scores(0)
                    gate_a(0)
                    dve.wait_ge(*filled(where, "O0"))
                    decayed(1, T_DK, P, kdp, kd_done)
                    statistics(0)
                    dve.wait_ge(*stat_done.at(where, 1))
                    first_states(1)
                    aggregate(0)
                    centred(0, "TD1")
                    states(1)
                    scores(1)
                    normed(0)
                    statistics(1)
                    dve.wait_ge(*stat_done.at(where, 2))
                    branch_b(0)
                    aggregate(1)
                    branch_a(0)
                    merge(0)
                    merge_low(0)
                    centred(1, "TR0")
                    normed(1)
                    swish(1)
                    gate_a(1)
                    branch_a(1)
                    branch_b(1)
                    merge(1)
                    merge_low(1)
                    update_residual(where, 16)
                mid = ("mid", seq, 0)
                dve.wait_ge(*filled(mid, "ST"))
                dve.tensor_scalar(msq[:, :], ps[:, slot_of(mid, "ST"), 0:TT], EPS, None, ALU.add).then_inc(msq_done.sem, 1)
                diagonal(mid)
                dve.wait_ge(*filled(mid, "R"))
                norm_apply(mid, seq, ps[:, slot_of(mid, "R"), :])
                with dve.Fori(0, GROUPS) as g:
                    where = ("ffn", seq, g)
                    dve.tensor_copy(convS[:, :, :, :], convT[:, :, :].rearrange("p (l c) t -> p l c t", l=2)[:, :, bass.ds(g * 2, 2), :]).then_inc(conv_set.sem, 1)

                    def side_taps(i, dst):
                        slot = place("ffn", f"U{i}")[0]
                        dve.wait_ge(*mid_tap.at(where, i + 1))
                        col = convS[:, i % 2, i // 2, :]
                        dve.scalar_tensor_tensor(dst[:, 1:S], ps[:, slot, 0:S - 1], col[:, 0:1], dst[:, 1:S],
                                                 ALU.mult, ALU.add).then_inc(side_tap.sem, 1)
                        dve.wait_ge(*side_tap.at(where, 2 * i + 1))
                        dve.scalar_tensor_tensor(dst[:, 0:S - 1], ps[:, slot, 1:S], col[:, 2:3], dst[:, 0:S - 1],
                                                 ALU.mult, ALU.add).then_inc(side_tap.sem, 1)

                    dve.wait_ge(*conv_set.at(where, 1))
                    for j in range(2):
                        side_taps(2 * j, ca)
                        side_taps(2 * j + 1, cl)
                        dve.wait_ge(*gelu_done.at(where, j + 1))
                        dve.wait_ge(*side_tap.at(where, 4 * j + 4))
                        dve.tensor_tensor(a_hi[:, j, :], cl[:, :], ca[:, :], ALU.mult).then_inc(ahi_done.sem, 1)
                        dve.tensor_tensor(cl[:, :], cl[:, :], ca[:, :], ALU.mult).then_inc(prod_done.sem, 1)
                        dve.wait_ge(*ahi_done.at(where, j + 1))
                        dve.wait_ge(*prod_done.at(where, j + 1))
                        dve.tensor_tensor(a_lo[:, j, :], cl[:, :], a_hi[:, j, :].bitcast(F32),
                                          ALU.subtract).then_inc(alo_done.sem, 1)
                    update_residual(where, 40)
            last = ("last", 1, 0)
            dve.wait_ge(*g_row_in.at(last, 0))
            for t in range(TT):
                scale_y(last, t)


def kernel(x_prompt, x_sample, c_prompt, c_sample, w_ada, b_ada, g_mix, w_in, ret_decay_f, ret_decay_b,
           ret_gn_gain, w_pool_grp, pool_scale, w_out, g_ffn, w_up, conv_w, conv_b, w_down, g_final):
    import concourse.bacc as bacc
    from concourse.bass_utils import run_bass_kernel_spmd

    arrays = {
        "x": np.concatenate([np.asarray(x_prompt), np.asarray(x_sample)], 0).reshape(N_SEQ * S, D),
        "c": np.concatenate([np.asarray(c_prompt), np.asarray(c_sample)], 0),
        "w_ada": np.asarray(w_ada)[0], "b_ada": np.asarray(b_ada)[0], "g_mix": np.asarray(g_mix)[0],
        "w_in": np.asarray(w_in)[0], "decay_f": np.asarray(ret_decay_f)[0], "decay_b": np.asarray(ret_decay_b)[0],
        "gn_gain": np.asarray(ret_gn_gain)[0], "w_pool": np.asarray(w_pool_grp)[0],
        "pool_scale": np.asarray(pool_scale)[0], "w_out": np.asarray(w_out)[0], "g_ffn": np.asarray(g_ffn)[0],
        "w_up": np.asarray(w_up)[0], "conv_w": np.asarray(conv_w)[0], "conv_b": np.asarray(conv_b)[0],
        "w_down": np.asarray(w_down)[0], "g_final": np.asarray(g_final), "consts": constants(),
    }
    arrays = {n: np.ascontiguousarray(a) for n, a in arrays.items()}
    nc = bacc.Bacc("TRN2", target_bir_lowering=False, num_devices=1)
    args = [nc.dram_tensor(f"in_{n}", a.shape, F32, kind="ExternalInput").ap() for n, a in arrays.items()]
    args.append(nc.dram_tensor("out_y", (N_SEQ * S, D), F32, kind="ExternalOutput").ap())
    encoder_program(nc, *args)
    r = run_bass_kernel_spmd(nc, [{f"in_{n}": a for n, a in arrays.items()}], core_ids=[0])
    y = r.results[0]["out_y"].reshape(N_SEQ, 1, S, D)
    return y[0], y[1]
```

```python
from contextlib import ExitStack

import numpy as np

import concourse.bass as bass
import concourse.mybir as mybir

F32 = mybir.dt.float32
F32R = mybir.dt.float32r
ACT = mybir.ActivationFunctionType
ALU = mybir.AluOpType

P = 128
D = 1024
S = 1024
KC = D // P
TT = S // P
HALF = 512
N_SEQ = 2
HEADS = 8
DK = 64
PAIRS = HEADS // 2
D_FF = 2816
FC = D_FF // P
GROUPS = FC // 2
POOL_W = 512
EPS = 1e-6
K_SCALE = DK ** -0.5
PAD = 8
Q0, K0, V0, GS0, P0 = 0, 512, 1024, 2048, 3072
GA0 = P0 + POOL_W
GB0 = GA0 + D

C_COS = 0
C_SIN = C_COS + TT * 32
C_DIFP = C_SIN + TT * 32
C_DIFN = C_DIFP + P
C_ID = C_DIFN + P
C_QUERY = C_ID + P
C_POS = C_QUERY + P
POOL_COLS = 21
C_POOL = C_POS + 2
C_ALL = C_POOL + PAIRS * POOL_COLS

T_DK, T_DC, T_GAIN, T_PS, T_LGF, T_LGB, T_LGQ, T_POOL = 0, 4, 6, 8, 10, 12, 14, 16
T_BUILT = 16
T_ALL = T_BUILT + POOL_COLS

R_BADA, R_GMIX, R_GAIN, R_PS, R_GFFN, R_C, R_ALL = 0, 48, 56, 64, 72, 80, 96

ADA_RING = 8
ADA_GROUPS = 2 * D // HALF
ADA_PARTS = 3
ADA_ROWS = ADA_GROUPS * N_SEQ
ADA_SLOT = (0, 2, 3)
Y_RING = 6


class Tally:

    ORDER = (("first", 0), ("mix", 0), ("mid", 0), ("ffn", 0), ("swap", 0), ("mix", 1), ("mid", 1), ("ffn", 1),
             ("last", 1))
    TIMES = {"first": 1, "mix": PAIRS, "mid": 1, "ffn": GROUPS, "swap": 1, "last": 1}

    def __init__(self, sem, setup=0, **per):
        self.sem, self.setup, self.per = sem, setup, per

    def at(self, where, n):
        region, seq, it = where
        base = self.setup + n
        for r, _ in self.ORDER[:self.ORDER.index((region, seq))]:
            base += self.TIMES[r] * self.per.get(r, 0)
        if self.per.get(region, 0) and self.TIMES[region] > 1:
            base = it * self.per[region] + base
        return self.sem, base


STEPS = {
    "first": [(f"X{t}", t % 4) for t in range(TT)] + [("R0", 1), ("R1", 1)],
    "mix": [("Q0", 1), ("Q1", 2), ("Q2", 3), ("Q3", 0), ("P", 1), ("GS0", 2), ("TQ", 0), ("TK", 1),
            ("KV0", 3), ("SC0", 0), ("GA0", 2), ("O0", 1), ("KV1", 0), ("SC1", 2), ("GB0", 3),
            ("O1", 1), ("BB0", 0), ("TR0", 2), ("GS1", 3), ("GA1", 1), ("TR1", 0), ("GB1", 2), ("BB1", 3),
            ("W0", 1), ("W1", 2), ("W2", 3), ("W3", 0), ("W4", 1), ("W5", 2), ("W6", 3), ("W7", 0)],
    "mid": [("ST0", 1), ("ST1", 1), ("R0", 0), ("R1", 0)],
    "ffn": [(f"U{i}", (i + 1) % 4) for i in range(4)] + [(f"W{d}", (d + 1) % 4) for d in range(KC)],
    "swap": [("X0", 1), ("X1", 2), ("X2", 3), ("X3", 0), ("Y0", 1), ("Y1", 2), ("X4", 3), ("X5", 0), ("Y2", 1), ("Y3", 2),
             ("X6", 3), ("X7", 0), ("Y4", 1), ("Y5", 2), ("R0", 3), ("R1", 3), ("Y6", 0), ("Y7", 3)],
    "last": [(f"Y{t}", (t + 1) % 4) for t in range(TT)],
}
BLOCKS = {
    "mix": [(3, 0), (3, 1), (3, 2), (3, 0), (1, 1), (1, 0), (1, 2), (1, 1), (1, 0), (1, 2), (1, 1), (1, 0), (1, 2)],
    "ffn": [(3, 0), (3, 1), (1, 2), (1, 0), (1, 1), (1, 2)],
}
HIGH_LOW = [("high", 0), ("high", 1), ("high", 2), ("low", 0), ("high", 3), ("low", 1), ("low", 2), ("low", 3)]
N_MIX, N_FFN = len(BLOCKS["mix"]), len(BLOCKS["ffn"])


def constants():
    c = np.zeros((P, C_ALL), np.float32)
    half = DK // 2
    inv = np.float32(10000.0) ** (-np.arange(half, dtype=np.float32) / np.float32(half))
    ang = np.arange(S, dtype=np.float32)[:, None] * inv[None, :].astype(np.float32)
    for col, f in ((C_COS, np.cos), (C_SIN, np.sin)):
        t = f(ang).astype(np.float32).reshape(TT, P, half).transpose(1, 0, 2)
        c[:, col:col + TT * half] = t.reshape(P, TT * half)
    p = np.arange(P)
    dif = p[None, :] - p[:, None]
    c[:, C_DIFP:C_DIFP + P] = np.maximum(dif, 0)
    c[:, C_DIFN:C_DIFN + P] = np.maximum(-dif, 0)
    c[:, C_ID:C_ID + P] = np.eye(P)
    c[:, C_QUERY:C_QUERY + P] = p[None, :] + 1
    c[:, C_POS:C_POS + 2] = np.stack([P - 1 - p, p], 1)
    for g in range(PAIRS):
        w = 2 ** (g + 1)
        o = C_POOL + g * POOL_COLS
        c[:, o:o + 4] = [1.0 if level <= g else 0.0 for level in range(4)]
        c[:, o + 4] = 1.0 / w
        t = np.concatenate([np.arange(PAD), np.arange(S - PAD, S)])
        cnt = np.minimum(t + w // 2, S) - np.maximum(t - w // 2, 0)
        c[:, o + 5:o + 21] = np.float32(w) / cnt.astype(np.float32)
    return c


def encoder_program(nc, x, c, w_ada, b_ada, g_mix, w_in, decay_f, decay_b, gn_gain, w_pool, pool_scale,
                    w_out, g_ffn, w_up, conv_w, conv_b, w_down, g_final, consts, y):
    ctx = ExitStack()
    with ctx:
        def sb(name, shape, dt=F32, stack=ctx):
            return stack.enter_context(nc.sbuf_tensor(name, shape, dt))

        def sem(name):
            return ctx.enter_context(nc.semaphore(name))

        ps = ctx.enter_context(nc.psum_tensor("ps", [P, 4, 2 * HALF], F32))

        roles = ExitStack()
        xT = [sb("xT0", [P, KC, S], F32, roles)]
        h_hi = [sb("h_hi0", [P, KC, S], F32R, roles)]
        h_lo = [sb("h_lo0", [P, KC, S], F32R, roles)]
        roles.close()
        h_lo.append(sb("h_lo1", [P, KC, S], F32R))
        xT.append(sb("xT1", [P, KC, S]))
        h_hi.append(sb("h_hi1", [P, KC, S], F32R))
        w_raw = sb("w_raw", [P, 2, 1024])
        w_hi = sb("w_hi", [P, 3, 1024], F32R)
        w_lo = sb("w_lo", [P, 3, 1024], F32R)
        cst = sb("cst", [P, C_ALL])
        ones = sb("ones", [P, P])
        vecT = sb("vecT", [P, R_ALL])
        convT = sb("convT", [P, 2 * FC, 4])
        modT = sb("modT", [P, N_SEQ, 48])
        silT = sb("silT", [P, KC, 2 * ADA_ROWS - N_SEQ])
        pairT = sb("pairT", [P, PAIRS, T_BUILT])
        pairS = sb("pairS", [P, T_ALL])
        convS = sb("convS", [P, 2, 2, 4])
        lg = sb("lg", [P, 2, PAIRS, 2])
        sil_raw = sb("sil_raw", [P, 16])
        msq = sb("msq", [P, TT])
        x_ms = sb("x_ms", [P, TT])
        y_ms = sb("y_ms", [P, TT])
        y_rstd = sb("y_rstd", [P, TT])
        rstd = sb("rstd", [P, TT])
        mhalf = sb("mhalf", [P, TT])
        bst = sb("bst", [P, TT, 6])
        mv = sb("mv", [P, TT, 2])
        veps = sb("veps", [P, TT])
        grs = sb("grs", [P, TT])

        ident = cst[:, C_ID:C_ID + P]

        mix = ExitStack()
        m_hi = sb("m_hi", [P, 2, S], F32R, mix)
        m_lo = sb("m_lo", [P, 2, S], F32R, mix)
        rot = sb("rot", [P, TT, 256], F32, mix)
        v_sb = sb("v_sb", [P, TT, 256], F32, mix)
        tokb = sb("tokb", [P, TT, P], F32, mix)
        kdp = sb("kdp", [P, TT, P], F32, mix)
        qdT = sb("qdT", [P, S], F32, mix)
        qT = sb("qT", [P, S], F32, mix)
        kT = sb("kT", [P, S], F32, mix)
        state = sb("state", [P, S + 2 * PAD], F32, mix)
        bufA = sb("bufA", [P, S], F32, mix)
        bufB = sb("bufB", [P, S], F32, mix)
        poolU = sb("poolU", [P, S + 2 * PAD], F32, mix)
        dec = sb("dec", [P, 4, P], F32, mix)
        wpool = sb("wpool", [P, 256], F32, mix)
        mix.close()

        other = ExitStack()
        a_hi = sb("a_hi", [P, 2, S], F32R, other)
        a_lo = sb("a_lo", [P, 2, S], F32R, other)
        ca = sb("ca", [P, S], F32, other)
        cl = sb("cl", [P, S], F32, other)
        g_row = sb("g_row", [P, S], F32, other)
        spare = sb("spare", [P, S], F32, other)
        tn = sb("tn", [P, 2, S], F32, other)
        hf = sb("hf", [P, 2, S], F32, other)
        diag = sb("diag", [P, S], F32, other)
        xin = sb("xin", [P, 4, S], F32, other)
        rrow = sb("rrow", [P, S], F32, other)
        other.close()
        out = ExitStack()
        y_sb = sb("y_sb", [P, Y_RING, S], F32, out)
        out.close()
        middle = ExitStack()
        merged = sb("merged", [P, 4, S], F32, middle)
        sq_b = sb("sq_b", [P, 4, S], F32, middle)
        middle.close()
        start = ExitStack()
        ada = sb("ada", [P, ADA_RING, 2, HALF], F32, start)
        over_tn = sb("over_tn", [P, 2, S], F32, start)
        rows = sb("rows", [P, 3, P], F32, start)
        hf_rest = sb("hf_rest", [P, 2 * S - 3 * P], F32, start)
        diag_over = sb("diag_over", [P, S], F32, start)
        ada_rows = sb("ada_rows", [ADA_ROWS, 2, HALF], F32, start)
        small = sb("small", [P, 6, 16], F32, start)
        start.close()
        sq = [xin[:, k, :] for k in range(4)] + [sq_b[:, k, :] for k in range(4)]

        def tally(name, setup=0, **per):
            return Tally(sem(name), setup, **per)

        full = [tally(f"psum_full{n}", 0, **{r: sum(slot == n for _, slot in STEPS[r]) for r in STEPS})
                for n in range(4)]

        def place(region, step):
            slot = dict(STEPS[region])[step]
            turns = [name for name, other in STEPS[region] if other == slot]
            return slot, turns.index(step) + 1

        def brought(region, i):
            return 16 * sum(n for j, (n, _) in enumerate(BLOCKS[region]) if j % 2 == i % 2 and j <= i)

        raw_in = [tally(f"raw_in{r}", 0, mix=brought("mix", N_MIX - 1 - (N_MIX - 1 - r) % 2),
                        ffn=brought("ffn", N_FFN - 2 + r)) for r in range(2)]
        hi_done = tally("w_hi_done", 0, mix=N_MIX, ffn=N_FFN)
        lo_done = tally("w_lo_done", 1, mix=N_MIX, ffn=N_FFN)
        q_block = tally("q_block_used", 0, mix=3)

        const_in = sem("const_in")
        rows_in = sem("rows_in")
        decay_in = sem("decay_in")
        ones_set = sem("ones_set")
        ada_in = [sem(f"ada_in{i}") for i in range(ADA_RING)]
        ada_used = sem("ada_used")
        ada_rows_set = sem("ada_rows_set")
        ada_turned = sem("ada_turned")
        mod_based = sem("mod_based")
        mod_ready = sem("mod_ready")
        vec_done = sem("vec_done")
        table_step = sem("table_step")
        sil_step = sem("sil_step")
        table_act = sem("table_act")
        table_args = sem("table_args")
        sil_tanh = sem("sil_tanh")
        sil_done = sem("sil_done")

        vec_turned = sem("vec_turned")
        x_in = [tally(f"x_in{i}", 0, first=32, swap=32) for i in range(4)]
        x_squared = tally("x_squared", 0, first=TT, swap=TT)
        xT_set = [tally("xT_set_dve", 0, first=TT // 2, swap=6), tally("xT_set_act", 0, first=TT // 2, swap=2)]
        sq_done = tally("sq_done", 0, mid=KC)
        sum_low = tally("sum_low", 0, mid=3)
        sum_all = tally("sum_all", 0, mid=6)
        msq_done = tally("msq_done", 0, mid=2)
        rstd_done = tally("rstd_done", 0, first=1, mid=2, swap=1)
        diag_done = tally("diag_done", 0, first=2, mid=2, swap=2)
        rrow_done = tally("rrow_done", 0, first=1, swap=1)
        tn_done = tally("tn_done", 0, first=KC + 1, mid=KC + 1, swap=KC + 1)
        hhi_done = tally("h_hi_done", 0, first=KC + 1, mid=KC + 1, swap=KC + 1)
        hf_done = tally("h_full_done", 0, first=KC + 1, mid=KC + 1, swap=KC + 1)
        hlo_done = tally("h_lo_done", 0, first=KC + 1, mid=KC + 1, swap=KC + 1)
        res_done = tally("residual_done", 4, mix=KC, ffn=KC)
        g_row_in = tally("g_row_in", 0, mid=16)
        y_squared = tally("y_squared", 0, swap=TT, last=TT)
        x_eps = tally("x_plus_eps", 0, first=1, swap=1)
        y_eps = tally("y_plus_eps", 0, swap=TT // 2, last=TT // 2)
        y_rstd_done = tally("y_rstd_done", 0, swap=TT // 2, last=TT // 2)
        y_scaled = tally("y_scaled", 0, swap=TT, last=TT)
        y_out = [tally(f"y_out{i}", 0, swap=16 * len(range(i, TT, Y_RING)), last=16 * len(range(i, TT, Y_RING)))
                 for i in range(Y_RING)]

        pair_set = tally("pair_set", 0, mix=1)
        dec_arg = tally("dec_arg", 0, mix=6)
        dec_done = tally("dec_done", 0, mix=1)
        wpool_in = tally("wpool_in", 0, mix=16)
        v_done = tally("v_done", 0, mix=4)
        rope_mul = tally("rope_mul", 0, mix=4)
        rope_done = tally("rope_done", 0, mix=4)
        qT_done = tally("qT_done", 0, mix=1)
        kT_done = tally("kT_done", 0, mix=1)
        kd_done = tally("kd_done", 0, mix=2)
        qdT_done = tally("qdT_done", 0, mix=2)
        state_step = tally("state_step", 0, mix=2 * (2 + 14))
        pt_done = tally("scores_done", 0, mix=2)
        p_copied = tally("p_copied", 0, mix=1)
        pool_step = tally("pool_step", 0, mix=8)
        stat_done = tally("gn_stats", 0, mix=2)
        mv_done = tally("gn_moments", 0, mix=2)
        veps_done = tally("gn_veps", 0, mix=2)
        grs_done = tally("gn_rstd", 0, mix=2)
        cent_done = tally("gn_centred", 0, mix=2)
        retn_done = tally("gn_done", 0, mix=2)
        th_done = tally("tanh_swish", 0, mix=2)
        sw_done = tally("swish_done", 0, mix=2)
        ta_done = tally("tanh_a", 0, mix=2)
        ga_done = tally("gate_a_done", 0, mix=2)
        tb_done = tally("tanh_b", 0, mix=2)
        ma_done = tally("branch_a_done", 0, mix=2)
        mb_done = tally("branch_b_done", 1, mix=2)
        mg_done = tally("merged", 0, mix=2)
        mhi_done = tally("merged_hi", 0, mix=2)
        mlo_done = tally("merged_lo", 0, mix=2)

        conv_set = tally("conv_set", 0, ffn=1)
        mid_tap = tally("middle_tap", 0, ffn=4)
        side_tap = tally("side_taps", 0, ffn=8)
        gelu_done = tally("gelu_done", 0, ffn=2)
        prod_done = tally("prod_done", 0, ffn=2)
        ahi_done = tally("a_hi_done", 0, ffn=2)
        alo_done = tally("a_lo_done", 0, ffn=2)

        def slot_of(where, step):
            return place(where[0], step)[0]

        def filled(where, step):
            slot, turn = place(where[0], step)
            return full[slot].at(where, turn)

        pieces = [(0, 0, HALF), (0, HALF, S)] + [(k, 0, S) for k in range(1, KC)]

        def sq_view(ap, n):
            return ap.rearrange("p (a b) -> p a b", a=n)

        w_in_v = w_in.rearrange("(k p) n -> p k n", p=P)
        w_out_v = w_out.rearrange("(k p) n -> p k n", p=P)
        w_pool_v = w_pool.rearrange("g p n -> p g n")
        w_up_v = w_up.rearrange("(k p) n -> p k n", p=P)
        w_down_v = w_down.rearrange("(k p) n -> p k n", p=P)
        w_ada_v = w_ada.rearrange("(k p) n -> p k n", p=P)

        block = ctx.enter_context(nc.Block())

        @block.sync
        def _(sp):
            sp.dma_start(cst[:, :], consts).then_inc(const_in, 16)
            chunked = "(c p) -> c p"
            parts = [(0, R_BADA, b_ada.rearrange(chunked, p=P)), (0, R_GMIX, g_mix.rearrange(chunked, p=P)),
                     (0, R_GAIN, gn_gain.rearrange(chunked, p=P)), (0, R_PS, pool_scale.rearrange(chunked, p=P)),
                     (0, R_GFFN, g_ffn.rearrange(chunked, p=P)),
                     (0, R_C, c.rearrange("s (c p) -> (s c) p", p=P)),
                     (1, 0, conv_w[0:2, :].rearrange("t (c p) -> (t c) p", p=P)),
                     (2, 0, conv_w[2:3, :].rearrange("t (c p) -> (t c) p", p=P)),
                     (2, 2 * FC, conv_b.rearrange(chunked, p=P))]
            for i, r, src in parts:
                sp.dma_start(rows[r:r + src.shape[0], i, :], src).then_inc(rows_in, 16)
            for i, src in enumerate((decay_f, decay_b)):
                sp.dma_start(lg[:, i, :, :].rearrange("p a b -> p (a b)"), src.partition_broadcast(P)).then_inc(decay_in, 16)
            with sp.Fori(0, ADA_PARTS * ADA_GROUPS // 2) as it:
                for s in range(ADA_RING):
                    sp.wait_ge(ada_used, it * ADA_RING + (s + 1))
                    k = 2 * (s % 4)
                    src = w_ada_v[:, k:k + 2, bass.ds((it * 2 + s // 4) * HALF, HALF)]
                    sp.dma_start(ada[:, s, :, :], src).then_inc(ada_in[s], 16)

            def load(where, i, parts):
                sp.wait_ge(*lo_done.at(where, max(i - 1, 0)))
                for dst, src in parts:
                    sp.dma_start(dst, src).then_inc(raw_in[i % 2].sem, 16)

            def mix_block(where, i):
                region, _, pr = where
                if i < 4:
                    dst = sq_view(w_raw[:, i % 2, :], 2)
                    load(where, i, [(dst[:, :, a:a + n], w_in_v[:, 2 * i:2 * i + 2, bass.ds(col, n)])
                                    for a, n, col in ((0, P, pr * P + Q0), (P, P, pr * P + K0),
                                                      (2 * P, 2 * P, pr * 2 * P + V0))])
                elif i < 11:
                    col = {4: pr * P + P0, 5: pr * 2 * P + GS0, 6: pr * 2 * P + GA0, 7: pr * 2 * P + GB0,
                           8: pr * 2 * P + (GS0 + P), 9: pr * 2 * P + (GA0 + P), 10: pr * 2 * P + (GB0 + P)}[i]
                    load(where, i, [(sq_view(w_raw[:, i % 2, :], KC), w_in_v[:, :, bass.ds(col, P)])])
                else:
                    src = w_out_v[:, bass.ds(pr * 2, 2), (i - 11) * HALF:(i - 10) * HALF]
                    load(where, i, [(sq_view(w_raw[:, i % 2, :], 2), src)])

            def ffn_block(where, i):
                g = where[2]
                if i < 4:
                    dst = sq_view(w_raw[:, i % 2, :], KC)
                    src = w_up_v[:, :, bass.ds(g * 2 * P + ((i // 2) * P + (i % 2) * D_FF), P)]
                    cuts = (0, 3, 6, KC) if i < 2 else (0, KC)
                    load(where, i, [(dst[:, a:b, :], src[:, a:b, :]) for a, b in zip(cuts, cuts[1:])])
                else:
                    src = w_down_v[:, bass.ds(g * 2, 2), (i - 4) * HALF:(i - 3) * HALF]
                    load(where, i, [(sq_view(w_raw[:, i % 2, :], 2), src)])

            for seq in range(N_SEQ):
                with sp.Fori(0, PAIRS) as pr:
                    where = ("mix", seq, pr)
                    for i in range(N_MIX):
                        mix_block(where, i)
                        if i == 6:
                            sp.wait_ge(*mb_done.at(where, 0))
                            sp.dma_start(wpool[:, :].unsqueeze(1), w_pool_v[:, bass.ds(pr, 1), :]).then_inc(wpool_in.sem, 16)
                with sp.Fori(0, GROUPS) as g:
                    for i in range(N_FFN):
                        ffn_block(("ffn", seq, g), i)
            for i in range(2):
                mix_block(("last", 1, 0), i)

        @block.tensor
        def _(pe):
            def weights(where, i):
                pe.wait_ge(*hi_done.at(where, i + 1))
                pe.wait_ge(*lo_done.at(where, i + 1))
                return BLOCKS[where[0]][i][1]

            def three_passes(slot, w_slot, col, act_hi, act_lo, k, first, last):
                for n, (w, a) in enumerate(((w_hi, act_hi), (w_hi, act_lo), (w_lo, act_hi))):
                    for b in range(2):
                        ins = pe.matmul(ps[:, slot, b * HALF:(b + 1) * HALF], w[:, w_slot, col:col + P],
                                        a[:, k, b * HALF:(b + 1) * HALF],
                                        start=first and n == 0, stop=last and n == 2)
                return ins

            def one_pass(slot, w, act, k, last):
                for b in range(2):
                    ins = pe.matmul(ps[:, slot, b * HALF:(b + 1) * HALF], w, act[:, k, b * HALF:(b + 1) * HALF],
                                    start=False, stop=last)
                return ins

            def unit(where, i, step):
                ws = weights(where, i)
                slot = slot_of(where, step)
                for k in range(KC):
                    ins = three_passes(slot, ws, k * P, h_hi[where[1]], h_lo[where[1]], k, k == 0, k == KC - 1)
                ins.then_inc(full[slot].sem, 1)

            def two_units(where, norm):
                for i in range(2):
                    pe.wait_ge(*res_done.at(where, i - 3))
                ws = [weights(where, i) for i in range(2)]
                for b in range(2):
                    tokens = slice(b * HALF, (b + 1) * HALF)
                    pe.wait_ge(*hhi_done.at(norm, b + 1))
                    for i in range(2):
                        out = ps[:, slot_of(where, f"U{i}"), tokens]
                        pe.matmul(out, w_hi[:, ws[i], 0:P], h_hi[where[1]][:, 0, tokens], start=True, stop=False)
                        pe.matmul(out, w_lo[:, ws[i], 0:P], h_hi[where[1]][:, 0, tokens], start=False, stop=False)
                    pe.wait_ge(*hlo_done.at(norm, b + 1))
                    for i in range(2):
                        out = ps[:, slot_of(where, f"U{i}"), tokens]
                        pe.matmul(out, w_hi[:, ws[i], 0:P], h_lo[where[1]][:, 0, tokens], start=False, stop=False)
                for k in range(1, KC):
                    pe.wait_ge(*hhi_done.at(norm, k + 2))
                    pe.wait_ge(*hlo_done.at(norm, k + 2))
                    for i in range(2):
                        slot = slot_of(where, f"U{i}")
                        ins = three_passes(slot, ws[i], k * P, h_hi[where[1]], h_lo[where[1]], k, False, k == KC - 1)
                        if k == KC - 1:
                            ins.then_inc(full[slot].sem, 1)

            def turn(where, step, source):
                slot = slot_of(where, step)
                for t in range(TT):
                    ins = pe.transpose(ps[:, slot, t * P:(t + 1) * P], source(t), ident)
                ins.then_inc(full[slot].sem, 1)

            def partial(where, block0, act_hi, act_lo, hi_t, lo_t, slot_read):
                for half in range(2):
                    ws = weights(where, block0 + half)
                    steps = [slot_of(where, f"W{4 * half + j}") for j in range(4)]
                    if half == 0:
                        pe.wait_ge(*hi_t.at(where, 1))
                        pe.wait_ge(*lo_t.at(where, 1))
                    for j, slot in enumerate(steps):
                        if half == 0:
                            pe.wait_ge(*slot_read[j])
                        else:
                            pe.wait_ge(*res_done.at(where, j + 1))
                        three_passes(slot, ws, j * P, act_hi, act_lo, 0, True, False)
                    if half == 0:
                        pe.wait_ge(*hi_t.at(where, 2))
                        for kind, j in HIGH_LOW:
                            slot = steps[j]
                            col = slice(HALF + j * P, HALF + (j + 1) * P)
                            if kind == "high":
                                one_pass(slot, w_hi[:, ws, col], act_hi, 1, False)
                                one_pass(slot, w_lo[:, ws, col], act_hi, 1, False)
                            else:
                                if j == 0:
                                    pe.wait_ge(*lo_t.at(where, 2))
                                one_pass(slot, w_hi[:, ws, col], act_lo, 1, True).then_inc(full[slot].sem, 1)
                    else:
                        for j, slot in enumerate(steps):
                            three_passes(slot, ws, HALF + j * P, act_hi, act_lo, 1, False,
                                         True).then_inc(full[slot].sem, 1)

            def spread_rstd(where):
                slot = slot_of(where, "R0")
                for b in range(2):
                    pe.wait_ge(*diag_done.at(where, b + 1))
                    pe.matmul(ps[:, slot, b * HALF:(b + 1) * HALF], ones[:, :], diag[:, b * HALF:(b + 1) * HALF],
                              start=True, stop=True).then_inc(full[slot].sem, 1)

            def turn_x(where, t):
                pe.wait_ge(*x_in[t % 4].at(where, 16 * (t // 4 + 1)))
                turn(where, f"X{t}", lambda k: xin[:, t % 4, k * P:(k + 1) * P])

            def turn_y(where, t):
                turn(where, f"Y{t}", lambda k: xT[where[1]][:, k, t * P:(t + 1) * P])

            pe.sem_inc(ada_used, 1)
            pe.wait_ge(const_in, 16)
            pe.wait_ge(ones_set, 2)
            first = ("first", 0, 0)
            for t in range(3):
                turn_x(first, t)
            pe.wait_ge(rows_in, 16 * 9)
            for i, n in enumerate((R_ALL, 4 * FC, 4 * FC)):
                ins = pe.transpose(ps[:, 3, i * P:i * P + n], rows[0:n, i, :], cst[0:n, C_ID:C_ID + n])
            ins.then_inc(vec_turned, 1)
            pe.wait_ge(vec_done, 2)
            turn_x(first, 3)
            pe.sem_inc(ada_used, ADA_RING - 1)
            for t in (4, 5):
                pe.wait_ge(*xT_set[t % 2].at(first, (t - 4) // 2 + 1))
                turn_x(first, t)
            def ada_turn(part):
                pe.wait_ge(ada_rows_set, part + 1)
                for j in range(4):
                    ins = pe.transpose(ps[:, ADA_SLOT[part], HALF + j * ADA_ROWS:HALF + (j + 1) * ADA_ROWS],
                                       ada_rows[:, part % 2, j * P:(j + 1) * P], cst[0:ADA_ROWS, C_ID:C_ID + ADA_ROWS])
                ins.then_inc(ada_turned, 1)

            pe.wait_ge(sil_done, 1)
            pe.wait_ge(*xT_set[0].at(first, 3))
            for part in range(ADA_PARTS):
                if part:
                    pe.wait_ge(*xT_set[part - 1].at(first, 4))
                for g in range(ADA_GROUPS):
                    window = N_SEQ * (ADA_GROUPS - 1 - g)
                    for k in range(KC):
                        turn_no, s = divmod((part * ADA_GROUPS + g) * 4 + k // 2, ADA_RING)
                        if k % 2 == 0:
                            pe.wait_ge(ada_in[s], 16 * (turn_no + 1))
                        ins = pe.matmul(ps[0:ADA_ROWS, ADA_SLOT[part], 0:HALF], silT[:, k, window:window + ADA_ROWS],
                                        ada[:, s, k % 2, :], start=g == 0 and k == 0,
                                        stop=g == ADA_GROUPS - 1 and k == KC - 1)
                        if k % 2:
                            ins.then_inc(ada_used, 1)
                        if part == 0 and g in (0, 1) and k == KC - 1:
                            pe.wait_ge(*xT_set[g].at(first, 2))
                            turn_x(first, 6 + g)
                        if part == 0 and g == 2 and k == KC - 1:
                            pe.wait_ge(*xT_set[1].at(first, 3))
                            spread_rstd(first)
                        if part and g == part - 1 and k == 3:
                            ada_turn(part - 1)
            ada_turn(ADA_PARTS - 1)
            pe.wait_ge(mod_based, ADA_PARTS)

            for seq in range(N_SEQ):
                pre = ("swap", 0, 0) if seq else first
                if seq:
                    for step, ready in (("X0", res_done.at(pre, -3)), ("X1", res_done.at(pre, -2)),
                                        ("X2", res_done.at(pre, -1)), ("X3", res_done.at(pre, 0)),
                                        ("Y0", xT_set[0].at(pre, 1)), ("Y1", xT_set[0].at(pre, 2)),
                                        ("X4", xT_set[0].at(pre, 3)), ("X5", xT_set[0].at(pre, 4)),
                                        ("Y2", y_scaled.at(pre, 1)), ("Y3", y_scaled.at(pre, 2)),
                                        ("X6", xT_set[0].at(pre, 5)), ("X7", xT_set[1].at(pre, 1)),
                                        ("Y4", y_scaled.at(pre, 3)), ("Y5", y_scaled.at(pre, 4)),
                                        ("R0", xT_set[0].at(pre, 6)), ("Y6", xT_set[1].at(pre, 2)),
                                        ("Y7", rrow_done.at(pre, 1))):
                        pe.wait_ge(*ready)
                        if step == "R0":
                            spread_rstd(pre)
                        elif step[0] == "X":
                            turn_x(pre, int(step[1]))
                        else:
                            turn_y(pre, int(step[1]))
                    pe.wait_ge(*y_scaled.at(pre, TT))
                with pe.Fori(0, PAIRS) as pr:
                    where = ("mix", seq, pr)
                    for i in range(4):
                        ws = weights(where, i)
                        for k in (2 * i, 2 * i + 1):
                            if k:
                                pe.wait_ge(*hhi_done.at(pre, k + 2))
                                pe.wait_ge(*hlo_done.at(pre, k + 2))
                            col = (k % 2) * HALF
                            for t in range(TT):
                                if k == 0 and t % 4 == 0:
                                    pe.wait_ge(*hhi_done.at(pre, t // 4 + 1))
                                    pe.wait_ge(*hlo_done.at(pre, t // 4 + 1))
                                slot = slot_of(where, f"Q{t // 2}")
                                if k == 0 and t % 2 == 0:
                                    pe.wait_ge(*res_done.at(where, t // 2 - 3))
                                for n, (a, w) in enumerate(((h_hi[seq], w_hi), (h_hi[seq], w_lo), (h_lo[seq], w_hi))):
                                    ins = pe.matmul(ps[:, slot, (t % 2) * HALF:(t % 2 + 1) * HALF],
                                                    a[:, k, t * P:(t + 1) * P], w[:, ws, col:col + HALF],
                                                    start=k == 0 and n == 0, stop=k == KC - 1 and n == 2)
                                if k == KC - 1 and t % 2:
                                    ins.then_inc(full[slot].sem, 1)
                        if i < 3:
                            ins.then_inc(q_block.sem, 1)

                    def products(h):
                        slot = slot_of(where, f"KV{h}")
                        if h:
                            pe.wait_ge(*pt_done.at(where, 1))
                        pe.wait_ge(*kd_done.at(where, h + 1))
                        pe.wait_ge(*v_done.at(where, 4))
                        for t in range(TT):
                            ins = pe.matmul(ps[:, slot, t * P:(t + 1) * P], kdp[:, t, :], v_sb[:, t, h * P:(h + 1) * P],
                                            start=True, stop=True)
                        ins.then_inc(full[slot].sem, 1)

                    def scores(h):
                        slot = slot_of(where, f"SC{h}")
                        if h:
                            pe.wait_ge(*ta_done.at(where, 1))
                        pe.wait_ge(*qT_done.at(where, 1))
                        pe.wait_ge(*kT_done.at(where, 1))
                        rows_h = slice(h * DK, (h + 1) * DK)
                        for t in range(TT):
                            ins = pe.matmul(ps[:, slot, t * P:(t + 1) * P], kT[rows_h, t * P:(t + 1) * P],
                                            qT[rows_h, t * P:(t + 1) * P], start=True, stop=True)
                        ins.then_inc(full[slot].sem, 1)

                    def outputs(h):
                        slot = slot_of(where, f"O{h}")
                        if h:
                            pe.wait_ge(*cent_done.at(where, 1))
                        else:
                            pe.wait_ge(*kT_done.at(where, 1))
                        pe.wait_ge(*pt_done.at(where, h + 1))
                        pe.wait_ge(*state_step.at(where, 16 * (h + 1)))
                        pe.wait_ge(*qdT_done.at(where, h + 1))
                        for t in range(TT):
                            o = ps[:, slot, t * P:(t + 1) * P]
                            pe.matmul(o, kdp[:, t, :], v_sb[:, t, h * P:(h + 1) * P], start=True, stop=False)
                            ins = pe.matmul(o, qdT[:, t * P:(t + 1) * P], state[:, t * P:(t + 1) * P], start=False, stop=True)
                        ins.then_inc(full[slot].sem, 1)

                    def branch_b(h):
                        slot = slot_of(where, f"BB{h}")
                        if h == 0:
                            pe.wait_ge(*state_step.at(where, 32))
                        else:
                            pe.wait_ge(*sw_done.at(where, 2))
                        pe.wait_ge(*pool_step.at(where, 8))
                        pe.wait_ge(*wpool_in.at(where, 16))
                        for b in range(2):
                            ins = pe.matmul(ps[:, slot, b * HALF:(b + 1) * HALF], wpool[:, h * P:(h + 1) * P],
                                            poolU[:, b * HALF:(b + 1) * HALF], start=True, stop=True)
                        ins.then_inc(full[slot].sem, 1)

                    def turn_ret(h):
                        pe.wait_ge(*retn_done.at(where, h + 1))
                        if h == 0:
                            pe.wait_ge(*pt_done.at(where, 2))
                        else:
                            pe.wait_ge(*mb_done.at(where, 1))
                        turn(where, f"TR{h}", lambda t: tokb[:, t, :])

                    pe.wait_ge(*v_done.at(where, 1))
                    unit(where, 4, "P")
                    pe.wait_ge(*v_done.at(where, 2))
                    unit(where, 5, "GS0")
                    pe.wait_ge(*rope_done.at(where, 4))
                    pe.wait_ge(*v_done.at(where, 4))
                    pe.wait_ge(*p_copied.at(where, 1))
                    for i, step in enumerate(("TQ", "TK")):
                        turn(where, step, lambda t: rot[:, t, i * P:(i + 1) * P])
                    products(0)
                    scores(0)
                    pe.wait_ge(*sw_done.at(where, 1))
                    unit(where, 6, "GA0")
                    outputs(0)
                    scores(1)
                    products(1)
                    pe.wait_ge(*state_step.at(where, 16))
                    unit(where, 7, "GB0")
                    outputs(1)
                    branch_b(0)
                    turn_ret(0)
                    pe.wait_ge(*tb_done.at(where, 1))
                    unit(where, 8, "GS1")
                    pe.wait_ge(*cent_done.at(where, 2))
                    unit(where, 9, "GA1")
                    turn_ret(1)
                    pe.wait_ge(*ma_done.at(where, 1))
                    unit(where, 10, "GB1")
                    branch_b(1)
                    partial(where, 11, m_hi, m_lo, mhi_done, mlo_done,
                            [ta_done.at(where, 2), tb_done.at(where, 2), mb_done.at(where, 2), ma_done.at(where, 2)])
                mid = ("mid", seq, 0)
                slot = slot_of(mid, "ST0")
                pe.wait_ge(*res_done.at(mid, -3))
                for b in range(2):
                    pe.wait_ge(*sum_all.at(mid, 4 + 2 * b))
                    for t in range(4 * b, 4 * b + 4):
                        ins = pe.matmul(ps[:, slot, b * HALF + t:b * HALF + t + 1], sq[4][:, t * P:(t + 1) * P], ones[:, 0:1],
                                        start=True, stop=True)
                    ins.then_inc(full[slot].sem, 1)
                spread_rstd(mid)
                with pe.Fori(0, GROUPS) as g:
                    where = ("ffn", seq, g)
                    two_units(where, mid)
                    for i in (2, 3):
                        pe.wait_ge(*res_done.at(where, i - 3))
                        unit(where, i, f"U{i}")
                    partial(where, 4, a_hi, a_lo, ahi_done, alo_done,
                            [side_tap.at(where, 2 * i + 2) for i in range(4)])
            last = ("last", 1, 0)
            pe.wait_ge(*res_done.at(last, 0))
            for t in range(TT):
                if t >= 4:
                    pe.wait_ge(*y_scaled.at(last, t - 3))
                turn_y(last, t)

        @block.scalar
        def _(act):
            def split(where, i):
                act.wait_ge(*raw_in[i % 2].at(where, brought(where[0], i)))
                act.activation(w_hi[:, BLOCKS[where[0]][i][1], :], w_raw[:, i % 2, :], ACT.Copy).then_inc(hi_done.sem, 1)

            def evac(where, step, dst, t):
                slot = slot_of(where, step)
                act.wait_ge(*filled(where, step))
                act.activation(dst, ps[:, slot, :], ACT.Copy).then_inc(t.sem, 1)

            def tanh_half(where, step, dst, t):
                slot = slot_of(where, step)
                act.wait_ge(*filled(where, step))
                act.activation(dst[:, :], ps[:, slot, :], ACT.Tanh, scale=0.5).then_inc(t.sem, 1)

            def square_x(where, t):
                act.wait_ge(*x_in[t % 4].at(where, 16 * (t // 4 + 1)))
                if t >= 2:
                    act.wait_ge(*x_squared.at(where, t - 1))
                act.activation(tn[:, t % 2, :], xin[:, t % 4, :], ACT.Square, scale=D ** -0.5,
                               accum_out=x_ms[:, t:t + 1]).then_inc(x_squared.sem, 1)

            def load_x(seq, t):
                act.dma_start(xin[:, t % 4, :], x[seq * S + t * P:seq * S + (t + 1) * P, :]).then_inc(x_in[t % 4].sem, 16)

            def reload_x(where, seq, t):
                act.wait_ge(*filled(where, f"X{t}"))
                act.wait_ge(*x_squared.at(where, t + 1))
                load_x(seq, t + 4)

            def copy_x(where, seq, t):
                slot = slot_of(where, f"X{t}")
                act.wait_ge(*filled(where, f"X{t}"))
                act.activation(xT[seq][:, :, t * P:(t + 1) * P], sq_view(ps[:, slot, :], KC),
                               ACT.Copy).then_inc(xT_set[1].sem, 1)

            def square_y(where, t):
                slot = slot_of(where, f"Y{t}")
                act.wait_ge(*filled(where, f"Y{t}"))
                if t >= 2:
                    act.wait_ge(*y_squared.at(where, t - 1))
                act.activation(hf[:, t % 2, :], ps[:, slot, :], ACT.Square, scale=D ** -0.5,
                               accum_out=y_ms[:, t:t + 1]).then_inc(y_squared.sem, 1)

            def store_y(where, t):
                act.wait_ge(*y_scaled.at(where, t + 1))
                act.dma_start(y[where[1] * S + t * P:where[1] * S + (t + 1) * P, :],
                              y_sb[:, t % Y_RING, :]).then_inc(y_out[t % Y_RING].sem, 16)

            def modulate(where, seq, shift, scale):
                for i, (k, begin, end) in enumerate(pieces):
                    act.wait_ge(*tn_done.at(where, i + 1))
                    if k >= 2:
                        act.wait_ge(*hlo_done.at(where, k))
                    a, b = modT[:, seq, scale + k:scale + k + 1], modT[:, seq, shift + k:shift + k + 1]
                    act.activation(h_hi[seq][:, k, begin:end], tn[:, k % 2, begin:end], ACT.Identity, bias=b,
                                   scale=a).then_inc(hhi_done.sem, 1)
                    act.activation(hf[:, k % 2, begin:end], tn[:, k % 2, begin:end], ACT.Identity, bias=b,
                                   scale=a).then_inc(hf_done.sem, 1)

            first = ("first", 0, 0)
            for t in range(4):
                load_x(0, t)
            for t in range(4):
                square_x(first, t)
                if t < 3:
                    reload_x(first, 0, t)
                if t == 1:
                    copy_x(first, 0, 1)
            act.wait_ge(vec_done, 1)
            act.activation(sil_raw[:, :], vecT[:, R_C:R_C + 2 * KC], ACT.Tanh, scale=0.5).then_inc(sil_tanh, 1)
            reload_x(first, 0, 3)
            copy_x(first, 0, 3)
            square_x(first, 4)
            square_x(first, 5)
            copy_x(first, 0, 5)
            square_x(first, 6)
            square_x(first, 7)
            copy_x(first, 0, 7)
            evac(first, "R1", rrow[:, :], rrow_done)
            act.wait_ge(mod_ready, 1)
            modulate(first, 0, 0, 8)
            act.wait_ge(table_step, 1)
            act.activation(small[:, 1, :], small[:, 0, :], ACT.Exp, scale=-1.0).then_inc(table_act, 1)
            act.wait_ge(table_args, 1)
            act.activation(pairT[:, :, 0:T_GAIN], pairT[:, :, 0:T_GAIN], ACT.Exp).then_inc(table_act, 1)
            split(("mix", 0, 0), 0)
            split(("mix", 0, 0), 1)

            for seq in range(N_SEQ):
                if seq:
                    swap = ("swap", 0, 0)
                    for t in range(4):
                        square_x(swap, t)
                    reload_x(swap, 1, 0)
                    reload_x(swap, 1, 1)
                    reload_x(swap, 1, 2)
                    reload_x(swap, 1, 3)
                    square_y(swap, 0)
                    square_y(swap, 1)
                    square_x(swap, 4)
                    square_x(swap, 5)
                    copy_x(swap, 1, 5)
                    square_y(swap, 2)
                    square_y(swap, 3)
                    square_x(swap, 6)
                    square_x(swap, 7)
                    copy_x(swap, 1, 7)
                    store_y(swap, 0)
                    store_y(swap, 1)
                    square_y(swap, 4)
                    square_y(swap, 5)
                    store_y(swap, 2)
                    store_y(swap, 3)
                    evac(swap, "R1", rrow[:, :], rrow_done)
                    square_y(swap, 6)
                    square_y(swap, 7)
                    store_y(swap, 4)
                    store_y(swap, 5)
                    act.wait_ge(*y_squared.at(swap, TT))
                    modulate(swap, 1, 0, 8)
                    store_y(swap, 6)
                    store_y(swap, 7)
                with act.Fori(0, PAIRS) as pr:
                    where = ("mix", seq, pr)
                    act.wait_ge(*full[0].at(where, 0))
                    split(where, 2)
                    act.wait_ge(*q_block.at(where, 1))
                    split(where, 3)
                    act.wait_ge(*q_block.at(where, 2))
                    split(where, 4)
                    act.wait_ge(*dec_arg.at(where, 6))
                    act.activation(dec[:, :, :], dec[:, :, :], ACT.Exp).then_inc(dec_done.sem, 1)
                    for i in range(4):
                        slot = slot_of(where, f"Q{i}")
                        act.wait_ge(*filled(where, f"Q{i}"))
                        act.wait_ge(*rope_mul.at(where, i + 1))
                        act.activation(v_sb[:, 2 * i:2 * i + 2, :], sq_view(ps[:, slot, :], 2)[:, :, 2 * P:4 * P],
                                       ACT.Copy).then_inc(v_done.sem, 1)
                        if i == 0:
                            act.wait_ge(*filled(where, "Q3"))
                            split(where, 5)
                    split(where, 6)
                    evac(where, "P", state[:, PAD:PAD + S], p_copied)
                    act.wait_ge(*rope_done.at(where, 4))
                    split(where, 7)
                    tanh_half(where, "GS0", bufA, th_done)
                    evac(where, "TK", kT[:, :], kT_done)
                    act.wait_ge(*filled(where, "GS0"))
                    split(where, 8)
                    tanh_half(where, "GA0", bufB, ta_done)
                    act.wait_ge(*filled(where, "GA0"))
                    split(where, 9)
                    act.wait_ge(*ga_done.at(where, 1))
                    tanh_half(where, "GB0", bufB, tb_done)
                    act.wait_ge(*filled(where, "GB0"))
                    split(where, 10)
                    act.wait_ge(*mg_done.at(where, 1))
                    act.activation(m_hi[:, 0, :], bufA[:, :], ACT.Copy).then_inc(mhi_done.sem, 1)
                    act.wait_ge(*mlo_done.at(where, 1))
                    tanh_half(where, "GS1", bufA, th_done)
                    act.wait_ge(*filled(where, "GS1"))
                    split(where, 11)
                    tanh_half(where, "GA1", bufB, ta_done)
                    act.wait_ge(*ga_done.at(where, 2))
                    tanh_half(where, "GB1", bufB, tb_done)
                    act.wait_ge(*filled(where, "GA1"))
                    split(where, 12)
                    act.wait_ge(*mg_done.at(where, 2))
                    act.activation(m_hi[:, 1, :], bufA[:, :], ACT.Copy).then_inc(mhi_done.sem, 1)
                    act.wait_ge(*filled(where, "GB1"))
                    act.wait_ge(*filled(where, "W3"))
                    split(("mix", seq, pr + 1), 0)
                    split(("mix", seq, pr + 1), 1)
                mid = ("mid", seq, 0)
                for k in range(KC):
                    act.wait_ge(*res_done.at(mid, k - 7))
                    act.activation(sq[k], xT[seq][:, k, :], ACT.Square, scale=D ** -0.5).then_inc(sq_done.sem, 1)
                modulate(mid, seq, 24, 32)
                act.dma_start(g_row[:, :], g_final.partition_broadcast(P)).then_inc(g_row_in.sem, 16)
                if seq == 0:
                    for t in range(4):
                        load_x(1, t)
                with act.Fori(0, GROUPS) as g:
                    where = ("ffn", seq, g)

                    def middle_tap(i, dst):
                        slot = slot_of(where, f"U{i}")
                        act.wait_ge(*filled(where, f"U{i}"))
                        col = convS[:, i % 2, i // 2, :]
                        act.activation(dst[:, :], ps[:, slot, :], ACT.Identity, bias=col[:, 3:4],
                                       scale=col[:, 1:2]).then_inc(mid_tap.sem, 1)

                    def gelu(j):
                        act.wait_ge(*side_tap.at(where, 4 * j + 2))
                        act.activation(ca[:, :], ca[:, :], ACT.Gelu_apprx_tanh).then_inc(gelu_done.sem, 1)

                    act.wait_ge(*full[0].at(where, 0))
                    split(where, 2)
                    act.wait_ge(*conv_set.at(where, 1))
                    middle_tap(0, ca)
                    act.wait_ge(*filled(where, "U0"))
                    split(where, 3)
                    gelu(0)
                    middle_tap(1, cl)
                    act.wait_ge(*prod_done.at(where, 1))
                    middle_tap(2, ca)
                    act.wait_ge(*filled(where, "U1"))
                    split(where, 4)
                    gelu(1)
                    act.wait_ge(*alo_done.at(where, 1))
                    middle_tap(3, cl)
                    act.wait_ge(*filled(where, "U2"))
                    split(where, 5)
                    act.wait_ge(*filled(where, "U3"))
                    split(("ffn", seq, g + 1), 0)
                    act.wait_ge(*filled(where, "W3"))
                    split(("ffn", seq, g + 1), 1)
            last = ("last", 1, 0)
            for t in range(TT):
                square_y(last, t)
                if t >= 3:
                    store_y(last, t - 3)
            for t in range(TT - 3, TT):
                store_y(last, t)
            for t in range(Y_RING):
                act.wait_ge(*y_out[t].at(last, 16 * len(range(t, TT, Y_RING))))

        @block.gpsimd
        def _(pool):
            def remainder(where, i):
                ws = BLOCKS[where[0]][i][1]
                pool.wait_ge(*hi_done.at(where, i + 1))
                pool.tensor_tensor(w_lo[:, ws, :], w_raw[:, i % 2, :], w_hi[:, ws, :].bitcast(F32),
                                   ALU.subtract).then_inc(lo_done.sem, 1)

            def inverse_root(dst, src):
                return pool.tensor_tensor(dst, src, mhalf[:, 0:src.shape[1]], ALU.pow)

            def rstd_of_x(where):
                pool.wait_ge(*x_squared.at(where, TT))
                pool.tensor_scalar(x_ms[:, :], x_ms[:, :], EPS, None, ALU.add).then_inc(x_eps.sem, 1)
                pool.wait_ge(*x_eps.at(where, 1))
                inverse_root(rstd[:, :], x_ms[:, :]).then_inc(rstd_done.sem, 1)

            def rstd_of_y(where, i):
                pool.wait_ge(*y_squared.at(where, 2 * i + 2))
                pair = slice(2 * i, 2 * i + 2)
                pool.tensor_scalar(y_ms[:, pair], y_ms[:, pair], EPS, None, ALU.add).then_inc(y_eps.sem, 1)
                pool.wait_ge(*y_eps.at(where, i + 1))
                inverse_root(y_rstd[:, pair], y_ms[:, pair]).then_inc(y_rstd_done.sem, 1)

            pool.sem_inc(lo_done.sem, 1)
            pool.wait_ge(ones_set, 2)
            rstd_of_x(("first", 0, 0))
            remainder(("mix", 0, 0), 0)
            remainder(("mix", 0, 0), 1)
            for seq in range(N_SEQ):
                if seq:
                    swap = ("swap", 0, 0)
                    rstd_of_y(swap, 0)
                    rstd_of_y(swap, 1)
                    rstd_of_x(swap)
                    rstd_of_y(swap, 2)
                    rstd_of_y(swap, 3)
                with pool.Fori(0, PAIRS) as pr:
                    where = ("mix", seq, pr)
                    for i in range(2, N_MIX):
                        remainder(where, i)
                        if i in (9, 10):
                            h = i - 9
                            pool.wait_ge(*veps_done.at(where, h + 1))
                            inverse_root(grs[:, :], veps[:, :]).then_inc(grs_done.sem, 1)
                    remainder(("mix", seq, pr + 1), 0)
                    remainder(("mix", seq, pr + 1), 1)
                mid = ("mid", seq, 0)
                for i, (a, b) in enumerate(((0, 1), (2, 3), (0, 2))):
                    if i < 2:
                        pool.wait_ge(*sq_done.at(mid, b + 1))
                    else:
                        pool.wait_ge(*sum_low.at(mid, 2))
                    pool.tensor_tensor(sq[a], sq[a], sq[b], ALU.add).then_inc(sum_low.sem, 1)
                for b in range(2):
                    pool.wait_ge(*msq_done.at(mid, b + 1))
                    inverse_root(rstd[:, 4 * b:4 * b + 4], msq[:, 4 * b:4 * b + 4]).then_inc(rstd_done.sem, 1)
                with pool.Fori(0, GROUPS) as g:
                    for i in range(2, N_FFN):
                        remainder(("ffn", seq, g), i)
                    remainder(("ffn", seq, g + 1), 0)
                    remainder(("ffn", seq, g + 1), 1)
            for i in range(TT // 2):
                rstd_of_y(("last", 1, 0), i)

        @block.vector
        def _(dve):
            steps = [0]

            def step(ins):
                ins.then_inc(table_step, 1)
                steps[0] += 1
                dve.wait_ge(table_step, steps[0])

            def copy_x(where, seq, t):
                slot = slot_of(where, f"X{t}")
                dve.wait_ge(*filled(where, f"X{t}"))
                dve.tensor_copy(xT[seq][:, :, t * P:(t + 1) * P], sq_view(ps[:, slot, :], KC)).then_inc(xT_set[0].sem, 1)

            def scale_y(where, t):
                slot = slot_of(where, f"Y{t}")
                dve.wait_ge(*y_rstd_done.at(where, t // 2 + 1))
                if t >= Y_RING:
                    dve.wait_ge(*y_out[t % Y_RING].at(where, 16))
                dve.scalar_tensor_tensor(y_sb[:, t % Y_RING, :], ps[:, slot, :], y_rstd[:, t:t + 1], g_row[:, :],
                                         ALU.mult, ALU.mult).then_inc(y_scaled.sem, 1)

            def diagonal(where):
                for b in range(2):
                    if b == 0 or where[0] == "mid":
                        dve.wait_ge(*rstd_done.at(where, b + 1))
                    dve.tensor_tensor(sq_view(diag[:, b * HALF:(b + 1) * HALF], 4), ident.unsqueeze(1).to_broadcast([P, 4, P]),
                                      rstd[:, 4 * b:4 * b + 4].unsqueeze(2).to_broadcast([P, 4, P]),
                                      ALU.mult).then_inc(diag_done.sem, 1)

            def norm_apply(where, seq, factor, between=None):
                for i in range(len(pieces) + 1):
                    if i < len(pieces):
                        k, begin, end = pieces[i]
                        if where[0] == "mid" and i < 2:
                            dve.wait_ge(*filled(where, f"R{i}"))
                        if k >= 2:
                            dve.wait_ge(*hf_done.at(where, k))
                        dve.tensor_tensor(tn[:, k % 2, begin:end], xT[seq][:, k, begin:end], factor[:, begin:end],
                                          ALU.mult).then_inc(tn_done.sem, 1)
                    if i == 1 and between is not None:
                        between()
                    if i:
                        k, begin, end = pieces[i - 1]
                        dve.wait_ge(*hf_done.at(where, i))
                        dve.tensor_tensor(h_lo[seq][:, k, begin:end], hf[:, k % 2, begin:end],
                                          h_hi[seq][:, k, begin:end].bitcast(F32), ALU.subtract).then_inc(hlo_done.sem, 1)

            def update_residual(where, gate):
                seq = where[1]
                for d in range(KC):
                    slot = slot_of(where, f"W{d}")
                    dve.wait_ge(*filled(where, f"W{d}"))
                    dve.scalar_tensor_tensor(xT[seq][:, d, :], ps[:, slot, :], modT[:, seq, gate + d:gate + d + 1],
                                             xT[seq][:, d, :], ALU.mult, ALU.add).then_inc(res_done.sem, 1)

            dve.sem_inc(res_done.sem, 4)
            dve.sem_inc(mb_done.sem, 1)
            dve.memset(silT[:, :, :], 0.0).then_inc(sil_step, 1)
            dve.memset(ones[:, :], 1.0).then_inc(ones_set, 1)
            dve.memset(mhalf[:, :], -0.5).then_inc(ones_set, 1)
            first = ("first", 0, 0)
            copy_x(first, 0, 0)
            dve.wait_ge(vec_turned, 1)
            dve.tensor_copy(vecT[:, :], ps[:, 3, 0:R_ALL]).then_inc(vec_done, 1)
            for i in range(2):
                ins = dve.tensor_copy(convT[:, :, 2 * i:2 * i + 2],
                                      ps[:, 3, (i + 1) * P:(i + 1) * P + 4 * FC].rearrange("p (t j) -> p j t", t=2))
            ins.then_inc(vec_done, 1)
            copy_x(first, 0, 2)
            dve.wait_ge(sil_tanh, 1)
            dve.scalar_tensor_tensor(sil_raw[:, :], sil_raw[:, :], 1.0, vecT[:, R_C:R_C + 2 * KC], ALU.add,
                                     ALU.mult).then_inc(sil_step, 1)
            dve.wait_ge(sil_step, 2)
            mid_col = ADA_ROWS - N_SEQ
            dve.tensor_scalar(silT[:, :, mid_col:mid_col + N_SEQ], sil_raw[:, :].rearrange("p (s k) -> p k s", s=N_SEQ),
                              0.5, None, ALU.mult).then_inc(sil_done, 1)
            copy_x(first, 0, 4)
            copy_x(first, 0, 6)
            diagonal(first)

            def copy_ada(part):
                dve.wait_ge(ada_used, ADA_RING + 4 * ADA_GROUPS * (part + 1))
                if part == 2:
                    dve.wait_ge(ada_turned, 1)
                dve.tensor_copy(ada_rows[:, part % 2, :], ps[0:ADA_ROWS, ADA_SLOT[part], 0:HALF]).then_inc(ada_rows_set, 1)

            def add_bias(part):
                dve.wait_ge(ada_turned, part + 1)
                a, b = 16 * part, 16 * (part + 1)
                turned = ps[:, ADA_SLOT[part], HALF:HALF + 4 * ADA_ROWS]
                turned = turned.rearrange("p (j g s) -> p g j s", g=ADA_GROUPS, s=N_SEQ)
                for s in range(N_SEQ):
                    ins = dve.tensor_tensor(modT[:, s, a:b].rearrange("p (g j) -> p g j", j=4), turned[:, :, :, s],
                                            vecT[:, R_BADA + a:R_BADA + b].rearrange("p (g j) -> p g j", j=4), ALU.add)
                ins.then_inc(mod_based, 1)

            def take_gain(scale, row):
                dve.scalar_tensor_tensor(modT[:, :, scale:scale + 8], modT[:, :, scale:scale + 8], 1.0,
                                         vecT[:, row:row + 8].unsqueeze(1).to_broadcast([P, 2, 8]), ALU.add,
                                         ALU.mult).then_inc(mod_ready, 1)

            copy_ada(0)
            add_bias(0)
            dve.wait_ge(mod_based, 1)
            take_gain(8, R_GMIX)
            dve.wait_ge(*rrow_done.at(first, 1))
            norm_apply(first, 0, rrow[:, :])
            dve.wait_ge(decay_in, 32)
            logit = lg[:, :, :, :].rearrange("p a b c -> p (a b c)")
            step(dve.scalar_tensor_tensor(small[:, 0, :], logit, -1.0, logit, ALU.mult, ALU.max))
            dve.wait_ge(table_act, 1)
            step(dve.tensor_scalar(small[:, 2, :], small[:, 1, :], 2.0, None, ALU.add))
            step(dve.reciprocal(small[:, 2, :], small[:, 2, :]))
            step(dve.tensor_tensor(small[:, 3, :], small[:, 1, :], small[:, 2, :], ALU.mult))
            step(dve.tensor_tensor(small[:, 4, :], small[:, 3, :], small[:, 3, :], ALU.mult))
            step(dve.tensor_scalar(small[:, 5, :], small[:, 4, :], 1.0 / 17, None, ALU.mult))
            for k in range(7, 0, -1):
                step(dve.scalar_tensor_tensor(small[:, 5, :], small[:, 5, :], 1.0 / (2 * k + 1), small[:, 4, :],
                                              ALU.add, ALU.mult))
            step(dve.scalar_tensor_tensor(small[:, 5, :], small[:, 5, :], 1.0, small[:, 3, :], ALU.add, ALU.mult))
            step(dve.tensor_scalar(small[:, 0, :], logit, 0.0, None, ALU.min))
            step(dve.scalar_tensor_tensor(logit, small[:, 5, :], -2.0, small[:, 0, :], ALU.mult, ALU.add))
            dve.wait_ge(const_in, 16)
            for d in range(2):
                pos = cst[:, C_POS + d:C_POS + d + 1]
                dve.tensor_scalar(pairT[:, :, T_DK + d:T_DK + 4:2], lg[:, d, :, :], pos, None, ALU.mult)
            for d in range(2):
                half = slice(d * DK, (d + 1) * DK)
                dve.tensor_scalar(pairT[half, :, T_DC:T_DC + 2], lg[half, d, :, :], float(P), None, ALU.mult)
            for h in range(2):
                half = slice(h * DK, (h + 1) * DK)
                for d, sign in enumerate((1.0, -1.0)):
                    dve.tensor_scalar(pairT[half, :, T_LGQ + d:T_LGQ + d + 1], lg[half, d, :, h:h + 1], sign, None, ALU.mult)
            for d, col in enumerate((T_LGF, T_LGB)):
                ins = dve.tensor_copy(pairT[:, :, col:col + 2], lg[:, d, :, :])
            ins.then_inc(table_args, 1)
            dve.wait_ge(table_act, 2)
            dve.tensor_scalar(pairT[:, :, T_DK:T_DK + 4], pairT[:, :, T_DK:T_DK + 4], K_SCALE, None, ALU.mult)
            for col, row, factor in ((T_GAIN, R_GAIN, 0.25), (T_PS, R_PS, 0.5)):
                step(dve.tensor_scalar(pairT[:, :, col:col + 2], vecT[:, row:row + 8].rearrange("p (a b) -> p a b", b=2),
                                       factor, None, ALU.mult))
            for part in (1, 2):
                copy_ada(part)
                add_bias(part)
            dve.wait_ge(mod_based, 3)
            take_gain(32, R_GFFN)
            dve.wait_ge(mod_ready, 2)

            for seq in range(N_SEQ):
                if seq:
                    swap = ("swap", 0, 0)
                    for t in range(4):
                        copy_x(swap, 1, t)
                    dve.wait_ge(*g_row_in.at(swap, 0))
                    scale_y(swap, 0)
                    scale_y(swap, 1)
                    copy_x(swap, 1, 4)
                    scale_y(swap, 2)
                    scale_y(swap, 3)
                    copy_x(swap, 1, 6)
                    diagonal(swap)
                    scale_y(swap, 4)
                    scale_y(swap, 5)
                    dve.wait_ge(*rrow_done.at(swap, 1))
                    norm_apply(swap, 1, rrow[:, :], lambda: (scale_y(swap, 6), scale_y(swap, 7)))
                    for t in range(Y_RING):
                        dve.wait_ge(*y_out[t].at(swap, 16 * len(range(t, TT, Y_RING))))
                with dve.Fori(0, PAIRS) as pr:
                    where = ("mix", seq, pr)

                    def scal(col):
                        return pairS[:, col:col + 1]

                    start_at = dve.snap(PAD - (pr * pr * pr + 5 * pr + 6) // 6)

                    dve.tensor_copy(pairS[:, 0:T_BUILT], pairT[:, bass.ds(pr, 1), :].rearrange("p a b -> p (a b)"))
                    dve.tensor_copy(pairS[:, T_BUILT:T_ALL],
                                    cst[:, bass.ds(pr * POOL_COLS + C_POOL, POOL_COLS)]).then_inc(pair_set.sem, 1)
                    dve.wait_ge(*pair_set.at(where, 1))
                    for h in range(2):
                        dve.tensor_scalar(dec[:, h, :], cst[:, C_DIFP:C_DIFP + P], scal(T_LGF + h), None,
                                          ALU.mult).then_inc(dec_arg.sem, 1)
                    for h in range(2):
                        dve.wait_ge(*dec_arg.at(where, h + 1))
                        dve.scalar_tensor_tensor(dec[:, h, :], cst[:, C_DIFN:C_DIFN + P], scal(T_LGB + h), dec[:, h, :],
                                                 ALU.mult, ALU.add).then_inc(dec_arg.sem, 1)
                    place_of = cst[:, C_QUERY:C_QUERY + P]
                    dve.tensor_scalar(dec[:, 2, :], place_of, scal(T_LGQ), None, ALU.mult).then_inc(dec_arg.sem, 1)
                    dve.scalar_tensor_tensor(dec[:, 3, :], place_of, -(P + 1.0), scal(T_LGQ + 1).to_broadcast([P, P]),
                                             ALU.add, ALU.mult).then_inc(dec_arg.sem, 1)

                    def rope_products(i):
                        slot = slot_of(where, f"Q{i}")
                        dve.wait_ge(*filled(where, f"Q{i}"))
                        qk = sq_view(ps[:, slot, :], 2)[:, :, 0:2 * P].rearrange("p t (v e) -> p t v e", e=32)
                        if i >= 2:
                            dve.wait_ge(*rope_done.at(where, i - 1))
                        for buf, col in ((bufA, C_COS), (bufB, C_SIN)):
                            table = cst[:, col + 64 * i:col + 64 * i + 64].rearrange("p (t e) -> p t e", t=2)
                            ins = dve.tensor_tensor(
                                buf[:, (i % 2) * HALF:(i % 2 + 1) * HALF].rearrange("p (t v e) -> p t v e", t=2, e=32),
                                qk, table.unsqueeze(2).to_broadcast([P, 2, 8, 32]), ALU.mult)
                        ins.then_inc(rope_mul.sem, 1)

                    def rope_sums(i):
                        dve.wait_ge(*rope_mul.at(where, i + 1))
                        a, b = (buf[:, (i % 2) * HALF:(i % 2 + 1) * HALF].rearrange("p (v s e) -> p v s e", s=2, e=32)
                                for buf in (bufA, bufB))
                        out = rot[:, 2 * i:2 * i + 2, :].rearrange("p t (v s e) -> p (t v) s e", s=2, e=32)
                        dve.tensor_tensor(out[:, :, 0, :], a[:, :, 0, :], b[:, :, 1, :], ALU.subtract)
                        dve.tensor_tensor(out[:, :, 1, :], a[:, :, 1, :], b[:, :, 0, :], ALU.add).then_inc(rope_done.sem, 1)

                    for i in range(5):
                        if i < 4:
                            rope_products(i)
                        if i:
                            rope_sums(i - 1)

                    def decayed_k(h):
                        for d in range(2):
                            ins = dve.tensor_scalar(kdp[:, :, d * DK:(d + 1) * DK], rot[:, :, P + h * DK:P + (h + 1) * DK],
                                                    scal(T_DK + 2 * h + d), None, ALU.mult)
                        ins.then_inc(kd_done.sem, 1)

                    def decayed_q(h):
                        head = slice(h * DK, (h + 1) * DK)
                        for d in range(2):
                            ins = dve.tensor_tensor(sq_view(qdT[d * DK:(d + 1) * DK, :], TT), sq_view(qT[head, :], TT),
                                                    dec[head, 2 + d, :].unsqueeze(1).to_broadcast([DK, TT, P]), ALU.mult)
                        ins.then_inc(qdT_done.sem, 1)

                    f, b = slice(0, DK), slice(DK, P)

                    def first_states(h):
                        dve.memset(state[f, 0:P], 0.0).then_inc(state_step.sem, 1)
                        dve.memset(state[b, (TT - 1) * P:TT * P], 0.0).then_inc(state_step.sem, 1)

                    def states(h):
                        dc = T_DC + h
                        slot = slot_of(where, f"KV{h}")
                        dve.wait_ge(*filled(where, f"KV{h}"))
                        for n in range(1, TT):
                            for rows_d, last, new, back in ((f, n - 1, n, 2), (b, TT - n, TT - 1 - n, 2)):
                                at = 16 * h + 2 * n + (1 if rows_d is b else 0)
                                dve.wait_ge(*state_step.at(where, at + 1 - back))
                                dve.scalar_tensor_tensor(
                                    state[rows_d, new * P:(new + 1) * P], state[rows_d, last * P:(last + 1) * P],
                                    pairS[rows_d, dc:dc + 1], ps[rows_d, slot, last * P:(last + 1) * P],
                                    ALU.mult, ALU.add).then_inc(state_step.sem, 1)

                    def scores(h):
                        slot = slot_of(where, f"SC{h}")
                        dve.wait_ge(*filled(where, f"SC{h}"))
                        if h == 0:
                            dve.wait_ge(*dec_done.at(where, 1))
                        dve.scalar_tensor_tensor(kdp[:, :, :], sq_view(ps[:, slot, :], TT), K_SCALE,
                                                 dec[:, h, :].unsqueeze(1).to_broadcast([P, TT, P]),
                                                 ALU.mult, ALU.mult).then_inc(pt_done.sem, 1)

                    def statistics(h):
                        slot = slot_of(where, f"O{h}")
                        dve.wait_ge(*filled(where, f"O{h}"))
                        for t in range(TT):
                            ins = dve.bn_stats(bst[:, t, :], ps[:, slot, t * P:(t + 1) * P])
                        ins.then_inc(stat_done.sem, 1)

                    def aggregate(h):
                        for t in range(TT):
                            ins = dve.bn_aggr(mv[:, t, :], bst[:, t, :])
                        ins.then_inc(mv_done.sem, 1)
                        dve.wait_ge(*mv_done.at(where, h + 1))
                        dve.tensor_scalar(veps[:, :], mv[:, :, 1], EPS, None, ALU.add).then_inc(veps_done.sem, 1)

                    def centred(h, turned):
                        if turned is not None:
                            dve.wait_ge(*filled(where, turned))
                        slot = place("mix", f"O{h}")[0]
                        dve.tensor_tensor(tokb[:, :, :], sq_view(ps[:, slot, :], TT),
                                          mv[:, :, 0:1].to_broadcast([P, TT, P]), ALU.subtract).then_inc(cent_done.sem, 1)

                    def normed(h):
                        dve.wait_ge(*grs_done.at(where, h + 1))
                        dve.wait_ge(*cent_done.at(where, h + 1))
                        dve.tensor_tensor(tokb[:, :, :], tokb[:, :, :], grs[:, :].unsqueeze(2).to_broadcast([P, TT, P]),
                                          ALU.mult).then_inc(retn_done.sem, 1)

                    def swish(h):
                        slot = slot_of(where, f"GS{h}")
                        dve.wait_ge(*filled(where, f"GS{h}"))
                        dve.wait_ge(*th_done.at(where, h + 1))
                        dve.scalar_tensor_tensor(bufA[:, :], bufA[:, :], 1.0, ps[:, slot, :], ALU.add,
                                                 ALU.mult).then_inc(sw_done.sem, 1)

                    def gate_a(h):
                        dve.wait_ge(*ta_done.at(where, h + 1))
                        dve.wait_ge(*sw_done.at(where, h + 1))
                        dve.scalar_tensor_tensor(bufA[:, :], bufB[:, :], 1.0, bufA[:, :], ALU.add,
                                                 ALU.mult).then_inc(ga_done.sem, 1)

                    def branch_a(h):
                        slot = slot_of(where, f"TR{h}")
                        dve.wait_ge(*filled(where, f"TR{h}"))
                        dve.wait_ge(*ga_done.at(where, h + 1))
                        dve.scalar_tensor_tensor(bufA[:, :], ps[:, slot, :], scal(T_GAIN + h), bufA[:, :], ALU.mult,
                                                 ALU.mult).then_inc(ma_done.sem, 1)

                    def branch_b(h):
                        slot = slot_of(where, f"BB{h}")
                        dve.wait_ge(*filled(where, f"BB{h}"))
                        dve.wait_ge(*tb_done.at(where, h + 1))
                        dve.scalar_tensor_tensor(bufB[:, :], bufB[:, :], 1.0, ps[:, slot, :], ALU.add,
                                                 ALU.mult).then_inc(mb_done.sem, 1)

                    def merge(h):
                        dve.wait_ge(*ma_done.at(where, h + 1))
                        dve.wait_ge(*mb_done.at(where, h + 1))
                        dve.scalar_tensor_tensor(bufA[:, :], bufB[:, :], scal(T_PS + h), bufA[:, :], ALU.mult,
                                                 ALU.add).then_inc(mg_done.sem, 1)

                    def merge_low(h):
                        dve.wait_ge(*mhi_done.at(where, h + 1))
                        dve.tensor_tensor(m_lo[:, h, :], bufA[:, :], m_hi[:, h, :].bitcast(F32),
                                          ALU.subtract).then_inc(mlo_done.sem, 1)

                    dve.wait_ge(*rope_done.at(where, 4))
                    decayed_k(0)

                    for at in (0, PAD + S):
                        dve.memset(state[:, at:at + PAD], 0.0).then_inc(pool_step.sem, 1)
                    dve.wait_ge(*p_copied.at(where, 1))
                    src, length = state, S + 2 * PAD
                    for level in range(4):
                        dve.wait_ge(*pool_step.at(where, 2 + level))
                        length -= 1 << level
                        dve.scalar_tensor_tensor(poolU[:, 0:length], src[:, 1 << level:(1 << level) + length],
                                                 scal(T_POOL + level), src[:, 0:length], ALU.mult,
                                                 ALU.add).then_inc(pool_step.sem, 1)
                        src = poolU
                    dve.wait_ge(*pool_step.at(where, 6))
                    for n, at in ((0, 0), (1, S - PAD)):
                        edge = poolU[:, bass.ds(start_at + at, PAD)]
                        ins = dve.tensor_tensor(edge, edge, pairS[:, T_POOL + 5 + 8 * n:T_POOL + 13 + 8 * n], ALU.mult)
                    ins.then_inc(pool_step.sem, 1)
                    dve.wait_ge(*pool_step.at(where, 7))
                    dve.scalar_tensor_tensor(poolU[:, 0:S], poolU[:, bass.ds(start_at, S)], scal(T_POOL + 4),
                                             state[:, PAD:PAD + S], ALU.mult, ALU.subtract).then_inc(pool_step.sem, 1)
                    dve.wait_ge(*filled(where, "TQ"))
                    dve.tensor_copy(qT[:, :], ps[:, slot_of(where, "TQ"), :]).then_inc(qT_done.sem, 1)
                    swish(0)
                    dve.wait_ge(*qT_done.at(where, 1))
                    dve.wait_ge(*dec_done.at(where, 1))
                    decayed_q(0)
                    dve.wait_ge(*pool_step.at(where, 8))
                    first_states(0)
                    states(0)
                    scores(0)
                    gate_a(0)
                    dve.wait_ge(*filled(where, "O0"))
                    decayed_k(1)
                    decayed_q(1)
                    statistics(0)
                    dve.wait_ge(*stat_done.at(where, 1))
                    first_states(1)
                    aggregate(0)
                    centred(0, None)
                    states(1)
                    scores(1)
                    normed(0)
                    statistics(1)
                    dve.wait_ge(*stat_done.at(where, 2))
                    branch_b(0)
                    aggregate(1)
                    branch_a(0)
                    merge(0)
                    merge_low(0)
                    centred(1, "TR0")
                    normed(1)
                    swish(1)
                    gate_a(1)
                    branch_a(1)
                    branch_b(1)
                    merge(1)
                    merge_low(1)
                    update_residual(where, 16)
                mid = ("mid", seq, 0)
                for a, b in ((4, 5), (6, 7)):
                    dve.wait_ge(*sq_done.at(mid, b + 1))
                    dve.tensor_tensor(sq[a], sq[a], sq[b], ALU.add).then_inc(sum_all.sem, 1)
                for half in range(2):
                    tokens = slice(half * HALF, (half + 1) * HALF)
                    for i, other in enumerate((6, 0)):
                        dve.wait_ge(*sum_all.at(mid, 2 + i * (2 * half + 1)))
                        if other == 0:
                            dve.wait_ge(*sum_low.at(mid, 3))
                        dve.tensor_tensor(sq[4][:, tokens], sq[4][:, tokens], sq[other][:, tokens],
                                          ALU.add).then_inc(sum_all.sem, 1)
                slot = slot_of(mid, "ST0")
                for half in range(2):
                    dve.wait_ge(*filled(mid, f"ST{half}"))
                    dve.tensor_scalar(msq[:, 4 * half:4 * half + 4], ps[:, slot, half * (HALF + 4):half * (HALF + 4) + 4], EPS,
                                      None, ALU.add).then_inc(msq_done.sem, 1)
                diagonal(mid)
                norm_apply(mid, seq, ps[:, slot_of(mid, "R0"), :])
                with dve.Fori(0, GROUPS) as g:
                    where = ("ffn", seq, g)
                    taps = convT[:, :, :].rearrange("p (l c) t -> p l c t", l=2)
                    dve.tensor_copy(convS[:, :, :, :], taps[:, :, bass.ds(g * 2, 2), :]).then_inc(conv_set.sem, 1)

                    def side_taps(i, dst):
                        slot = place("ffn", f"U{i}")[0]
                        dve.wait_ge(*mid_tap.at(where, i + 1))
                        col = convS[:, i % 2, i // 2, :]
                        dve.scalar_tensor_tensor(dst[:, 1:S], ps[:, slot, 0:S - 1], col[:, 0:1], dst[:, 1:S],
                                                 ALU.mult, ALU.add).then_inc(side_tap.sem, 1)
                        dve.wait_ge(*side_tap.at(where, 2 * i + 1))
                        dve.scalar_tensor_tensor(dst[:, 0:S - 1], ps[:, slot, 1:S], col[:, 2:3], dst[:, 0:S - 1],
                                                 ALU.mult, ALU.add).then_inc(side_tap.sem, 1)

                    dve.wait_ge(*conv_set.at(where, 1))
                    for j in range(2):
                        side_taps(2 * j, ca)
                        side_taps(2 * j + 1, cl)
                        dve.wait_ge(*gelu_done.at(where, j + 1))
                        dve.wait_ge(*side_tap.at(where, 4 * j + 4))
                        dve.tensor_tensor(a_hi[:, j, :], cl[:, :], ca[:, :], ALU.mult).then_inc(ahi_done.sem, 1)
                        dve.tensor_tensor(cl[:, :], cl[:, :], ca[:, :], ALU.mult).then_inc(prod_done.sem, 1)
                        dve.wait_ge(*ahi_done.at(where, j + 1))
                        dve.wait_ge(*prod_done.at(where, j + 1))
                        dve.tensor_tensor(a_lo[:, j, :], cl[:, :], a_hi[:, j, :].bitcast(F32),
                                          ALU.subtract).then_inc(alo_done.sem, 1)
                    update_residual(where, 40)
            last = ("last", 1, 0)
            dve.wait_ge(*g_row_in.at(last, 0))
            for t in range(TT):
                scale_y(last, t)


def kernel(x_prompt, x_sample, c_prompt, c_sample, w_ada, b_ada, g_mix, w_in, ret_decay_f, ret_decay_b,
           ret_gn_gain, w_pool_grp, pool_scale, w_out, g_ffn, w_up, conv_w, conv_b, w_down, g_final):
    import concourse.bacc as bacc
    from concourse.bass_utils import run_bass_kernel_spmd

    arrays = {
        "x": np.concatenate([np.asarray(x_prompt), np.asarray(x_sample)], 0).reshape(N_SEQ * S, D),
        "c": np.concatenate([np.asarray(c_prompt), np.asarray(c_sample)], 0),
        "w_ada": np.asarray(w_ada)[0], "b_ada": np.asarray(b_ada)[0], "g_mix": np.asarray(g_mix)[0],
        "w_in": np.asarray(w_in)[0], "decay_f": np.asarray(ret_decay_f)[0], "decay_b": np.asarray(ret_decay_b)[0],
        "gn_gain": np.asarray(ret_gn_gain)[0], "w_pool": np.asarray(w_pool_grp)[0],
        "pool_scale": np.asarray(pool_scale)[0], "w_out": np.asarray(w_out)[0], "g_ffn": np.asarray(g_ffn)[0],
        "w_up": np.asarray(w_up)[0], "conv_w": np.asarray(conv_w)[0], "conv_b": np.asarray(conv_b)[0],
        "w_down": np.asarray(w_down)[0], "g_final": np.asarray(g_final), "consts": constants(),
    }
    arrays = {n: np.ascontiguousarray(a) for n, a in arrays.items()}
    nc = bacc.Bacc("TRN2", target_bir_lowering=False, num_devices=1)
    args = [nc.dram_tensor(f"in_{n}", a.shape, F32, kind="ExternalInput").ap() for n, a in arrays.items()]
    args.append(nc.dram_tensor("out_y", (N_SEQ * S, D), F32, kind="ExternalOutput").ap())
    encoder_program(nc, *args)
    r = run_bass_kernel_spmd(nc, [{f"in_{n}": a for n, a in arrays.items()}], core_ids=[0])
    y = r.results[0]["out_y"].reshape(N_SEQ, 1, S, D)
    return y[0], y[1]
```
